# Optimizing a Trainium2 kernel written in Bass

```python
import math, functools
import jax
import jax.numpy as jnp
from jax import lax
import numpy as np

D_MODEL = 1024
BATCH = 1
SEQ = 1024
DEPTH = 1

GRID_W = 64
CTX_LEN = 256
N_MIXERS = 4
D_MIX = D_MODEL
D_GROUP = D_MIX // N_MIXERS
CHUNK = 64
SHORT_CONV = 3
N_DIR = 2
EPS = 1e-6
N_MOD = 6

GLA_HEADS = 4
GLA_DK = D_GROUP // (2 * GLA_HEADS)
GLA_DV = D_GROUP // GLA_HEADS
GLA_RANK = 16
GLA_TAU = 16.0

HY_ORDER = 2
HY_EMB = 33
HY_BANDS = (HY_EMB - 1) // 2
HY_FILTER_HIDDEN = 64
HY_DECAY_TARGET = 1e-2
HY_FAST_DECAY = 0.3
HY_SLOW_DECAY = 1.5

MB_HEADS = 4
MB_HEADDIM = D_GROUP // MB_HEADS
MB_STATE = 128
MB_GROUPS = 2
MB_CONV_CH = D_GROUP + 2 * MB_GROUPS * MB_STATE

DN_HEADS = 4
DN_DK = D_GROUP // DN_HEADS
DN_DV = D_GROUP // DN_HEADS

N_EXPERTS = 16
EC_CAPACITY = 2
D_EXPERT = 1024

GLA_COLS = 2 * GLA_HEADS * GLA_DK + 2 * D_GROUP + N_DIR * GLA_RANK
HY_COLS = (HY_ORDER + 1) * D_GROUP
MB_COLS = D_GROUP + MB_CONV_CH + N_DIR * MB_HEADS
DN_COLS = 4 * D_GROUP + 2 * N_DIR * DN_HEADS
D_IN_PROJ = GLA_COLS + HY_COLS + MB_COLS + DN_COLS

kernel_name = 'hybrid_parallel_heads_ec_moe_diffusion'

F32 = jnp.float32

def rmsnorm(x, w):
    xf = x.astype(F32)
    y = xf * lax.rsqrt(jnp.mean(xf * xf, axis=-1, keepdims=True) + EPS)
    return (y * w.astype(F32)).astype(x.dtype)

def head_rmsnorm(o, w, n_heads):
    b_, l_, hd = o.shape
    oh = o.reshape(b_, l_, n_heads, hd // n_heads)
    oh = oh * lax.rsqrt(jnp.mean(oh * oh, axis=-1, keepdims=True) + EPS)
    return oh.reshape(b_, l_, hd) * w.astype(F32)

def l2norm(t):
    return t * lax.rsqrt(jnp.sum(t * t, axis=-1, keepdims=True) + EPS)

def to_heads(t, n_heads):
    b_, l_, hd = t.shape
    return t.reshape(b_, l_, n_heads, hd // n_heads).transpose(0, 2, 1, 3).astype(F32)

def from_heads(t):
    b_, h_, l_, d_ = t.shape
    return t.transpose(0, 2, 1, 3).reshape(b_, l_, h_ * d_)

def to_col_major(u, rows):
    b_, l_, ch = u.shape
    return u.reshape(b_, rows, GRID_W, ch).transpose(0, 2, 1, 3).reshape(b_, l_, ch)

def to_row_major(u, rows):
    b_, l_, ch = u.shape
    return u.reshape(b_, GRID_W, rows, ch).transpose(0, 2, 1, 3).reshape(b_, l_, ch)

def short_conv(u, w, b=None):
    k_, ch = w.shape
    y = lax.conv_general_dilated(u, w[:, None, :].astype(u.dtype), window_strides=(1,),
                                 padding=[(k_ // 2, k_ // 2)], dimension_numbers=('NWC', 'WIO', 'NWC'),
                                 feature_group_count=ch)
    if b is not None:
        y = y + b.astype(u.dtype)
    return y

def modulation(cond, w_mod, b_mod):
    m = jax.nn.silu(cond.astype(F32)) @ w_mod.astype(F32) + b_mod.astype(F32)
    return jnp.split(m, N_MOD, axis=-1)

def modulate(x, g, shift, scale):
    return (rmsnorm(x, g).astype(F32) * (1.0 + scale) + shift).astype(x.dtype)

def bidirectional_scan(scan_f, scan_b, ctx_in, lat_in, s0, t_axis, need_ctx):
    rev = lambda ts: tuple(jnp.flip(t, t_axis) for t in ts)
    oc_f, s_f = scan_f(*ctx_in[0], s0)
    oc_b, s_b = scan_b(*rev(ctx_in[1]), s0)
    ol_f, _ = scan_f(*lat_in[0], s_f)
    ol_b, _ = scan_b(*rev(lat_in[1]), s_b)
    o_lat = ol_f + jnp.flip(ol_b, t_axis)
    o_ctx = (oc_f + jnp.flip(oc_b, t_axis)) if need_ctx else None
    return o_ctx, o_lat

def gla_scan(q, k, v, g, s0):
    b_, h_, l_, dk = q.shape
    dv = v.shape[-1]
    n = l_ // CHUNK
    q, k, v, g = [t.reshape(b_, h_, n, CHUNK, t.shape[-1]) for t in (q, k, v, g)]
    cum = jnp.cumsum(g, axis=-2)
    cum_last = cum[..., -1:, :]
    q_g = q * jnp.exp(cum)
    k_g = k * jnp.exp(-cum)
    k_end = k * jnp.exp(cum_last - cum)
    causal = jnp.tril(jnp.ones((CHUNK, CHUNK), bool))
    attn = jnp.where(causal, jnp.einsum('bhnid,bhnjd->bhnij', q_g, k_g), 0.0)
    o_intra = jnp.einsum('bhnij,bhnjv->bhniv', attn, v)
    chunk_decay = jnp.exp(cum_last[..., 0, :])

    def step(s, inp):
        qg, ke, vv, dec = inp
        o = jnp.einsum('bhcd,bhdv->bhcv', qg, s)
        s = s * dec[..., None] + jnp.einsum('bhcd,bhcv->bhdv', ke, vv)
        return s, o

    xs = tuple(jnp.moveaxis(t, 2, 0) for t in (q_g, k_end, v, chunk_decay))
    s_fin, o_inter = lax.scan(step, s0, xs)
    o = o_intra + jnp.moveaxis(o_inter, 0, 2)
    return o.reshape(b_, h_, l_, dv), s_fin

def gla_mixer(u_ctx, u_lat, w2, b, norm_w, need_ctx):
    nq = GLA_HEADS * GLA_DK

    def prep(u):
        q, k, v, og, lr = jnp.split(u, [nq, 2 * nq, 2 * nq + D_GROUP, 2 * nq + 2 * D_GROUP], axis=-1)
        q = to_heads(q, GLA_HEADS) * GLA_DK ** -0.5
        k = to_heads(k, GLA_HEADS)
        v = to_heads(v, GLA_HEADS)
        lr = lr.astype(F32).reshape(lr.shape[0], lr.shape[1], N_DIR, GLA_RANK)
        z = jnp.einsum('blsr,srk->blsk', lr, w2.astype(F32)) + b.astype(F32)
        log_alpha = jax.nn.log_sigmoid(z) / GLA_TAU
        g_f = to_heads(log_alpha[:, :, 0], GLA_HEADS)
        g_b = to_heads(log_alpha[:, :, 1], GLA_HEADS)
        return ((q, k, v, g_f), (q, k, v, g_b)), og

    ctx_in, og_c = prep(u_ctx)
    lat_in, og_l = prep(u_lat)
    s0 = jnp.zeros((u_lat.shape[0], GLA_HEADS, GLA_DK, GLA_DV), F32)
    o_c, o_l = bidirectional_scan(gla_scan, gla_scan, ctx_in, lat_in, s0, 2, need_ctx)

    def out(o, og):
        return (head_rmsnorm(from_heads(o), norm_w, GLA_HEADS) * jax.nn.silu(og.astype(F32))).astype(u_lat.dtype)

    return (out(o_c, og_c) if need_ctx else None), out(o_l, og_l)

def hyena_filters(l_, w1, b1, w2, b2, w3, b3, w4, freq):
    pos = jnp.arange(l_, dtype=F32)
    t = pos / max(l_ - 1, 1)
    bands = jnp.linspace(1e-4, HY_BANDS - 1, HY_BANDS, dtype=F32)
    ang = (2.0 * math.pi / l_) * pos[:, None] * bands[None, :]
    feats = jnp.concatenate([t[:, None], jnp.cos(ang), -jnp.sin(ang)], axis=-1)
    f = freq.astype(F32)
    h = jnp.sin(f[0] * (feats @ w1.astype(F32) + b1.astype(F32)))
    h = jnp.sin(f[1] * (h @ w2.astype(F32) + b2.astype(F32)))
    h = jnp.sin(f[2] * (h @ w3.astype(F32) + b3.astype(F32)))
    h = h @ w4.astype(F32)
    max_decay = math.log(HY_DECAY_TARGET) / HY_FAST_DECAY
    min_decay = math.log(HY_DECAY_TARGET) / HY_SLOW_DECAY
    deltas = jnp.abs(jnp.linspace(min_decay, max_decay, D_GROUP, dtype=F32))
    window = jnp.exp(-t[:, None] * deltas[None, :])
    return h.reshape(l_, HY_ORDER, N_DIR, D_GROUP) * window[:, None, None, :]

def long_conv(u, h_fwd, h_bwd, d_skip):
    l_, ch = h_fwd.shape
    kern = jnp.concatenate([h_fwd, jnp.zeros((1, ch), F32), jnp.flip(h_bwd[1:], 0)], axis=0)
    spec = jnp.fft.rfft(u, n=2 * l_, axis=1) * jnp.fft.rfft(kern, axis=0)[None]
    y = jnp.fft.irfft(spec, n=2 * l_, axis=1)[:, :l_]
    return y + u * d_skip

def hyena_mixer(u_ctx, u_lat, conv_w, conv_b, w1, b1, w2, b2, w3, b3, w4, freq, d_skip, need_ctx):
    d = d_skip.astype(F32)

    def run(u):
        l_ = u.shape[1]
        uc = short_conv(u, conv_w, conv_b).astype(F32)
        v, x1, x2 = jnp.split(uc, [D_GROUP, 2 * D_GROUP], axis=-1)
        h = hyena_filters(l_, w1, b1, w2, b2, w3, b3, w4, freq)
        z = x1 * long_conv(v, h[:, 0, 0], h[:, 0, 1], d[0])
        return (x2 * long_conv(z, h[:, 1, 0], h[:, 1, 1], d[1])).astype(u.dtype)

    return (run(u_ctx) if need_ctx else None), run(u_lat)

def ssd_scan(x, dt, bm, cm, s0, a):
    b_, l_, h_, p_ = x.shape
    g_, n_ = bm.shape[-2:]
    r_ = h_ // g_
    n = l_ // CHUNK
    cum = jnp.cumsum((dt * a).reshape(b_, n, CHUNK, g_, r_), axis=2)
    xdt = (x * dt[..., None]).reshape(b_, n, CHUNK, g_, r_, p_)
    bc = bm.reshape(b_, n, CHUNK, g_, n_)
    cc = cm.reshape(b_, n, CHUNK, g_, n_)
    cum_t = jnp.moveaxis(cum, 2, -1)
    causal = jnp.tril(jnp.ones((CHUNK, CHUNK), bool))
    seg = jnp.exp(jnp.where(causal, cum_t[..., :, None] - cum_t[..., None, :], -jnp.inf))
    cb = jnp.einsum('bnigs,bnjgs->bngij', cc, bc)
    y_diag = jnp.einsum('bngij,bngrij,bnjgrp->bnigrp', cb, seg, xdt)
    to_end = jnp.exp(cum[:, :, -1:] - cum)
    states = jnp.einsum('bncgs,bncgr,bncgrp->bngrsp', bc, to_end, xdt)
    chunk_decay = jnp.exp(cum[:, :, -1])
    c_dec = jnp.exp(cum)

    def step(s, inp):
        c_i, cd_i, st_i, dec_i = inp
        y_off = jnp.einsum('bcgs,bcgr,bgrsp->bcgrp', c_i, cd_i, s)
        s = s * dec_i[..., None, None] + st_i
        return s, y_off

    xs = tuple(jnp.moveaxis(t, 1, 0) for t in (cc, c_dec, states, chunk_decay))
    s_fin, y_off = lax.scan(step, s0, xs)
    y = y_diag + jnp.moveaxis(y_off, 0, 1)
    return y.reshape(b_, l_, h_, p_), s_fin

def mamba_mixer(u_ctx, u_lat, conv_w, conv_b, a_log, dt_bias, d_skip, norm_w, rows, need_ctx):
    nx = MB_HEADS * MB_HEADDIM
    nbc = MB_GROUPS * MB_STATE

    def prep(u):
        b_, l_, _ = u.shape
        z, xbc, dt_raw = jnp.split(u, [D_GROUP, D_GROUP + MB_CONV_CH], axis=-1)
        xbc = jax.nn.silu(short_conv(xbc, conv_w, conv_b)).astype(F32)
        xs, bm, cm = jnp.split(xbc, [nx, nx + nbc], axis=-1)
        xs = xs.reshape(b_, l_, MB_HEADS, MB_HEADDIM)
        bm = bm.reshape(b_, l_, MB_GROUPS, MB_STATE)
        cm = cm.reshape(b_, l_, MB_GROUPS, MB_STATE)
        dt = jax.nn.softplus(dt_raw.astype(F32).reshape(b_, l_, N_DIR, MB_HEADS) + dt_bias.astype(F32))
        return ((xs, dt[:, :, 0], bm, cm), (xs, dt[:, :, 1], bm, cm)), xs, z

    u_lat = to_col_major(u_lat, rows)
    ctx_in, x_c, z_c = prep(u_ctx)
    lat_in, x_l, z_l = prep(u_lat)
    a = -jnp.exp(a_log.astype(F32))
    s0 = jnp.zeros((u_lat.shape[0], MB_GROUPS, MB_HEADS // MB_GROUPS, MB_STATE, MB_HEADDIM), F32)
    o_c, o_l = bidirectional_scan(functools.partial(ssd_scan, a=a[0]), functools.partial(ssd_scan, a=a[1]),
                                  ctx_in, lat_in, s0, 1, need_ctx)
    d = d_skip.astype(F32)

    def out(o, xs, z):
        y = (o + xs * d[:, None]).reshape(o.shape[0], o.shape[1], D_GROUP)
        return head_rmsnorm(y * jax.nn.silu(z.astype(F32)), norm_w, MB_HEADS).astype(u_lat.dtype)

    y_l = to_row_major(out(o_l, x_l, z_l), rows)
    return (out(o_c, x_c, z_c) if need_ctx else None), y_l

def delta_scan(q, k, v, beta, g, s0):
    b_, h_, l_, dk = q.shape
    dv = v.shape[-1]
    n = l_ // CHUNK
    q, k, v = [t.reshape(b_, h_, n, CHUNK, t.shape[-1]) for t in (q, k, v)]
    beta = beta.reshape(b_, h_, n, CHUNK)
    cum = jnp.cumsum(g.reshape(b_, h_, n, CHUNK), axis=-1)
    incl = jnp.tril(jnp.ones((CHUNK, CHUNK), bool))
    strict = jnp.tril(jnp.ones((CHUNK, CHUNK), bool), -1)
    decay = jnp.exp(jnp.where(incl, cum[..., :, None] - cum[..., None, :], -jnp.inf))
    k_beta = k * beta[..., None]
    m = jnp.where(strict, jnp.einsum('bhnid,bhnjd->bhnij', k_beta, k) * decay, 0.0)
    rhs = jnp.concatenate([v * beta[..., None], k_beta * jnp.exp(cum)[..., None]], axis=-1)
    sol = lax.linalg.triangular_solve(m + jnp.eye(CHUNK, dtype=m.dtype), rhs, left_side=True, lower=True,
                                      unit_diagonal=True)
    u_val, w_key = sol[..., :dv], sol[..., dv:]
    attn = jnp.where(incl, jnp.einsum('bhnid,bhnjd->bhnij', q, k) * decay, 0.0)
    q_dec = q * jnp.exp(cum)[..., None]
    k_end = k * jnp.exp(cum[..., -1:] - cum)[..., None]
    chunk_decay = jnp.exp(cum[..., -1])

    def step(s, inp):
        qd, ke, uu, ww, aa, dc = inp
        v_new = uu - jnp.einsum('bhcd,bhdv->bhcv', ww, s)
        o = jnp.einsum('bhcd,bhdv->bhcv', qd, s) + jnp.einsum('bhcs,bhsv->bhcv', aa, v_new)
        s = s * dc[..., None, None] + jnp.einsum('bhcd,bhcv->bhdv', ke, v_new)
        return s, o

    xs = tuple(jnp.moveaxis(t, 2, 0) for t in (q_dec, k_end, u_val, w_key, attn, chunk_decay))
    s_fin, o = lax.scan(step, s0, xs)
    return jnp.moveaxis(o, 0, 2).reshape(b_, h_, l_, dv), s_fin

def deltanet_mixer(u_ctx, u_lat, conv_w, a_log, dt_bias, norm_w, need_ctx):
    nqk = DN_HEADS * DN_DK
    nv = DN_HEADS * DN_DV

    def prep(u):
        b_, l_, _ = u.shape
        qkv, og, beta_raw, a_raw = jnp.split(u, [2 * nqk + nv, 2 * nqk + 2 * nv, 2 * nqk + 2 * nv + N_DIR * DN_HEADS],
                                             axis=-1)
        qkv = jax.nn.silu(short_conv(qkv, conv_w))
        q, k, v = jnp.split(qkv, [nqk, 2 * nqk], axis=-1)
        q = l2norm(to_heads(q, DN_HEADS)) * DN_DK ** -0.5
        k = l2norm(to_heads(k, DN_HEADS))
        v = to_heads(v, DN_HEADS)
        beta = jax.nn.sigmoid(beta_raw.astype(F32)).reshape(b_, l_, N_DIR, DN_HEADS).transpose(2, 0, 3, 1)
        g = -jnp.exp(a_log.astype(F32)) * jax.nn.softplus(
            a_raw.astype(F32).reshape(b_, l_, N_DIR, DN_HEADS) + dt_bias.astype(F32))
        g = g.transpose(2, 0, 3, 1)
        return ((q, k, v, beta[0], g[0]), (q, k, v, beta[1], g[1])), og

    ctx_in, og_c = prep(u_ctx)
    lat_in, og_l = prep(u_lat)
    s0 = jnp.zeros((u_lat.shape[0], DN_HEADS, DN_DK, DN_DV), F32)
    o_c, o_l = bidirectional_scan(delta_scan, delta_scan, ctx_in, lat_in, s0, 2, need_ctx)

    def out(o, og):
        return (head_rmsnorm(from_heads(o), norm_w, DN_HEADS) * jax.nn.silu(og.astype(F32))).astype(u_lat.dtype)

    return (out(o_c, og_c) if need_ctx else None), out(o_l, og_l)

def ec_moe(h, router, w_gate, w_up, w_down):
    b_, t_, d_ = h.shape
    cap = EC_CAPACITY * t_ // N_EXPERTS
    aff = jax.nn.softmax(jnp.einsum('btd,de->bte', h, router).astype(F32), axis=-1)
    weight, idx = lax.top_k(jnp.swapaxes(aff, 1, 2), cap)
    xs = jax.vmap(lambda hb, ib: hb[ib])(h, idx)
    a = jnp.einsum('becd,edf->becf', xs, w_gate)
    u = jnp.einsum('becd,edf->becf', xs, w_up)
    y = jnp.einsum('becf,efd->becd', jax.nn.silu(a) * u, w_down) * weight[..., None].astype(h.dtype)
    scatter = lambda ib, yb: jnp.zeros((t_, d_), h.dtype).at[ib.reshape(-1)].add(yb.reshape(-1, d_))
    return jax.vmap(scatter)(idx, y)

def setup_inputs(seed: int = 0) -> dict:
    key = jax.random.key(seed)
    keys = iter(jax.random.split(key, 48))

    def nrm(shape, scale):
        return jax.random.normal(next(keys), shape, F32) * scale

    def gains(shape):
        return 1.0 + nrm(shape, 0.05)

    def a_log(shape):
        return jnp.log(jax.random.uniform(next(keys), shape, F32, 1.0, 16.0))

    def dt_bias(shape):
        dt = jnp.exp(jax.random.uniform(next(keys), shape, F32, math.log(1e-3), math.log(1e-1)))
        return dt + jnp.log(-jnp.expm1(-dt))

    d = D_MODEL
    hf = HY_FILTER_HIDDEN
    return {
        'x': nrm((BATCH, SEQ, d), 1.0),
        'c': nrm((BATCH, d), 1.0),
        'ctx': nrm((BATCH, CTX_LEN, d), 1.0),
        'c_ctx': nrm((d,), 1.0),
        'w_mod': nrm((DEPTH, d, N_MOD * d), 0.5 * d ** -0.5),
        'b_mod': nrm((DEPTH, N_MOD * d), 0.02),
        'norm_g': gains((DEPTH, 4, d)),
        'w_in': nrm((DEPTH, d, D_IN_PROJ), d ** -0.5),
        'w_out': nrm((DEPTH, D_MIX, d), D_MIX ** -0.5),
        'gla_w2': nrm((DEPTH, N_DIR, GLA_RANK, GLA_HEADS * GLA_DK), GLA_RANK ** -0.5),
        'gla_b': nrm((DEPTH, N_DIR, GLA_HEADS * GLA_DK), 0.1),
        'gla_norm': gains((DEPTH, D_GROUP)),
        'hy_conv_w': nrm((DEPTH, SHORT_CONV, HY_COLS), SHORT_CONV ** -0.5),
        'hy_conv_b': nrm((DEPTH, HY_COLS), 0.02),
        'hy_w1': nrm((DEPTH, HY_EMB, hf), HY_EMB ** -0.5),
        'hy_b1': nrm((DEPTH, hf), 0.1),
        'hy_w2': nrm((DEPTH, hf, hf), hf ** -0.5),
        'hy_b2': nrm((DEPTH, hf), 0.1),
        'hy_w3': nrm((DEPTH, hf, hf), hf ** -0.5),
        'hy_b3': nrm((DEPTH, hf), 0.1),
        'hy_w4': nrm((DEPTH, hf, HY_ORDER * N_DIR * D_GROUP), 0.1 * hf ** -0.5),
        'hy_freq': gains((DEPTH, 3, hf)),
        'hy_d': nrm((DEPTH, HY_ORDER, D_GROUP), 1.0),
        'mb_conv_w': nrm((DEPTH, SHORT_CONV, MB_CONV_CH), SHORT_CONV ** -0.5),
        'mb_conv_b': nrm((DEPTH, MB_CONV_CH), 0.02),
        'mb_a_log': a_log((DEPTH, N_DIR, MB_HEADS)),
        'mb_dt_bias': dt_bias((DEPTH, N_DIR, MB_HEADS)),
        'mb_d': gains((DEPTH, MB_HEADS)),
        'mb_norm': gains((DEPTH, D_GROUP)),
        'dn_conv_w': nrm((DEPTH, SHORT_CONV, 2 * DN_HEADS * DN_DK + DN_HEADS * DN_DV), SHORT_CONV ** -0.5),
        'dn_a_log': a_log((DEPTH, N_DIR, DN_HEADS)),
        'dn_dt_bias': dt_bias((DEPTH, N_DIR, DN_HEADS)),
        'dn_norm': gains((DEPTH, D_GROUP)),
        'moe_router': nrm((DEPTH, d, N_EXPERTS), d ** -0.5),
        'moe_w_gate': nrm((DEPTH, N_EXPERTS, d, D_EXPERT), d ** -0.5),
        'moe_w_up': nrm((DEPTH, N_EXPERTS, d, D_EXPERT), d ** -0.5),
        'moe_w_down': nrm((DEPTH, N_EXPERTS, D_EXPERT, d), D_EXPERT ** -0.5),
    }

def reference(x, c, ctx, c_ctx, w_mod, b_mod, norm_g, w_in, w_out, gla_w2, gla_b, gla_norm,
              hy_conv_w, hy_conv_b, hy_w1, hy_b1, hy_w2, hy_b2, hy_w3, hy_b3, hy_w4, hy_freq, hy_d,
              mb_conv_w, mb_conv_b, mb_a_log, mb_dt_bias, mb_d, mb_norm,
              dn_conv_w, dn_a_log, dn_dt_bias, dn_norm,
              moe_router, moe_w_gate, moe_w_up, moe_w_down):
    rows = x.shape[1] // GRID_W
    xc = ctx
    splits = [GLA_COLS, GLA_COLS + HY_COLS, GLA_COLS + HY_COLS + MB_COLS]
    for i in range(DEPTH):
        need_ctx = i < DEPTH - 1
        sh1, sc1, g1, sh2, sc2, g2 = [t[:, None, :] for t in modulation(c, w_mod[i], b_mod[i])]
        sh1c, sc1c, g1c, sh2c, sc2c, g2c = modulation(c_ctx, w_mod[i], b_mod[i])

        u_l = modulate(x, norm_g[i, 0], sh1, sc1) @ w_in[i]
        u_c = modulate(xc, norm_g[i, 0], sh1c, sc1c) @ w_in[i]
        ua_c, ub_c, uc_c, ud_c = jnp.split(u_c, splits, axis=-1)
        ua_l, ub_l, uc_l, ud_l = jnp.split(u_l, splits, axis=-1)
        ya_c, ya_l = gla_mixer(ua_c, ua_l, gla_w2[i], gla_b[i], gla_norm[i], need_ctx)
        yb_c, yb_l = hyena_mixer(ub_c, ub_l, hy_conv_w[i], hy_conv_b[i], hy_w1[i], hy_b1[i], hy_w2[i], hy_b2[i],
                                 hy_w3[i], hy_b3[i], hy_w4[i], hy_freq[i], hy_d[i], need_ctx)
        yc_c, yc_l = mamba_mixer(uc_c, uc_l, mb_conv_w[i], mb_conv_b[i], mb_a_log[i], mb_dt_bias[i], mb_d[i],
                                 mb_norm[i], rows, need_ctx)
        yd_c, yd_l = deltanet_mixer(ud_c, ud_l, dn_conv_w[i], dn_a_log[i], dn_dt_bias[i], dn_norm[i], need_ctx)
        y_l = jnp.concatenate([ya_l, yb_l, yc_l, yd_l], axis=-1) @ w_out[i]
        x = x + (g1 * rmsnorm(y_l, norm_g[i, 1]).astype(F32)).astype(x.dtype)

        h_l = modulate(x, norm_g[i, 2], sh2, sc2)
        m_l = ec_moe(h_l, moe_router[i], moe_w_gate[i], moe_w_up[i], moe_w_down[i])
        x = x + (g2 * rmsnorm(m_l, norm_g[i, 3]).astype(F32)).astype(x.dtype)

        if need_ctx:
            y_c = jnp.concatenate([ya_c, yb_c, yc_c, yd_c], axis=-1) @ w_out[i]
            xc = xc + (g1c * rmsnorm(y_c, norm_g[i, 1]).astype(F32)).astype(xc.dtype)
            h_c = modulate(xc, norm_g[i, 2], sh2c, sc2c)
            m_c = ec_moe(h_c, moe_router[i], moe_w_gate[i], moe_w_up[i], moe_w_down[i])
            xc = xc + (g2c * rmsnorm(m_c, norm_g[i, 3]).astype(F32)).astype(xc.dtype)
    return x


_drawn_inputs = setup_inputs


def setup_inputs(seed=0):
    import zlib

    import numpy as np

    out = dict(_drawn_inputs(seed))
    spreads = {}
    factors = {'ctx': 2.688,
     'c_ctx': 2.747,
     'gla_b': 2.947,
     'gla_norm': 2.96,
     'mb_conv_b': 4.334,
     'mb_d': 6.671,
     'mb_norm': 3.189,
     'dn_norm': 2.945}
    for name, (base, spread) in spreads.items():
        noise = np.random.default_rng([zlib.crc32(name.encode()), seed]).standard_normal(out[name].shape)
        drawn = base * np.exp(spread * noise) if base else spread * noise
        out[name] = jnp.asarray(drawn.astype(out[name].dtype))
    for name, factor in factors.items():
        out[name] = (out[name] * factor).astype(out[name].dtype)
    return out
```

```python
import math
from collections import namedtuple
from contextlib import contextmanager

import numpy as np

import concourse.bass as bass
from concourse import mybir

F32 = mybir.dt.float32
U32 = mybir.dt.uint32
ACT = mybir.ActivationFunctionType
ALU = mybir.AluOpType
AX = mybir.AxisListType

P = 128
D = 1024
KD = D // P
SEQ, CTX = 1024, 256
TOK = SEQ + CTX
CT, LT = CTX // P, SEQ // P
T = CT + LT
GRID_W = 64
GRID_H = SEQ // GRID_W
N_MOD = 6
EPS = 1e-6
DG = 256
HEADS = 4
HV = DG // HEADS
GLA_DK = 32
GLA_RANK = 16
GLA_TAU = 16.0
GLA_COLS, HY_COLS, MB_COLS, DN_COLS = 800, 768, 1032, 1040
HY0, MB0, DN0 = 800, 1568, 2600
WCOLS = 1040
NE = 16
CAP = 2 * SEQ // NE
FF = 1024
BIG = 1.0e30
BANK = 512
CHUNKS = ((0, 256), (256, 512), (768, 512))
PADS = (0, 257, 258, 1283)
CTX_AT, LAT_AT = 1, 259

SBUF0, SBUF_END = 16512, 229344


def tables():
    i = np.arange(P)
    j, c = i[:, None], i[None, :]
    f = np.float32
    low = (j <= c).astype(f)
    up = (j >= c).astype(f)
    mid = P // 2
    tabs = {}
    tabs["ident"] = np.eye(P, dtype=f)
    for name, m, strict_after in (("f", low, (j > c).astype(f)), ("b", up, (j < c).astype(f))):
        tabs["tri_" + name] = m
        tabs["after_" + name] = strict_after
        tabs["neg_" + name] = ((1.0 - m) * -BIG).astype(f)
    tabs["head32"] = np.repeat((j // GLA_DK == np.arange(4)[None, :]).astype(f), 1, axis=1)
    wide = {}
    for name, m in (("f", low), ("b", up)):
        cm = np.concatenate([m - m[:, mid:mid + 1], m[:, mid:mid + 1], np.ones((P, 1), f)], axis=1) / GLA_TAU
        wide["gcum_" + name] = cm.astype(f)
        wide["gafter_" + name] = (tabs["after_" + name] / GLA_TAU).astype(f)
    levels = []
    s = 1
    while s < P:
        m = ((j // (2 * s) == c // (2 * s)) & (j // s != c // s) & (j > c)).astype(f)
        levels.append(m)
        s *= 2
    tabs["levels_f"] = np.stack(levels, 1).reshape(P, -1)
    tabs["levels_b"] = np.stack([m.T for m in levels], 1).reshape(P, -1)
    gbd = (j // GLA_DK == np.arange(DG)[None, :] // HV).astype(f)
    wide["gla_bd"] = gbd
    q = np.arange(DG)[None, :]
    tabs["dn_bd"] = (j // HV == (q % P) // HV).astype(f)
    tabs["half"] = (j // HV == np.arange(2)[None, :]).astype(f)

    def packed(ts):
        offs, at = {}, 0
        for n, m in ts.items():
            offs[n] = (at, m.shape[1])
            at += m.shape[1]
        return np.ascontiguousarray(np.concatenate(list(ts.values()), 1)), offs

    return packed(tabs), packed(wide)


HALF = SEQ // 2
HT = HALF // P


def even_odd(t):
    return 2 * P * (t % HT) + t // HT


PARITY = np.concatenate([np.arange(0, SEQ, 2), np.arange(1, SEQ, 2)])


def dft_tables():
    n = np.arange(SEQ, dtype=np.float64)[:, None]
    th = math.pi * (2 * np.arange(HALF)[None, :] + 1) / (2 * SEQ)
    half = np.stack([np.cos(th * (n + 0.5)), np.sin(th * (n + 0.5))]).astype(np.float32)
    whole = np.stack([np.cos(th * n), np.sin(th * n)]).astype(np.float32)
    half, whole = half[:, PARITY], whole[:, PARITY]
    return half, np.ascontiguousarray(half.transpose(0, 2, 1)), whole


def filter_tables():
    pos = np.arange(SEQ, dtype=np.float32)
    t = pos / np.float32(SEQ - 1)
    bands = np.linspace(1e-4, 15, 16, dtype=np.float32)
    ang = np.float32(2.0 * math.pi / SEQ) * pos[:, None] * bands[None, :]
    feats = np.concatenate([t[:, None], np.cos(ang), -np.sin(ang)], axis=-1).astype(np.float32)
    lo, hi = math.log(1e-2) / 1.5, math.log(1e-2) / 0.3
    deltas = np.abs(np.linspace(lo, hi, DG, dtype=np.float32))
    window = np.exp(-t[:, None] * deltas[None, :]).astype(np.float32) / np.float32(SEQ)
    return np.ascontiguousarray(feats.T[:, PARITY]), np.ascontiguousarray(window[PARITY])


def shape_tables():
    (tab, _), (gla_tab, _) = tables()
    half, half_t, whole = dft_tables()
    feats, window = filter_tables()
    return {"tab": tab, "gla_tab": gla_tab, "dft_fwd": half, "dft_inv": half_t, "dft_whole": whole, "feats": feats, "window": window}


class Plan:

    def __init__(self, nc, at, end=SBUF_END):
        self.nc, self.at, self.end = nc, at, end

    def take(self, name, shape, dtype=F32):
        n = int(np.prod(shape[1:])) * 4
        t = self.nc.alloc_sbuf_tensor_at(name, list(shape), dtype, offset=self.at)
        self.at += (n + 31) // 32 * 32
        assert self.at <= self.end, (name, self.at, self.end)
        return t


class Chain:

    def __init__(self, eng, sem):
        self.eng, self.sem, self.n = eng, sem, 0

    def __call__(self, ins):
        self.n += 1
        ins.then_inc(self.sem, 1)
        self.eng.wait_ge(self.sem, self.n)


SPENT = []
SPENT_MAX = 110


@contextmanager
def Stage(nc, name, sems):
    if len(SPENT) > SPENT_MAX:
        nc.clear_and_free_semaphores(list(SPENT))
        nc.all_engine_barrier()
        SPENT.clear()
    named = {}
    for n in sems.split():
        n, _, ring = n.partition("*")
        got = [nc.alloc_semaphore(f"{name}_{n}{i}") for i in range(int(ring or 1))]
        SPENT.extend(got)
        named[n] = got if ring else got[0]
    with nc.Block() as block:
        yield namedtuple("Signals", ["block", *named])(block, *named.values())


class Store:
    pass


def load_and_modulate(nc, S, A):
    off = S.off
    with Stage(nc, "mod", "params rows_in silu_c wmod*2 cols_done pcols_t pcols mod_done vecs act dve chain out") as s:
        plan = Plan(nc, S.hT_at)
        wm = [plan.take(f"w_mod{b}", [P, KD, D]) for b in range(2)]
        cc = plan.take("cond", [P, 2, KD])
        sc = plan.take("silu_cond", [P, KD, 2])
        prow = plan.take("param_rows", [66, P])
        bmod = plan.take("b_mod_cols", [P, N_MOD, KD])
        ngc = plan.take("norm_g_cols", [P, 4, KD])
        modc = plan.take("mod_cols", [P, N_MOD, KD, 2])
        vec = plan.take("row_vectors", [P, 4, KD])
        n_small = [0]

        @s.block.sync
        def _(sp):
            def load(dst, src):
                sp.dma_start(dst, src).then_inc(s.params, 16)
                n_small[0] += 16
            load(S.tab[:, :], A["tab"])
            load(cc[:, 0, :], A["c"].rearrange("a (p k) -> p (a k)", p=P))
            load(cc[:, 1, :], A["c_ctx"].rearrange("(p k) -> p k", p=P))
            load(prow[0:18, :], A["hy_conv_w"].rearrange("a t (b p) -> (a t b) p", p=P))
            load(prow[18:24, :], A["hy_conv_b"].rearrange("a (b p) -> (a b) p", p=P))
            load(prow[24:42, :], A["mb_conv_w"].rearrange("a t (b p) -> (a t b) p", p=P))
            load(prow[42:48, :], A["mb_conv_b"].rearrange("a (b p) -> (a b) p", p=P))
            load(prow[48:66, :], A["dn_conv_w"].rearrange("a t (b p) -> (a t b) p", p=P))
            load(bmod[:, :, :], A["b_mod"].rearrange("a (j p k) -> p (a j) k", p=P, k=KD))
            load(ngc[:, :, :], A["norm_g"].rearrange("a j (p k) -> p (a j) k", p=P))
            for dst, src in ((S.gla_norm, A["gla_norm"]), (S.mb_norm, A["mb_norm"]), (S.dn_norm, A["dn_norm"])):
                sp.dma_start(dst[:, :], src.rearrange("a n -> (a n)").partition_broadcast(P)).then_inc(s.rows_in, 16)
            for i, n in enumerate(("mb_a_log", "mb_dt_bias", "dn_a_log", "dn_dt_bias")):
                sp.dma_start(S.gates[:, i, :], A[n].rearrange("a d h -> (a d h)").partition_broadcast(P)
                             ).then_inc(s.rows_in, 16)
            sp.dma_start(S.mb_d[:, :], A["mb_d"].rearrange("a h -> (a h)").partition_broadcast(P)
                         ).then_inc(s.rows_in, 16)
            for j in range(N_MOD):
                if j >= 2:
                    sp.wait_ge(s.cols_done, j - 1)
                sp.dma_start(wm[j % 2][:, :, :],
                             A["w_mod"][0, :, j * D:(j + 1) * D].rearrange("(p k) n -> p k n", p=P)
                             ).then_inc(s.wmod[j % 2], 16)
            sp.wait_ge(s.rows_in, 8 * 16)
            sp.wait_ge(s.vecs, 1)
            sp.dma_start(A["rows"].rearrange("j (p k) -> p j k", p=P), vec[:, :, :]).then_inc(s.out, 16)
            sp.wait_ge(s.out, 16)

        @s.block.scalar
        def _(act):
            act.wait_ge(s.params, n_small[0])
            nc.scalar.activation(sc[:, :, :].rearrange("p k s -> p s k"), cc[:, :, :], ACT.Silu).then_inc(s.silu_c, 1)

        @s.block.tensor
        def _(pe):
            pe.wait_ge(s.params, n_small[0])
            nc.tensor.transpose(S.ps[:, 1, 0:66], prow[:, :], S.t("ident")[0:66, 0:66]).then_inc(s.pcols_t, 1)
            pe.wait_ge(s.silu_c, 1)
            for j in range(N_MOD):
                pe.wait_ge(s.wmod[j % 2], 16 * (j // 2 + 1))
                for k in range(KD):
                    for kk in range(KD):
                        last = nc.tensor.matmul(S.ps[:, 0, (j * KD + k) * 2:(j * KD + k) * 2 + 2],
                                                wm[j % 2][:, kk, k::KD], sc[:, kk, :],
                                                start=(kk == 0), stop=(kk == KD - 1))
                last.then_inc(s.cols_done, 1)

        @s.block.vector
        def _(dve):
            ch = Chain(dve, s.chain)
            dve.wait_ge(s.pcols_t, 1)
            ch(nc.vector.tensor_copy(S.pcols[:, 0:66], S.ps[:, 1, 0:66]))
            ch(nc.vector.memset(S.pcols[:, 66:69], 0.0))
            ch(nc.vector.memset(S.pcols[:, 67:68], 1.0))
            dve.wait_ge(s.params, n_small[0])
            dve.wait_ge(s.cols_done, N_MOD)
            m = S.ps[:, 0, 0:N_MOD * KD * 2].rearrange("p (j k s) -> p j k s", j=N_MOD, k=KD)
            for st in range(2):
                ch(nc.vector.tensor_tensor(modc[:, :, :, st], m[:, :, :, st], bmod[:, :, :], ALU.add))
            for st in range(2):
                ch(nc.vector.scalar_tensor_tensor(S.mod1[:, 0, st, :], modc[:, 1, :, st], 1.0, ngc[:, 0, :],
                                                  ALU.add, ALU.mult))
                ch(nc.vector.tensor_copy(S.mod1[:, 1, st, :], modc[:, 0, :, st]))
            ch(nc.vector.tensor_tensor(vec[:, 0, :], modc[:, 2, :, 0], ngc[:, 1, :], ALU.mult))
            ch(nc.vector.scalar_tensor_tensor(vec[:, 1, :], modc[:, 4, :, 0], 1.0, ngc[:, 2, :], ALU.add, ALU.mult))
            ch(nc.vector.tensor_copy(vec[:, 2, :], modc[:, 3, :, 0]))
            nc.vector.tensor_tensor(vec[:, 3, :], modc[:, 5, :, 0], ngc[:, 3, :], ALU.mult).then_inc(s.vecs, 1)


def normalise(nc, S, A):
    with Stage(nc, "nrm", "x_in*3 ss rt xs_done tr evac_a evac_v chain w_in freed") as s:
        plan = Plan(nc, S.stage_at)
        xt = [plan.take(f"x_tile{b}", [P, D]) for b in range(3)]
        xn = [plan.take(f"x_norm{b}", [P, D]) for b in range(2)]
        sq = plan.take("x_square", [P, D])
        ss = plan.take("x_sum", [P, T, 3])

        @s.block.sync
        def _(sp):
            for t in range(T):
                src = A["ctx"][0, t * P:(t + 1) * P, :] if t < CT else A["x"][0, (t - CT) * P:(t - CT + 1) * P, :]
                if t >= 3:
                    sp.wait_ge(s.xs_done, t - 2)
                sp.dma_start(xt[t % 3][:, :], src).then_inc(s.x_in[t % 3], 16)
            load_weights(sp, S, A, 0, GLA_COLS)

        def evac(act, t):
            act.wait_ge(s.tr, t + 1)
            st = 1 if t < CT else 0
            for k in range(4):
                last = nc.scalar.activation(S.hT[:, k, t * P:(t + 1) * P],
                                            S.ps[:, 2 * (t % 2), k * P:(k + 1) * P], ACT.Identity,
                                            bias=S.mod1[:, 1, st, k:k + 1], scale=S.mod1[:, 0, st, k:k + 1])
            last.then_inc(s.evac_a, 1)

        @s.block.scalar
        def _(act):
            for t in range(T):
                act.wait_ge(s.x_in[t % 3], 16 * (t // 3 + 1))
                if t >= 1:
                    act.wait_ge(s.ss, t)
                nc.scalar.activation(sq[:, :], xt[t % 3][:, :], ACT.Square, accum_out=ss[:, t, 0:1]).then_inc(s.ss, 1)
                act.wait_ge(s.ss, t + 1)
                nc.scalar.activation(ss[:, t, 1:2], ss[:, t, 0:1], ACT.Sqrt, bias=S.eps[:, 0:1], scale=1.0 / D
                                     ).then_inc(s.rt, 1)
                if t >= 1:
                    evac(act, t - 1)
            evac(act, T - 1)

        @s.block.vector
        def _(dve):
            ch = Chain(dve, s.chain)

            def evac_v(t):
                dve.wait_ge(s.tr, t + 1)
                st = 1 if t < CT else 0
                for k in range(4, 8):
                    last = nc.vector.tensor_scalar(S.hT[:, k, t * P:(t + 1) * P],
                                                   S.ps[:, 2 * (t % 2) + 1, (k - 4) * P:(k - 3) * P],
                                                   S.mod1[:, 0, st, k:k + 1], S.mod1[:, 1, st, k:k + 1],
                                                   ALU.mult, ALU.add)
                last.then_inc(s.evac_v, 1)

            for t in range(T):
                dve.wait_ge(s.rt, t + 1)
                ch(nc.vector.reciprocal(ss[:, t, 2:3], ss[:, t, 1:2]))
                if t >= 2:
                    dve.wait_ge(s.tr, t - 1)
                nc.vector.tensor_scalar(xn[t % 2][:, :], xt[t % 3][:, :], ss[:, t, 2:3], None, ALU.mult
                                        ).then_inc(s.xs_done, 1)
                if t >= 1:
                    evac_v(t - 1)
            evac_v(T - 1)

        @s.block.tensor
        def _(pe):
            for t in range(T):
                pe.wait_ge(s.xs_done, t + 1)
                if t >= 2:
                    pe.wait_ge(s.evac_a, t - 1)
                    pe.wait_ge(s.evac_v, t - 1)
                for k in range(KD):
                    last = nc.tensor.transpose(S.ps[:, 2 * (t % 2) + k // 4, (k % 4) * P:(k % 4 + 1) * P],
                                               xn[t % 2][:, k::KD], S.t("ident"))
                last.then_inc(s.tr, 1)


def load_weights(sp, S, A, col, n):
    src = A["w_in"][0, :, col:col + n].rearrange("(p k) n -> p k n", p=P)
    for h in range(2):
        sp.dma_start(S.w[:, 4 * h:4 * h + 4, 0:n], src[:, 4 * h:4 * h + 4, :]).then_inc(S.w_ready, 16)
    S.w_count += 32


def project_conv(nc, S, A, name, blocks, plan, ctx=True):
    chunks = CHUNKS if ctx else CHUNKS[1:]
    groups = ((0, 2), (2, 6), (6, 10)) if ctx else ((2, 6), (6, 10))
    NC = len(chunks)
    lo = CTX_AT if ctx else LAT_AT
    tok0 = 0 if ctx else CTX
    t_first = 0 if ctx else CT
    with Stage(nc, name, "zeroed prod evac centre conv_ch conv_done act_ch lines tok_t tok_e cm_done") as s:
        line = [plan.take(f"{name}_line{b}", [P, 1284]) for b in range(2)]
        cv = [plan.take(f"{name}_conv{b}", [P, 1284]) for b in range(2)]
        out = [plan.take(f"{name}_act{b}", [P, TOK]) for b in range(2)]
        NB = len(blocks)
        toks = [i for i, b in enumerate(blocks) if b["tok"] is not None]

        def dst(i):
            return blocks[i]["cm"] if blocks[i]["cm"] is not None else out[i % 2][:, :]

        @s.block.gpsimd
        def _(pool):
            for b in range(2):
                last = nc.gpsimd.memset(line[b][:, 0:1], 0.0)
                last = nc.gpsimd.memset(line[b][:, 257:259], 0.0)
                last = nc.gpsimd.memset(line[b][:, 1283:1284], 0.0)
            last.then_inc(s.zeroed, 1)

        def to_tokens(pe, i):
            b = blocks[i]
            pe.wait_ge(s.cm_done, i + 1)
            n = toks.index(i)
            for g, (t0, t1) in enumerate(groups):
                if n * NC + g >= 2:
                    pe.wait_ge(s.tok_e, n * NC + g - 1)
                for t in range(t0, t1):
                    if b.get("by_parity"):
                        at = even_odd(t - CT)
                        src = dst(i)[:, at:at + 2 * P - 1:2]
                    else:
                        src = dst(i)[:, t * P - tok0:(t + 1) * P - tok0]
                    last = nc.tensor.transpose(S.ps[:, 6 + (n * NC + g) % 2, (t - t0) * P:(t - t0 + 1) * P], src,
                                               S.t("ident"))
                last.then_inc(s.tok_t, 1)

        @s.block.tensor
        def _(pe):
            pe.wait_ge(S.w_ready, S.w_count)
            for i, b in enumerate(blocks):
                for c, (t0, n) in enumerate(chunks):
                    if i >= 2:
                        pe.wait_ge(s.evac, NC * (i - 2) + c + 1)
                    for k in range(KD):
                        last = nc.tensor.matmul(S.ps[:, 3 * (i % 2) + c, 0:n], S.w[:, k, b["col"]:b["col"] + P],
                                                S.hT[:, k, t0:t0 + n], start=(k == 0), stop=(k == KD - 1))
                    last.then_inc(s.prod, 1)
                if i >= 1 and blocks[i - 1]["tok"] is not None:
                    to_tokens(pe, i - 1)
            if blocks[NB - 1]["tok"] is not None:
                to_tokens(pe, NB - 1)

        @s.block.scalar
        def _(act):
            act.wait_ge(s.zeroed, 1)

            def finish(i):
                b = blocks[i]
                act.wait_ge(s.conv_done, i + 1)
                if i >= 2 and blocks[i - 2]["tok"] is not None and blocks[i - 2]["cm"] is None:
                    act.wait_ge(s.tok_t, NC * (toks.index(i - 2) + 1))
                d = dst(i)
                c = cv[i % 2]
                f = ACT.Silu if b["silu"] else ACT.Identity
                if ctx:
                    nc.scalar.activation(d[:, 0:CTX], c[:, CTX_AT:CTX_AT + CTX], f)
                nc.scalar.activation(d[:, CTX - tok0:TOK - tok0], c[:, LAT_AT:LAT_AT + SEQ], f).then_inc(s.cm_done, 1)

            for i, b in enumerate(blocks):
                if i >= 2:
                    act.wait_ge(s.conv_done, i - 1)
                for c, (t0, n) in enumerate(chunks):
                    act.wait_ge(s.prod, NC * i + c + 1)
                    src = S.ps[:, 3 * (i % 2) + c, 0:n]
                    if t0 < CTX:
                        d = line[i % 2][:, CTX_AT:CTX_AT + CTX]
                    else:
                        l0 = t0 - CTX
                        r0 = l0 // GRID_W
                        if b["colmajor"]:
                            d = line[i % 2][:, LAT_AT:LAT_AT + SEQ].rearrange("p (w r) -> p r w", r=GRID_H)
                            d = d[:, r0:r0 + 8, :]
                            src = src.rearrange("p (r w) -> p r w", w=GRID_W)
                        else:
                            d = line[i % 2][:, LAT_AT + l0:LAT_AT + l0 + n]
                    nc.scalar.activation(d, src, ACT.Copy).then_inc(s.evac, 1)
                act.wait_ge(s.evac, NC * (i + 1))
                if i >= 2:
                    act.wait_ge(s.cm_done, i - 1)
                bias = S.pcols[:, b["bias"]:b["bias"] + 1] if b["bias"] is not None else S.zero[:, 0:1]
                w1 = b["tap"] + b["step"]
                nc.scalar.activation(cv[i % 2][:, lo:1283], line[i % 2][:, lo:1283], ACT.Identity, bias=bias,
                                     scale=S.pcols[:, w1:w1 + 1]).then_inc(s.centre, 1)
                if i >= 1:
                    finish(i - 1)
            finish(NB - 1)

        @s.block.vector
        def _(dve):
            ch = Chain(dve, s.conv_ch)

            def copy_tokens(i):
                b = blocks[i]
                n = toks.index(i)
                for g, (t0, t1) in enumerate(groups):
                    dve.wait_ge(s.tok_t, n * NC + g + 1)
                    src = S.ps[:, 6 + (n * NC + g) % 2, 0:(t1 - t0) * P].rearrange("p (t c) -> p t c", c=P)
                    a0 = CT if b.get("latents") else t_first
                    if t1 <= a0:
                        nc.vector.engine_nop().then_inc(s.tok_e, 1)
                    else:
                        nc.vector.tensor_copy(b["tok"][:, t0 - a0:t1 - a0, :], src[:, :, b.get("sub", 0):P]
                                              ).then_inc(s.tok_e, 1)

            for i, b in enumerate(blocks):
                dve.wait_ge(s.centre, i + 1)
                c, l = cv[i % 2], line[i % 2]
                ch(nc.vector.scalar_tensor_tensor(c[:, lo:1283], l[:, lo - 1:1282], S.pcols[:, b["tap"]:b["tap"] + 1],
                                                  c[:, lo:1283], ALU.mult, ALU.add))
                w2 = b["tap"] + 2 * b["step"]
                nc.vector.scalar_tensor_tensor(c[:, lo:1283], l[:, lo + 1:1284], S.pcols[:, w2:w2 + 1],
                                               c[:, lo:1283], ALU.mult, ALU.add).then_inc(s.conv_done, 1)
                if i >= 1 and blocks[i - 1]["tok"] is not None:
                    copy_tokens(i - 1)
            if blocks[NB - 1]["tok"] is not None:
                copy_tokens(NB - 1)


def token_products(nc, S, s, pe, jobs):
    pe.wait_ge(S.w_ready, S.w_count)
    for i, (t, col, n) in enumerate(jobs):
        if i >= 6:
            pe.wait_ge(s.tp_out, i - 5)
        for k in range(KD):
            lhs = S.hT[:, k, t * P:(t + 1) * P]
            last = nc.tensor.matmul(S.ps[:, i % 6, 0:n], lhs, S.w[:, k, col:col + n], start=(k == 0), stop=(k == KD - 1))
        last.then_inc(s.tp, 1)


def token_copies(nc, S, s, act, jobs, dsts):
    for i in range(len(jobs)):
        act.wait_ge(s.tp, i + 1)
        for d, a, n in dsts[i]:
            last = nc.scalar.activation(d, S.ps[:, i % 6, a:a + n], ACT.Copy)
        last.then_inc(s.tp_out, 1)


def head_norm(nc, S, name, o, gate, norm_w, gate_first, block0, plan, colmajor, extra=None, loads=None):
    with Stage(nc, name, "sil sq red rt chain tr cp") as s:
        n = LT * HEADS
        sq = plan.take(name + "_sq", [P, LT, DG])
        st = plan.take(name + "_stat", [P, 3, n])
        o4 = o[:, :, :].rearrange("p t (h v) -> p (t h) v", v=HV)

        if loads is not None:
            @s.block.sync
            def _(sp):
                loads(sp)

        @s.block.scalar
        def _(act):
            nc.scalar.activation(gate[:, :, :], gate[:, :, :], ACT.Silu).then_inc(s.sil, 1)
            act.wait_ge(s.red, 1)
            nc.scalar.activation(st[:, 1, :], st[:, 0, :], ACT.Sqrt, bias=S.eps[:, 0:1], scale=1.0 / HV
                                 ).then_inc(s.rt, 1)
            for i in range(4):
                act.wait_ge(s.tr, i + 1)
                kb, half = i // 2, i % 2
                if colmajor:
                    d = S.yT[:, block0 + kb, :].rearrange("p (r w) -> p w r", w=GRID_W)
                    d = d[:, half * 32:half * 32 + 32, :]
                    src = S.ps[:, i % 2, :].rearrange("p (w r) -> p w r", r=GRID_H)
                else:
                    d = S.yT[:, block0 + kb, half * 512:half * 512 + 512]
                    src = S.ps[:, i % 2, :]
                nc.scalar.activation(d, src, ACT.Copy).then_inc(s.cp, 1)

        @s.block.vector
        def _(dve):
            ch = Chain(dve, s.chain)
            if extra is not None:
                extra(dve, ch)
            dve.wait_ge(s.sil, 1)
            if gate_first:
                ch(nc.vector.tensor_tensor(o[:, :, :], o[:, :, :], gate[:, :, :], ALU.mult))
            ch(nc.vector.tensor_tensor(sq[:, :, :], o[:, :, :], o[:, :, :], ALU.mult))
            nc.vector.tensor_reduce(st[:, 0, :], sq[:, :, :].rearrange("p t (h v) -> p (t h) v", v=HV), AX.X, ALU.add
                                    ).then_inc(s.red, 1)
            dve.wait_ge(s.rt, 1)
            ch(nc.vector.reciprocal(st[:, 2, :], st[:, 1, :]))
            ch(nc.vector.tensor_tensor(o4, o4, st[:, 2, :].unsqueeze(2).to_broadcast([P, n, HV]), ALU.mult))
            w = norm_w[:, :].unsqueeze(1).to_broadcast([P, LT, DG])
            if gate_first:
                nc.vector.tensor_tensor(o[:, :, :], o[:, :, :], w, ALU.mult).then_inc(s.sq, 1)
            else:
                ch(nc.vector.tensor_tensor(o[:, :, :], o[:, :, :], w, ALU.mult))
                nc.vector.tensor_tensor(o[:, :, :], o[:, :, :], gate[:, :, :], ALU.mult).then_inc(s.sq, 1)

        @s.block.tensor
        def _(pe):
            pe.wait_ge(s.sq, 1)
            for i in range(4):
                kb, half = i // 2, i % 2
                if i >= 2:
                    pe.wait_ge(s.cp, i - 1)
                for t in range(4):
                    last = nc.tensor.transpose(S.ps[:, i % 2, t * P:(t + 1) * P],
                                               o[:, half * 4 + t, kb * P:(kb + 1) * P], S.t("ident"))
                last.then_inc(s.tr, 1)


ORDER = {"f": list(range(T)), "b": [1, 0] + list(range(T - 1, CT - 1, -1))}


def units():
    return [(2 * st + d, st, d, ORDER["fb"[d]][st]) for st in range(T) for d in range(2)]


def gla(nc, S, A):
    plan = Plan(nc, S.stage_at)
    v = plan.take("gla_v", [P, T, DG])
    og = plan.take("gla_og", [P, LT, DG])
    kt = plan.take("gla_k_tok", [P, T, P])
    qT = plan.take("gla_qT", [P, TOK])
    kT = plan.take("gla_kT", [P, TOK])
    la = plan.take("gla_log_alpha", [P, T, 2, P])
    o = plan.take("gla_o", [P, LT, DG])
    gt = plan.take("gla_tables", [P, S.gn])
    goff = S.goff

    def G(name):
        return gt[:, goff[name][0]:goff[name][0] + goff[name][1]]

    mark = plan.at
    with Stage(nc, "gla_p", "tabs ones w2 w2_in prod evac tp tp_out z e1 e2 abs_done chain") as s:
        lr = plan.take("gla_lrT", [33, TOK])
        w2 = plan.take("gla_w2", [33, 2, P])
        ab = plan.take("gla_abs", [P, T, 2, P])
        cms = ((0, P, qT, GLA_DK ** -0.5), (P, P, kT, 1.0), (768, 32, lr, 1.0))
        jobs, dsts = [], []
        for t in range(T):
            jobs.append((t, 128, 512 if t >= CT else 384))
            d = [(kt[:, t, :], 0, P), (v[:, t, :], P, DG)]
            if t >= CT:
                d.append((og[:, t - CT, 0:128], 384, 128))
                dsts.append(d)
                jobs.append((t, 640, 128))
                d = [(og[:, t - CT, 128:256], 0, 128)]
            dsts.append(d)

        @s.block.sync
        def _(sp):
            sp.dma_start(gt[:, :], A["gla_tab"]).then_inc(s.tabs, 16)
            sp.wait_ge(s.w2, 1)
            for d in range(2):
                sp.dma_start(w2[16 * d:16 * d + 16, d, :], A["gla_w2"][0, d, :, :]).then_inc(s.w2_in, 16)
            sp.dma_start(w2[32:33, :, :], A["gla_b"]).then_inc(s.w2_in, 16)
            sp.wait_ge(s.tabs, 16)

        @s.block.gpsimd
        def _(pool):
            nc.gpsimd.memset(lr[32:33, :], 1.0).then_inc(s.ones, 1)
            pool.wait_ge(s.ones, 1)
            nc.gpsimd.memset(w2[:, :, :], 0.0).then_inc(s.w2, 1)

        @s.block.tensor
        def _(pe):
            pe.wait_ge(S.w_ready, S.w_count)
            for i, (col, m, dst, _) in enumerate(cms):
                for c, (t0, n) in enumerate(CHUNKS):
                    q = 3 * i + c
                    if q >= 6:
                        pe.wait_ge(s.evac, q - 5)
                    for k in range(KD):
                        last = nc.tensor.matmul(S.ps[0:m, q % 6, 0:n], S.w[:, k, col:col + m], S.hT[:, k, t0:t0 + n],
                                                start=(k == 0), stop=(k == KD - 1))
                    last.then_inc(s.prod, 1)
            pe.wait_ge(s.evac, 9)
            token_products(nc, S, s, pe, jobs)
            pe.wait_ge(s.tp_out, len(jobs))
            pe.wait_ge(s.w2_in, 48)
            pe.wait_ge(s.ones, 1)
            for t in range(T):
                last = nc.tensor.matmul(S.ps[:, t // 2, (t % 2) * 256:(t % 2) * 256 + 256],
                                        lr[:, t * P:(t + 1) * P], w2[:, :, :].rearrange("p d c -> p (d c)"),
                                        start=True, stop=True)
            last.then_inc(s.z, 1)

        @s.block.scalar
        def _(act):
            for i, (col, m, dst, scale) in enumerate(cms):
                for c, (t0, n) in enumerate(CHUNKS):
                    q = 3 * i + c
                    act.wait_ge(s.prod, q + 1)
                    nc.scalar.activation(dst[0:m, t0:t0 + n], S.ps[0:m, q % 6, 0:n], ACT.Copy, scale=scale
                                         ).then_inc(s.evac, 1)
            token_copies(nc, S, s, act, jobs, dsts)
            act.wait_ge(s.z, 1)
            nc.scalar.activation(ab[:, :, :, :].rearrange("p t d c -> p (t d c)"),
                                 S.ps[:, 0:5, :].rearrange("p b n -> p (b n)"), ACT.Abs).then_inc(s.abs_done, 1)
            act.wait_ge(s.abs_done, 1)
            nc.scalar.activation(ab[:, :, :, :], ab[:, :, :, :], ACT.Exp, scale=-1.0).then_inc(s.e1, 1)
            act.wait_ge(s.e1, 1)
            nc.scalar.activation(ab[:, :, :, :], ab[:, :, :, :], ACT.Ln, bias=S.one[:, 0:1]).then_inc(s.e2, 1)

        @s.block.vector
        def _(dve):
            dve.wait_ge(s.z, 1)
            z = S.ps[:, 0:5, :].rearrange("p b n -> p (b n)")
            abf = ab[:, :, :, :].rearrange("p t d c -> p (t d c)")
            dve.wait_ge(s.e2, 1)
            nc.vector.scalar_tensor_tensor(la[:, :, :, :].rearrange("p t d c -> p (t d c)"), z, 0.0, abf,
                                           ALU.min, ALU.subtract).then_inc(s.chain, 1)

    plan.at = mark
    with Stage(nc, "gla_s", "cum exps prep_v prep_p attn masked o kv s_use s_ch o_out chain pch lastq") as s:
        ex = [plan.take(f"gla_exp{b}", [P, 258]) for b in range(3)]
        en = [plan.take(f"gla_expn{b}", [P, P]) for b in range(3)]
        qg = [plan.take(f"gla_qg{b}", [P, P]) for b in range(3)]
        qb = [plan.take(f"gla_qbd{b}", [P, HEADS, P]) for b in range(3)]
        kg = [plan.take(f"gla_kg{b}", [P, P]) for b in range(3)]
        ke = [plan.take(f"gla_ke{b}", [P, P]) for b in range(3)]
        am = [plan.take(f"gla_attn{b}", [P, HEADS, P]) for b in range(2)]
        kv = [plan.take(f"gla_kv{b}", [P, DG]) for b in range(2)]
        Sd = [plan.take(f"gla_state{b}", [P, DG]) for b in range(2)]
        Su = [plan.take(f"gla_state_use{b}", [P, DG]) for b in range(4)]
        U = units()
        N = len(U)

        @s.block.sync
        def _(sp):
            load_weights(sp, S, A, MB0, MB_COLS)

        @s.block.tensor
        def _(pe):
            for n in range(N + 2):
                if n < N:
                    _, st, d, t = U[n]
                    dn = "fb"[d]
                    if n >= 2:
                        pe.wait_ge(s.exps, n - 1)
                    nc.tensor.matmul(S.ps[:, n % 2, 0:130], la[:, t, d, :], G("gcum_" + dn), start=True, stop=True)
                    nc.tensor.matmul(S.ps[:, n % 2, 130:258], G("gafter_" + dn), la[:, t, d, :],
                                     start=True, stop=True).then_inc(s.cum, 1)
                if 1 <= n <= N:
                    m = n - 1
                    t = U[m][3]
                    pe.wait_ge(s.prep_v, m + 1)
                    pe.wait_ge(s.prep_p, m + 1)
                    if m >= 2:
                        pe.wait_ge(s.masked, m - 1)
                        pe.wait_ge(s.s_use, m - 1)
                    nc.tensor.matmul(S.ps[:, 2 + m % 2, :], kg[m % 3][:, :], qb[m % 3][:, :, :].rearrange("p h c -> p (h c)"),
                                     start=True, stop=True).then_inc(s.attn, 1)
                    nc.tensor.matmul(S.ps[:, 6 + m % 2, 0:DG], ke[m % 3][:, :], v[:, t, :], start=True, stop=True
                                     ).then_inc(s.kv, 1)
                if n >= 2:
                    m = n - 2
                    t = U[m][3]
                    pe.wait_ge(s.masked, m + 1)
                    pe.wait_ge(s.s_use, m + 1)
                    if m >= 2:
                        pe.wait_ge(s.o_out, m - 1)
                    nc.tensor.matmul(S.ps[:, 4 + m % 2, 0:DG], qg[m % 3][:, :], Su[m % 4][:, :], start=True, stop=False,
                                     skip_group_check=True)
                    for h in range(HEADS):
                        last = nc.tensor.matmul(S.ps[:, 4 + m % 2, h * HV:(h + 1) * HV], am[m % 2][:, h, :],
                                                v[:, t, h * HV:(h + 1) * HV], start=False, stop=(h == HEADS - 1),
                                                skip_group_check=True)
                    last.then_inc(s.o, 1)

        @s.block.scalar
        def _(act):
            for n in range(N):
                act.wait_ge(s.cum, n + 1)
                if n >= 3:
                    act.wait_ge(s.prep_v, n - 2)
                    act.wait_ge(s.prep_p, n - 2)
                    act.wait_ge(s.s_use, n - 2)
                    act.wait_ge(s.s_ch, n - 2)
                nc.scalar.activation(ex[n % 3][:, :], S.ps[:, n % 2, 0:258], ACT.Exp)
                nc.scalar.activation(en[n % 3][:, :], S.ps[:, n % 2, 0:P], ACT.Exp, scale=-1.0).then_inc(s.exps, 1)

        @s.block.gpsimd
        def _(pool):
            for n in range(N):
                _, st, d, t = U[n]
                pool.wait_ge(s.exps, n + 1)
                if n >= 3:
                    pool.wait_ge(s.attn, n - 2)
                    pool.wait_ge(s.kv, n - 2)
                nc.gpsimd.tensor_tensor(kg[n % 3][:, :], kT[:, t * P:(t + 1) * P], en[n % 3][:, :], ALU.mult)
                nc.gpsimd.tensor_tensor(ke[n % 3][:, :], kt[:, t, :], ex[n % 3][:, 130:258], ALU.mult
                                        ).then_inc(s.prep_p, 1)

        @s.block.vector
        def _(dve):
            ch = Chain(dve, s.chain)
            for d in range(2):
                ch(nc.vector.memset(Sd[d][:, :], 0.0))
            hm = S.t("head32").unsqueeze(2).to_broadcast([P, HEADS, P])

            def prep(n):
                _, st, d, t = U[n]
                dve.wait_ge(s.exps, n + 1)
                if n >= 3:
                    dve.wait_ge(s.o, n - 2)
                ch(nc.vector.tensor_tensor(qg[n % 3][:, :], qT[:, t * P:(t + 1) * P], ex[n % 3][:, 0:P], ALU.mult))
                nc.vector.tensor_tensor(qb[n % 3][:, :, :], qg[n % 3][:, :].unsqueeze(1).to_broadcast([P, HEADS, P]),
                                        hm, ALU.mult).then_inc(s.prep_v, 1)

            def mask(m):
                _, st, d, t = U[m]
                dve.wait_ge(s.attn, m + 1)
                if m >= 2:
                    dve.wait_ge(s.o, m - 1)
                tri = S.t("tri_" + "fb"[d]).unsqueeze(1).to_broadcast([P, HEADS, P])
                nc.vector.tensor_tensor(am[m % 2][:, :, :], S.ps[:, 2 + m % 2, :].rearrange("p (h c) -> p h c", c=P),
                                        tri, ALU.mult).then_inc(s.masked, 1)

            def state(m):
                _, st, d, t = U[m]
                dve.wait_ge(s.kv, m + 1)
                if m >= 2:
                    dve.wait_ge(s.s_ch, m - 1)
                ch(nc.vector.tensor_tensor(kv[m % 2][:, :], S.ps[:, 6 + m % 2, 0:DG], G("gla_bd"), ALU.mult))
                if m >= 4:
                    dve.wait_ge(s.o, m - 3)
                nc.vector.tensor_scalar(Su[m % 4][:, :], Sd[d][:, :], ex[m % 3][:, P:P + 1], None, ALU.mult
                                        ).then_inc(s.s_use, 1)
                dve.wait_ge(s.s_use, m + 1)
                nc.vector.scalar_tensor_tensor(Sd[d][:, :], Sd[d][:, :], ex[m % 3][:, P + 1:P + 2], kv[m % 2][:, :],
                                               ALU.mult, ALU.add).then_inc(s.s_ch, 1)

            def take(m):
                _, st, d, t = U[m]
                dve.wait_ge(s.o, m + 1)
                add_output(nc, dve, s, S.ps[:, 4 + m % 2, 0:DG], o, st, d, t, s.o_out)

            for n in range(N + 3):
                if n < N:
                    prep(n)
                if 1 <= n <= N:
                    mask(n - 1)
                    state(n - 1)
                if 3 <= n:
                    take(n - 3)

    plan.at = mark
    head_norm(nc, S, "gla_n", o, og, S.gla_norm, False, 0, plan, False)


def add_output(nc, dve, s, src, o, st, d, t, done):
    if t < CT:
        nc.vector.engine_nop().then_inc(done, 1)
        return
    first = st < T - st + 1
    if first:
        nc.vector.tensor_copy(o[:, t - CT, :], src).then_inc(done, 1)
    else:
        dve.wait_ge(done, 2 * (T + 1 - st) + (1 - d) + 1)
        nc.vector.tensor_tensor(o[:, t - CT, :], src, o[:, t - CT, :], ALU.add).then_inc(done, 1)


def gate_sums(nc, S, s, pe, g, bank):
    out = S.ps[:, bank, 0:240].rearrange("p (w d n) -> p w d n", w=3, d=2)
    for d in range(2):
        rhs = g[:, :, d, :]
        for w, m in enumerate((S.t("tri_" + "fb"[d]), S.t("after_" + "fb"[d]), S.ones[:, :])):
            last = nc.tensor.matmul(out[:, w, d, :], m, rhs, start=True, stop=True)
    return last


def mamba(nc, S, A):
    plan = Plan(nc, S.stage_at)
    xt = plan.take("mb_x", [P, T, DG])
    bt = plan.take("mb_b", [P, T, DG])
    bT = plan.take("mb_bT", [P, 2, TOK])
    cT = plan.take("mb_cT", [P, 2, TOK])
    z = plan.take("mb_z", [P, LT, DG])
    dt = plan.take("mb_dt", [P, T, 2, HEADS])
    ga = plan.take("mb_g", [P, T, 2, HEADS])
    cu = plan.take("mb_cum", [P, 3, 2, T * HEADS])
    eu = plan.take("mb_cum_exp", [P, 3, 2, T * HEADS])
    small = plan.at
    o = plan.take("mb_o", [P, LT, DG])
    mark = plan.at
    blocks = []
    for b in range(6):
        cm = None if b < 2 else (bT if b < 4 else cT)[:, b % 2, :]
        tok = (xt if b < 2 else bt)[:, :, (b % 2) * P:(b % 2 + 1) * P] if b < 4 else None
        blocks.append(dict(col=256 + b * P, tap=24 + b, step=6, bias=42 + b, silu=True, colmajor=True, cm=cm, tok=tok))
    for b in range(2):
        blocks.append(dict(col=b * P, tap=66, step=1, bias=None, silu=False, colmajor=True, cm=None,
                           tok=z[:, :, b * P:(b + 1) * P], latents=True))
    blocks.append(dict(col=MB_COLS - P, tap=66, step=1, bias=None, silu=False, colmajor=True, cm=None,
                       tok=dt[:, :, :, :].rearrange("p t d h -> p t (d h)"), sub=P - 8))
    project_conv(nc, S, A, "mb_c", blocks, Plan(nc, small))
    with Stage(nc, "mb_t", "biased ab e1 e2 ea sp chain sums") as s:
        ab = plan.take("mb_abs", [P, T * 8])
        ea = plan.take("mb_decay", [P, 8])
        @s.block.tensor
        def _(pe):
            pe.wait_ge(s.sp, 1)
            gate_sums(nc, S, s, pe, ga, 6).then_inc(s.sums, 1)

        @s.block.scalar
        def _(act):
            act.wait_ge(s.biased, 1)
            nc.scalar.activation(ab[:, :], dt[:, :, :, :].rearrange("p t d h -> p (t d h)"), ACT.Abs).then_inc(s.ab, 1)
            act.wait_ge(s.ab, 1)
            nc.scalar.activation(ab[:, :], ab[:, :], ACT.Exp, scale=-1.0).then_inc(s.e1, 1)
            act.wait_ge(s.e1, 1)
            nc.scalar.activation(ab[:, :], ab[:, :], ACT.Ln, bias=S.one[:, 0:1]).then_inc(s.e2, 1)
            nc.scalar.activation(ea[:, :], S.gates[:, 0, :], ACT.Exp).then_inc(s.ea, 1)
            act.wait_ge(s.sums, 1)
            nc.scalar.activation(eu[:, :, :, :], S.ps[:, 6, 0:240].rearrange("p (w d n) -> p w d n", w=3, d=2), ACT.Exp
                                 ).then_inc(s.ea, 1)

        @s.block.vector
        def _(dve):
            ch = Chain(dve, s.chain)
            dtf = dt[:, :, :, :].rearrange("p t d h -> p t (d h)")
            nc.vector.tensor_tensor(dtf, dtf, S.gates[:, 1, :].unsqueeze(1).to_broadcast([P, T, 8]), ALU.add
                                    ).then_inc(s.biased, 1)
            dt1 = dt[:, :, :, :].rearrange("p t d h -> p (t d h)")
            dve.wait_ge(s.e2, 1)
            ch(nc.vector.scalar_tensor_tensor(dt1, dt1, 0.0, ab[:, :], ALU.max, ALU.add))
            dve.wait_ge(s.ea, 1)
            ch(nc.vector.tensor_scalar(ea[:, :], ea[:, :], -1.0, None, ALU.mult))
            nc.vector.tensor_tensor(ga[:, :, :, :].rearrange("p t d h -> p t (d h)"), dtf,
                                    ea[:, :].unsqueeze(1).to_broadcast([P, T, 8]), ALU.mult).then_inc(s.sp, 1)
            dve.wait_ge(s.ea, 2)
            ch(nc.vector.tensor_copy(cu[:, :, :, :], S.ps[:, 6, 0:240].rearrange("p (w d n) -> p w d n", w=3, d=2)))

    plan.at = mark
    with Stage(nc, "mb_s", "rows rel seg cb at xdt xde y y_out st s_new chain pch") as s:
        sg = [plan.take(f"mb_seg{b}", [P, HEADS, P]) for b in range(2)]
        am = [plan.take(f"mb_attn{b}", [P, HEADS, P]) for b in range(2)]
        xd = [plan.take(f"mb_xdt{b}", [P, DG]) for b in range(3)]
        xe = [plan.take(f"mb_xde{b}", [P, DG]) for b in range(3)]
        yo = [plan.take(f"mb_yo{b}", [P, DG]) for b in range(2)]
        St = [plan.take(f"mb_state{b}", [P, DG]) for b in range(2)]
        U = units()
        N = len(U)

        @s.block.sync
        def _(sp):
            load_weights(sp, S, A, DN0, DN_COLS)

        @s.block.tensor
        def _(pe):
            for n in range(N + 2):
                if n < N:
                    _, st, d, t = U[n]
                    if n >= 2:
                        pe.wait_ge(s.rel, n - 1)
                        pe.wait_ge(s.at, n - 1)
                    for h in range(HEADS):
                        last = nc.tensor.matmul(S.ps[:, n % 2, h * P:(h + 1) * P],
                                                ga[:, t, d, h:h + 1].to_broadcast([P, P]), S.t("tri_" + "fb"[d]),
                                                start=True, stop=True)
                    last.then_inc(s.rows, 1)
                    for g in range(2):
                        last = nc.tensor.matmul(S.ps[:, 2 + n % 2, g * P:(g + 1) * P], bT[:, g, t * P:(t + 1) * P],
                                                cT[:, g, t * P:(t + 1) * P], start=True, stop=True)
                    last.then_inc(s.cb, 1)
                if 1 <= n <= N:
                    m = n - 1
                    t = U[m][3]
                    pe.wait_ge(s.xde, m + 1)
                    if m >= 2:
                        pe.wait_ge(s.s_new, m - 1)
                    for g in range(2):
                        last = nc.tensor.matmul(S.ps[:, 6 + m % 2, g * P:(g + 1) * P], bt[:, t, g * P:(g + 1) * P],
                                                xe[m % 3][:, g * P:(g + 1) * P], start=True, stop=True)
                    last.then_inc(s.st, 1)
                if n >= 2:
                    m = n - 2
                    t, d = U[m][3], U[m][2]
                    pe.wait_ge(s.at, m + 1)
                    pe.wait_ge(s.s_new, m - 1) if m >= 2 else pe.wait_ge(s.chain, 2)
                    if m >= 2:
                        pe.wait_ge(s.y_out, m - 1)
                    for h in range(HEADS):
                        nc.tensor.matmul(S.ps[:, 4 + m % 2, h * HV:(h + 1) * HV], am[m % 2][:, h, :],
                                         xd[m % 3][:, h * HV:(h + 1) * HV], start=True, stop=True)
                    for g in range(2):
                        last = nc.tensor.matmul(S.ps[:, 4 + m % 2, DG + g * P:DG + (g + 1) * P],
                                                cT[:, g, t * P:(t + 1) * P], St[d][:, g * P:(g + 1) * P],
                                                start=True, stop=True)
                    last.then_inc(s.y, 1)

        @s.block.scalar
        def _(act):
            for n in range(N):
                act.wait_ge(s.rel, n + 1)
                nc.scalar.activation(sg[n % 2][:, :, :], sg[n % 2][:, :, :], ACT.Exp).then_inc(s.seg, 1)

        @s.block.gpsimd
        def _(pool):
            for n in range(N):
                _, st, d, t = U[n]
                if n >= 3:
                    pool.wait_ge(s.y, n - 2)
                    pool.wait_ge(s.st, n - 2)
                nc.gpsimd.tensor_tensor(xd[n % 3][:, :].rearrange("p (h v) -> p h v", v=HV),
                                        xt[:, t, :].rearrange("p (h v) -> p h v", v=HV),
                                        dt[:, t, d, :].unsqueeze(2).to_broadcast([P, HEADS, HV]), ALU.mult
                                        ).then_inc(s.xdt, 1)
                pool.wait_ge(s.xdt, n + 1)
                nc.gpsimd.tensor_tensor(xe[n % 3][:, :].rearrange("p (h v) -> p h v", v=HV),
                                        xd[n % 3][:, :].rearrange("p (h v) -> p h v", v=HV),
                                        eu[:, 1, d, t * HEADS:(t + 1) * HEADS].unsqueeze(2).to_broadcast([P, HEADS, HV]),
                                        ALU.mult).then_inc(s.xde, 1)

        @s.block.vector
        def _(dve):
            ch = Chain(dve, s.chain)
            for d in range(2):
                ch(nc.vector.memset(St[d][:, :], 0.0))

            def front(n):
                _, st, d, t = U[n]
                dve.wait_ge(s.rows, n + 1)
                if n >= 2:
                    dve.wait_ge(s.at, n - 1)
                for h in range(HEADS):
                    c = t * HEADS + h
                    last = nc.vector.scalar_tensor_tensor(sg[n % 2][:, h, :], S.ps[:, n % 2, h * P:(h + 1) * P],
                                                          cu[:, 0, d, c:c + 1], S.t("neg_" + "fb"[d]),
                                                          ALU.subtract, ALU.add)
                last.then_inc(s.rel, 1)

            def scores(n):
                dve.wait_ge(s.seg, n + 1)
                dve.wait_ge(s.cb, n + 1)
                if n >= 2:
                    dve.wait_ge(s.y, n - 1)
                nc.vector.tensor_tensor(am[n % 2][:, :, :].rearrange("p (g r) c -> p g r c", g=2),
                                        sg[n % 2][:, :, :].rearrange("p (g r) c -> p g r c", g=2),
                                        S.ps[:, 2 + n % 2, 0:DG].rearrange("p (g c) -> p g c", g=2).unsqueeze(2)
                                        .to_broadcast([P, 2, 2, P]), ALU.mult).then_inc(s.at, 1)

            def tail(m):
                _, st, d, t = U[m]
                cols = slice(t * HEADS, (t + 1) * HEADS)
                dve.wait_ge(s.y, m + 1)
                ch(nc.vector.tensor_tensor(yo[m % 2][:, :].rearrange("p (h v) -> p h v", v=HV),
                                           S.ps[:, 4 + m % 2, DG:2 * DG].rearrange("p (h v) -> p h v", v=HV),
                                           eu[:, 0, d, cols].unsqueeze(2).to_broadcast([P, HEADS, HV]), ALU.mult))
                if t >= CT and not st < T - st + 1:
                    dve.wait_ge(s.y_out, 2 * (T + 1 - st) + (1 - d) + 1)
                    ch(nc.vector.tensor_tensor(yo[m % 2][:, :], yo[m % 2][:, :], o[:, t - CT, :], ALU.add))
                if t >= CT:
                    nc.vector.tensor_tensor(o[:, t - CT, :], yo[m % 2][:, :], S.ps[:, 4 + m % 2, 0:DG], ALU.add
                                            ).then_inc(s.y_out, 1)
                else:
                    nc.vector.engine_nop().then_inc(s.y_out, 1)
                sd = St[d][:, :].rearrange("p (h v) -> p h v", v=HV)
                ch(nc.vector.tensor_tensor(sd, sd, eu[:, 2, d, cols].unsqueeze(2).to_broadcast([P, HEADS, HV]), ALU.mult))
                dve.wait_ge(s.st, m + 1)
                nc.vector.tensor_tensor(St[d][:, :], St[d][:, :], S.ps[:, 6 + m % 2, 0:DG], ALU.add
                                        ).then_inc(s.s_new, 1)

            for n in range(N + 3):
                if n < N:
                    front(n)
                if n >= 3:
                    tail(n - 3)
                if 1 <= n <= N:
                    scores(n - 1)

    plan.at = mark

    def skip(dve, ch):
        xl = xt[:, CT:T, :]
        for h in range(HEADS):
            hs = slice(h * HV, (h + 1) * HV)
            ch(nc.vector.scalar_tensor_tensor(o[:, :, hs], xl[:, :, hs], S.mb_d[:, h:h + 1], o[:, :, hs],
                                              ALU.mult, ALU.add))

    head_norm(nc, S, "mb_n", o, z, S.mb_norm, True, 4, plan, True, skip)


def deltanet(nc, S, A):
    plan = Plan(nc, S.stage_at)
    vt = plan.take("dn_v", [P, T, DG])
    kt = plan.take("dn_k", [P, T, DG])
    kz = plan.take("dn_kz", [P, HEADS, TOK])
    qT = plan.take("dn_qT", [P, 2, TOK])
    o = plan.take("dn_o", [P, LT, DG])
    ga = plan.take("dn_g", [P, T, 2, HEADS])
    be = plan.take("dn_beta", [P, T, 2, HEADS])
    bec = plan.take("dn_beta_cum", [P, 2, T * HEADS])
    cu = plan.take("dn_cum", [P, 3, 2, T * HEADS])
    eu = plan.take("dn_cum_exp", [P, 3, 2, T * HEADS])
    mark = plan.at
    qt = nc.alloc_sbuf_tensor_at("dn_q", [P, T, DG], F32, offset=S.stage_at + 2 * T * DG * 4)
    plan = Plan(nc, S.stage_at + 3 * T * DG * 4)
    blocks = []
    for b in range(6):
        tok = (qt, kt, vt)[b // 2][:, :, (b % 2) * P:(b % 2 + 1) * P]
        blocks.append(dict(col=b * P, tap=48 + b, step=6, bias=None, silu=True, colmajor=False, cm=None, tok=tok))
    project_conv(nc, S, A, "dn_c", blocks, plan)

    plan = Plan(nc, mark)
    with Stage(nc, "dn_l", "sq red rt normed tr tr_out chain") as s:
        sq = plan.take("dn_square", [P, T, DG])
        ss = plan.take("dn_norms", [P, 3, 2, T * HEADS])
        qc = plan.take("dn_qn", [P, T, DG])

        @s.block.vector
        def _(dve):
            ch = Chain(dve, s.chain)
            for i, x in enumerate((qt, kt)):
                ch(nc.vector.tensor_tensor(sq[:, :, :], x[:, :, :], x[:, :, :], ALU.mult))
                nc.vector.tensor_reduce(ss[:, 0, i, :], sq[:, :, :].rearrange("p t (h v) -> p (t h) v", v=HV), AX.X,
                                        ALU.add).then_inc(s.red, 1)
                dve.wait_ge(s.red, i + 1)
            dve.wait_ge(s.rt, 2)
            ch(nc.vector.reciprocal(ss[:, 2, :, :], ss[:, 1, :, :]))
            for i, (x, y) in enumerate(((qt, qc), (kt, kt))):
                nc.vector.tensor_tensor(y[:, :, :].rearrange("p t (h v) -> p (t h) v", v=HV),
                                        x[:, :, :].rearrange("p t (h v) -> p (t h) v", v=HV),
                                        ss[:, 2, i, :].unsqueeze(2).to_broadcast([P, T * HEADS, HV]), ALU.mult
                                        ).then_inc(s.normed, 1)
            for i in range(10, 20):
                p, t = (i - 10) // 5, 2 * (i % 5)
                dve.wait_ge(s.tr, i + 1)
                for h in range(2):
                    last = nc.vector.tensor_scalar(kz[:, 2 * p + h, t * P:(t + 2) * P], S.ps[:, 4 + i % 4, 0:2 * P],
                                                   S.t("half")[:, h:h + 1], None, ALU.mult)
                last.then_inc(s.tr_out, 1)

        @s.block.scalar
        def _(act):
            for i, sc in enumerate((HV, 1.0)):
                act.wait_ge(s.red, i + 1)
                nc.scalar.activation(ss[:, 1, i, :], ss[:, 0, i, :], ACT.Sqrt,
                                     bias=(S.eps64 if i == 0 else S.eps)[:, 0:1], scale=float(sc)).then_inc(s.rt, 1)
            for i in range(10):
                p, t = i // 5, 2 * (i % 5)
                act.wait_ge(s.tr, i + 1)
                nc.scalar.activation(qT[:, p, t * P:(t + 2) * P], S.ps[:, i % 4, 0:2 * P], ACT.Copy).then_inc(s.sq, 1)

        @s.block.tensor
        def _(pe):
            for i in range(20):
                src = qc if i < 10 else kt
                p, t = (i % 10) // 5, 2 * (i % 5)
                pe.wait_ge(s.normed, 1 if i < 10 else 2)
                b = i % 4 + (0 if i < 10 else 4)
                if 4 <= i < 10:
                    pe.wait_ge(s.sq, i - 3)
                if i >= 14:
                    pe.wait_ge(s.tr_out, i - 13)
                for u in range(2):
                    last = nc.tensor.transpose(S.ps[:, b, u * P:(u + 1) * P], src[:, t + u, p * P:(p + 1) * P],
                                               S.t("ident"))
                last.then_inc(s.tr, 1)

    plan = Plan(nc, mark)
    with Stage(nc, "dn_t", "tp tp_out biased ab e1 e2 ea sp chain sums sg") as s:
        ab = plan.take("dn_abs", [P, T * 8])
        raw = plan.take("dn_raw", [P, T, 16])
        ea = plan.take("dn_decay", [P, 8])
        jobs, dsts = [], []
        for t in range(T):
            jobs.append((t, 1024, 16))
            dsts.append([(raw[:, t, :], 0, 16)])

        @s.block.tensor
        def _(pe):
            token_products(nc, S, s, pe, jobs)
            pe.wait_ge(s.sp, 1)
            gate_sums(nc, S, s, pe, ga, 6).then_inc(s.sums, 1)

        @s.block.scalar
        def _(act):
            token_copies(nc, S, s, act, jobs, dsts)
            act.wait_ge(s.tp_out, len(jobs))
            nc.scalar.activation(be[:, :, :, :].rearrange("p t d h -> p t (d h)"), raw[:, :, 0:8], ACT.Sigmoid
                                 ).then_inc(s.sg, 1)
            act.wait_ge(s.biased, 1)
            nc.scalar.activation(ab[:, :], ga[:, :, :, :].rearrange("p t d h -> p (t d h)"), ACT.Abs).then_inc(s.ab, 1)
            act.wait_ge(s.ab, 1)
            nc.scalar.activation(ab[:, :], ab[:, :], ACT.Exp, scale=-1.0).then_inc(s.e1, 1)
            act.wait_ge(s.e1, 1)
            nc.scalar.activation(ab[:, :], ab[:, :], ACT.Ln, bias=S.one[:, 0:1]).then_inc(s.e2, 1)
            nc.scalar.activation(ea[:, :], S.gates[:, 2, :], ACT.Exp).then_inc(s.ea, 1)
            act.wait_ge(s.sums, 1)
            nc.scalar.activation(eu[:, :, :, :], S.ps[:, 6, 0:240].rearrange("p (w d n) -> p w d n", w=3, d=2), ACT.Exp
                                 ).then_inc(s.ea, 1)

        @s.block.vector
        def _(dve):
            ch = Chain(dve, s.chain)
            dve.wait_ge(s.tp_out, len(jobs))
            gf = ga[:, :, :, :].rearrange("p t d h -> p t (d h)")
            g1 = ga[:, :, :, :].rearrange("p t d h -> p (t d h)")
            nc.vector.tensor_tensor(gf, raw[:, :, 8:16], S.gates[:, 3, :].unsqueeze(1).to_broadcast([P, T, 8]), ALU.add
                                    ).then_inc(s.biased, 1)
            dve.wait_ge(s.e2, 1)
            ch(nc.vector.scalar_tensor_tensor(g1, g1, 0.0, ab[:, :], ALU.max, ALU.add))
            dve.wait_ge(s.ea, 1)
            ch(nc.vector.tensor_scalar(ea[:, :], ea[:, :], -1.0, None, ALU.mult))
            nc.vector.tensor_tensor(gf, gf, ea[:, :].unsqueeze(1).to_broadcast([P, T, 8]), ALU.mult).then_inc(s.sp, 1)
            dve.wait_ge(s.ea, 2)
            ch(nc.vector.tensor_copy(cu[:, :, :, :], S.ps[:, 6, 0:240].rearrange("p (w d n) -> p w d n", w=3, d=2)))
            for d in range(2):
                ch(nc.vector.tensor_tensor(bec[:, d, :].rearrange("p (t h) -> p t h", h=HEADS),
                                           eu[:, 0, d, :].rearrange("p (t h) -> p t h", h=HEADS), be[:, :, d, :],
                                           ALU.mult))

    plan = Plan(nc, mark)
    with Stage(nc, "dn_s", "rows kk qk rel seg z at zt m_nat mt mt_out d_init dt_init p_ps p_sb dp pd d_new dt_new "
                           "rhs rhs_v ke uw uw_out ws v_new q_out av o_out s_new chain pchain r_free") as s:
        NL = 7
        X = [plan.take(f"dn_x{b}", [P, HEADS, P]) for b in range(2)]
        MT = [plan.take(f"dn_mT{b}", [P, HEADS, P]) for b in range(2)]
        AT = [plan.take(f"dn_attnT{b}", [P, HEADS, P]) for b in range(2)]
        Dn = [plan.take(f"dn_inv{b}", [P, HEADS, P]) for b in range(2)]
        DT = [plan.take(f"dn_invT{b}", [P, HEADS, P]) for b in range(2)]
        St = [plan.take(f"dn_state{b}", [P, DG]) for b in range(2)]
        oq = [plan.take(f"dn_oq{b}", [P, DG]) for b in range(2)]
        flat = lambda x: x[:, :, :].rearrange("p h c -> p (h c)")

        def lev(l, d):
            return S.t("levels_" + "fb"[d])[:, l * P:(l + 1) * P]

        def hb(x):
            return x.unsqueeze(1).to_broadcast([P, HEADS, P])

        def tile_of(st, d):
            return ORDER["fb"[d]][st]

        @s.block.tensor
        def _(pe):
            for st in range(T):
                for d in range(2):
                    n, t, b = 2 * st + d, tile_of(st, d), 4 * d
                    ts_ = slice(t * P, (t + 1) * P)
                    if n >= 2:
                        pe.wait_ge(s.uw_out, n - 1)
                        pe.wait_ge(s.v_new, n - 1)
                        pe.wait_ge(s.q_out, n - 1)
                    for h in range(HEADS):
                        last = nc.tensor.matmul(S.ps[:, b, h * P:(h + 1) * P], ga[:, t, d, h:h + 1].to_broadcast([P, P]),
                                                S.t("tri_" + "fb"[d]), start=True, stop=True)
                    last.then_inc(s.rows, 1)
                    for h in range(HEADS):
                        last = nc.tensor.matmul(S.ps[:, b + 1, h * P:(h + 1) * P], kz[:, h, ts_], kz[:, h, ts_],
                                                start=True, stop=True)
                    last.then_inc(s.kk, 1)
                    for h in range(HEADS):
                        last = nc.tensor.matmul(S.ps[:, b + 2, h * P:(h + 1) * P], kz[:, h, ts_], qT[:, h // 2, ts_],
                                                start=True, stop=True)
                    last.then_inc(s.qk, 1)
                for d in range(2):
                    n, b = 2 * st + d, 4 * d
                    pe.wait_ge(s.z, n + 1)
                    if n >= 2:
                        pe.wait_ge(s.s_new, n - 1)
                        pe.wait_ge(s.o_out, n - 1)
                    for h in range(HEADS):
                        last = nc.tensor.transpose(S.ps[:, b + 3, h * P:(h + 1) * P], MT[d][:, h, :], S.t("ident"))
                    last.then_inc(s.zt, 1)
                for d in range(2):
                    n, b = 2 * st + d, 4 * d
                    pe.wait_ge(s.m_nat, n + 1)
                    for h in range(HEADS):
                        last = nc.tensor.transpose(S.ps[:, b + 3, h * P:(h + 1) * P], X[d][:, h, :], S.t("ident"))
                    last.then_inc(s.mt, 1)
                for l in range(1, NL):
                    for d in range(2):
                        n, b = 2 * st + d, 4 * d
                        e = (n // 2 * (NL - 1) + l - 1) * 2 + d
                        if l == 1:
                            pe.wait_ge(s.mt_out, n + 1)
                            pe.wait_ge(s.d_init, n + 1)
                            pe.wait_ge(s.dt_init, n + 1)
                        else:
                            pe.wait_ge(s.d_new, e - 1)
                        for h in range(HEADS):
                            last = nc.tensor.matmul(S.ps[:, b, h * P:(h + 1) * P], MT[d][:, h, :], Dn[d][:, h, :],
                                                    start=True, stop=True)
                        last.then_inc(s.p_ps, 1)
                    for d in range(2):
                        n, b = 2 * st + d, 4 * d
                        e = (n // 2 * (NL - 1) + l - 1) * 2 + d
                        pe.wait_ge(s.p_sb, e + 1)
                        if l > 1:
                            pe.wait_ge(s.dt_new, e - 1)
                        for h in range(HEADS):
                            last = nc.tensor.matmul(S.ps[:, b + 2, h * P:(h + 1) * P], X[d][:, h, :], DT[d][:, h, :],
                                                    start=True, stop=True)
                        last.then_inc(s.pd, 1)
                        if l < NL - 1:
                            for h in range(HEADS):
                                last = nc.tensor.matmul(S.ps[:, b + 1, h * P:(h + 1) * P], DT[d][:, h, :], X[d][:, h, :],
                                                        start=True, stop=True)
                            last.then_inc(s.dp, 1)
                for d in range(2):
                    n, t, b = 2 * st + d, tile_of(st, d), 4 * d
                    pe.wait_ge(s.dt_new, 2 * (NL - 1) * (st + 1) - (1 - d))
                    pe.wait_ge(s.rhs, n + 1)
                    pe.wait_ge(s.rhs_v, n + 1)
                    for h in range(HEADS):
                        nc.tensor.matmul(S.ps[:, b + 1, h * HV:(h + 1) * HV], DT[d][:, h, :], X[d][:, h, 0:HV],
                                         start=True, stop=True)
                    for h in range(HEADS):
                        r0 = (h % 2) * HV
                        last = nc.tensor.matmul(S.ps[r0:r0 + HV, b + 1, DG + (h // 2) * P:DG + (h // 2 + 1) * P],
                                                X[d][:, h, HV:P], DT[d][:, h, :], start=True, stop=True)
                    last.then_inc(s.uw, 1)
                for d in range(2):
                    n, t, b = 2 * st + d, tile_of(st, d), 4 * d
                    ts_ = slice(t * P, (t + 1) * P)
                    pe.wait_ge(s.uw_out, n + 1)
                    if st == 0:
                        pe.wait_ge(s.chain, 2)
                    wT = flat(MT[d])[:, DG:2 * DG]
                    for p in range(2):
                        nc.tensor.matmul(S.ps[:, b + 2, p * P:(p + 1) * P], wT[:, p * P:(p + 1) * P],
                                         St[d][:, p * P:(p + 1) * P], start=True, stop=True)
                    for p in range(2):
                        last = nc.tensor.matmul(S.ps[:, b + 2, DG + p * P:DG + (p + 1) * P], qT[:, p, ts_],
                                                St[d][:, p * P:(p + 1) * P], start=True, stop=True)
                    last.then_inc(s.ws, 1)
                for d in range(2):
                    n, t, b = 2 * st + d, tile_of(st, d), 4 * d
                    pe.wait_ge(s.v_new, n + 1)
                    pe.wait_ge(s.ke, n + 1)
                    vn, ke = flat(Dn[d])[:, 0:DG], flat(Dn[d])[:, DG:2 * DG]
                    for h in range(HEADS):
                        nc.tensor.matmul(S.ps[:, b + 3, h * HV:(h + 1) * HV], AT[d][:, h, :], vn[:, h * HV:(h + 1) * HV],
                                         start=True, stop=True)
                    for p in range(2):
                        last = nc.tensor.matmul(S.ps[:, b + 3, DG + p * P:DG + (p + 1) * P], ke[:, p * P:(p + 1) * P],
                                                vn[:, p * P:(p + 1) * P], start=True, stop=True)
                    last.then_inc(s.av, 1)

        @s.block.scalar
        def _(act):
            for st in range(T):
                for d in range(2):
                    n = 2 * st + d
                    act.wait_ge(s.rel, n + 1)
                    nc.scalar.activation(flat(X[d]), flat(X[d]), ACT.Exp).then_inc(s.seg, 1)
                for d in range(2):
                    n = 2 * st + d
                    act.wait_ge(s.mt, n + 1)
                    nc.scalar.activation(flat(MT[d]), S.ps[:, 4 * d + 3, :], ACT.Copy).then_inc(s.mt_out, 1)
                for d in range(2):
                    n = 2 * st + d
                    act.wait_ge(s.uw, n + 1)
                    nc.scalar.activation(flat(MT[d]), S.ps[:, 4 * d + 1, :], ACT.Copy).then_inc(s.uw_out, 1)

        @s.block.gpsimd
        def _(pool):
            pc = Chain(pool, s.pchain)
            for st in range(T):
                for d in range(2):
                    n, t = 2 * st + d, tile_of(st, d)
                    pool.wait_ge(s.mt_out, n + 1)
                    pc(nc.gpsimd.tensor_tensor(DT[d][:, :, :], MT[d][:, :, :], hb(lev(0, 1 - d)), ALU.mult))
                    nc.gpsimd.tensor_tensor(DT[d][:, :, :], hb(S.t("ident")), DT[d][:, :, :], ALU.subtract
                                            ).then_inc(s.dt_init, 1)
                for d in range(2):
                    n, t = 2 * st + d, tile_of(st, d)
                    cols = slice(t * HEADS, (t + 1) * HEADS)
                    pool.wait_ge(s.pd, 2 * (NL - 1) * (st + 1) - (1 - d))
                    nc.gpsimd.tensor_tensor(X[d][:, :, 0:HV], vt[:, t, :].rearrange("p (h v) -> p h v", v=HV),
                                            be[:, t, d, :].unsqueeze(2).to_broadcast([P, HEADS, HV]), ALU.mult
                                            ).then_inc(s.rhs_v, 1)
                    nc.gpsimd.tensor_tensor(X[d][:, :, HV:P], kt[:, t, :].rearrange("p (h v) -> p h v", v=HV),
                                            bec[:, d, cols].unsqueeze(2).to_broadcast([P, HEADS, HV]), ALU.mult
                                            ).then_inc(s.rhs, 1)
                    nc.gpsimd.tensor_tensor(flat(Dn[d])[:, DG:2 * DG].rearrange("p (h v) -> p h v", v=HV),
                                            kt[:, t, :].rearrange("p (h v) -> p h v", v=HV),
                                            eu[:, 1, d, cols].unsqueeze(2).to_broadcast([P, HEADS, HV]), ALU.mult
                                            ).then_inc(s.ke, 1)

        @s.block.vector
        def _(dve):
            ch = Chain(dve, s.chain)
            for d in range(2):
                ch(nc.vector.memset(St[d][:, :], 0.0))
            for st in range(T):
                for d in range(2):
                    n, t, b = 2 * st + d, tile_of(st, d), 4 * d
                    dve.wait_ge(s.rows, n + 1)
                    if n >= 2:
                        dve.wait_ge(s.uw, n - 1)
                    for h in range(HEADS):
                        c = t * HEADS + h
                        last = nc.vector.scalar_tensor_tensor(X[d][:, h, :], S.ps[:, b, h * P:(h + 1) * P],
                                                              cu[:, 0, d, c:c + 1], S.t("neg_" + "fb"[d]),
                                                              ALU.subtract, ALU.add)
                    last.then_inc(s.rel, 1)
                for d in range(2):
                    n, t, b = 2 * st + d, tile_of(st, d), 4 * d
                    dve.wait_ge(s.seg, n + 1)
                    dve.wait_ge(s.kk, n + 1)
                    dve.wait_ge(s.qk, n + 1)
                    if n >= 2:
                        dve.wait_ge(s.ws, n - 1)
                        dve.wait_ge(s.av, n - 1)
                    nc.vector.tensor_tensor(flat(MT[d]), flat(X[d]), S.ps[:, b + 1, :], ALU.mult).then_inc(s.z, 1)
                    nc.vector.tensor_tensor(flat(AT[d]), flat(X[d]), S.ps[:, b + 2, :], ALU.mult).then_inc(s.at, 1)
                for d in range(2):
                    n, t, b = 2 * st + d, tile_of(st, d), 4 * d
                    dve.wait_ge(s.zt, n + 1)
                    dve.wait_ge(s.at, n + 1)
                    nc.vector.tensor_tensor(X[d][:, :, :], S.ps[:, b + 3, :].rearrange("p (h c) -> p h c", c=P),
                                            be[:, t, d, :].unsqueeze(2).to_broadcast([P, HEADS, P]), ALU.mult
                                            ).then_inc(s.m_nat, 1)
                for d in range(2):
                    n, t, b = 2 * st + d, tile_of(st, d), 4 * d
                    dve.wait_ge(s.m_nat, n + 1)
                    ch(nc.vector.tensor_tensor(Dn[d][:, :, :], X[d][:, :, :], hb(lev(0, d)), ALU.mult))
                    nc.vector.tensor_tensor(Dn[d][:, :, :], hb(S.t("ident")), Dn[d][:, :, :], ALU.subtract
                                            ).then_inc(s.d_init, 1)
                for l in range(1, NL):
                    for d in range(2):
                        n, b = 2 * st + d, 4 * d
                        e = (n // 2 * (NL - 1) + l - 1) * 2 + d
                        dve.wait_ge(s.p_ps, e + 1)
                        if l == 1:
                            dve.wait_ge(s.mt, n + 1)
                        nc.vector.tensor_tensor(X[d][:, :, :], S.ps[:, b, :].rearrange("p (h c) -> p h c", c=P),
                                                hb(lev(l, d)), ALU.mult).then_inc(s.p_sb, 1)
                    for d in range(2):
                        n, b = 2 * st + d, 4 * d
                        e = (n // 2 * (NL - 1) + l - 1) * 2 + d
                        if l < NL - 1:
                            dve.wait_ge(s.dp, (n // 2 * (NL - 2) + l - 1) * 2 + d + 1)
                            if l == 1:
                                dve.wait_ge(s.d_init, n + 1)
                            nc.vector.tensor_tensor(flat(Dn[d]), flat(Dn[d]), S.ps[:, b + 1, :], ALU.subtract
                                                    ).then_inc(s.d_new, 1)
                        else:
                            nc.vector.engine_nop().then_inc(s.d_new, 1)
                        dve.wait_ge(s.pd, e + 1)
                        if l == 1:
                            dve.wait_ge(s.dt_init, n + 1)
                        else:
                            dve.wait_ge(s.dt_new, e - 1)
                            dve.wait_ge(s.d_new, e - 1)
                        nc.vector.tensor_tensor(flat(DT[d]), flat(DT[d]), S.ps[:, b + 2, :], ALU.subtract
                                                ).then_inc(s.dt_new, 1)
                for d in range(2):
                    n, t, b = 2 * st + d, tile_of(st, d), 4 * d
                    cols = slice(t * HEADS, (t + 1) * HEADS)
                    dve.wait_ge(s.ws, n + 1)
                    nc.vector.tensor_tensor(flat(Dn[d])[:, 0:DG], flat(MT[d])[:, 0:DG], S.ps[:, b + 2, 0:DG], ALU.subtract
                                            ).then_inc(s.v_new, 1)
                    nc.vector.tensor_tensor(oq[d][:, :].rearrange("p (h v) -> p h v", v=HV),
                                            S.ps[:, b + 2, DG:2 * DG].rearrange("p (h v) -> p h v", v=HV),
                                            eu[:, 0, d, cols].unsqueeze(2).to_broadcast([P, HEADS, HV]), ALU.mult
                                            ).then_inc(s.q_out, 1)
                for d in range(2):
                    n, t, b = 2 * st + d, tile_of(st, d), 4 * d
                    cols = slice(t * HEADS, (t + 1) * HEADS)
                    sd = St[d][:, :].rearrange("p (h v) -> p h v", v=HV)
                    ch(nc.vector.tensor_tensor(sd, sd, eu[:, 2, d, cols].unsqueeze(2).to_broadcast([P, HEADS, HV]),
                                               ALU.mult))
                    dve.wait_ge(s.av, n + 1)
                    if t >= CT:
                        dve.wait_ge(s.q_out, n + 1)
                        if not st < T - st + 1:
                            dve.wait_ge(s.o_out, 2 * (T + 1 - st) + (1 - d) + 1)
                            ch(nc.vector.tensor_tensor(oq[d][:, :], oq[d][:, :], o[:, t - CT, :], ALU.add))
                        nc.vector.tensor_tensor(o[:, t - CT, :], oq[d][:, :], S.ps[:, b + 3, 0:DG], ALU.add
                                                ).then_inc(s.o_out, 1)
                    else:
                        nc.vector.engine_nop().then_inc(s.o_out, 1)
                    dve.wait_ge(s.q_out, n + 1)
                    dve.wait_ge(s.o_out, n + 1)
                    ch(nc.vector.tensor_tensor(oq[d][:, :], S.ps[:, b + 3, DG:2 * DG], S.t("dn_bd"), ALU.mult))
                    nc.vector.tensor_tensor(St[d][:, :], St[d][:, :], oq[d][:, :], ALU.add).then_inc(s.s_new, 1)

    plan = Plan(nc, mark)
    og = plan.take("dn_og", [P, LT, DG])
    with Stage(nc, "dn_g", "tp tp_out") as s:
        jobs = [(t, 768, DG) for t in range(CT, T)]
        dsts = [[(og[:, t - CT, :], 0, DG)] for t in range(CT, T)]

        @s.block.tensor
        def _(pe):
            token_products(nc, S, s, pe, jobs)

        @s.block.scalar
        def _(act):
            token_copies(nc, S, s, act, jobs, dsts)

    head_norm(nc, S, "dn_n", o, og, S.dn_norm, False, 6, Plan(nc, S.stage_at), False,
              loads=lambda sp: load_weights(sp, S, A, HY0, HY_COLS))


def hyena(nc, S, A):
    plan = Plan(nc, S.stage_at)
    v = plan.take("hy_v", [P, LT, DG])
    x1 = plan.take("hy_x1", [P, LT, DG])
    mark = plan.at
    blocks = []
    for b in range(6):
        cm = S.yT[:, 2 + b % 2, :] if b >= 4 else None
        tok = (v if b < 2 else x1)[:, :, (b % 2) * P:(b % 2 + 1) * P] if b < 4 else None
        blocks.append(dict(col=b * P, tap=b, step=6, bias=18 + b, silu=False, colmajor=False, cm=cm, tok=tok,
                           by_parity=True))
    project_conv(nc, S, A, "hy_c", blocks, plan, ctx=False)

    low = Plan(nc, S.hT_at, S.stage_at)
    hs = low.take("hy_sum", [P, LT, 2, DG])
    hd = low.take("hy_diff", [P, LT, 2, DG])
    plan = Plan(nc, mark)
    HF, EMB = 64, 33
    TWO_PI = 2.0 * math.pi
    MAGIC = 12582912.0
    with Stage(nc, "hy_f", "small lin arg sin taps tapped zeroed sd chain pch") as s:
        feats = plan.take("hy_feats", [EMB, SEQ])
        ws = [plan.take(f"hy_fw{i}", [EMB if i == 0 else HF, HF]) for i in range(3)]
        w4 = plan.take("hy_fw3", [HF, 2 * 2 * DG])
        bs = plan.take("hy_fb", [HF, 3])
        fr = plan.take("hy_ff", [HF, 3])
        win = plan.take("hy_window", [P, LT, DG])
        arg = plan.take("hy_arg", [HF, SEQ])
        rnd = plan.take("hy_round", [HF, SEQ])
        h = plan.take("hy_h", [HF, SEQ])
        tap = [plan.take(f"hy_taps{b}", [P, 2, DG]) for b in range(2)]

        @s.block.sync
        def _(sp):
            n = 0
            for dst, src in ((feats[:, :], A["feats"]), (ws[0][:, :], A["hy_w1"][0]), (ws[1][:, :], A["hy_w2"][0]),
                             (ws[2][:, :], A["hy_w3"][0]), (w4[:, :], A["hy_w4"][0]),
                             (bs[:, 0:1], A["hy_b1"].rearrange("a p -> p a")), (bs[:, 1:2], A["hy_b2"].rearrange("a p -> p a")),
                             (bs[:, 2:3], A["hy_b3"].rearrange("a p -> p a")),
                             (fr[:, 0:1], A["hy_freq"][0, 0:1, :].rearrange("a p -> p a")),
                             (fr[:, 1:2], A["hy_freq"][0, 1:2, :].rearrange("a p -> p a")),
                             (fr[:, 2:3], A["hy_freq"][0, 2:3, :].rearrange("a p -> p a")),
                             (win[:, :, :], A["window"].rearrange("(t p) c -> p t c", p=P))):
                sp.dma_start(dst, src).then_inc(s.small, 16)
                n += 16
            assert n == 12 * 16

        @s.block.tensor
        def _(pe):
            pe.wait_ge(s.small, 12 * 16)
            for i in range(3):
                if i:
                    pe.wait_ge(s.sin, i)
                rhs = feats if i == 0 else h
                for c in range(2):
                    last = nc.tensor.matmul(S.ps[0:HF, c, :], ws[i][:, :], rhs[:, c * 512:(c + 1) * 512],
                                            start=True, stop=True)
                last.then_inc(s.lin, 1)
            pe.wait_ge(s.sin, 3)
            for i in range(2 * LT):
                lt, q = i // 2, i % 2
                if i >= 4:
                    pe.wait_ge(s.tapped, i - 3)
                nc.tensor.matmul(S.ps[:, 2 + i % 4, :], h[:, lt * P:(lt + 1) * P], w4[:, q * 512:(q + 1) * 512],
                                 start=True, stop=True).then_inc(s.taps, 1)

        @s.block.scalar
        def _(act):
            for i in range(3):
                act.wait_ge(s.arg, i + 1)
                nc.scalar.activation(h[:, :], arg[:, :], ACT.Sin).then_inc(s.sin, 1)

        @s.block.vector
        def _(dve):
            ch = Chain(dve, s.chain)
            for i in range(3):
                dve.wait_ge(s.lin, i + 1)
                u = S.ps[0:HF, 0:2, :].rearrange("p a b -> p (a b)")
                ch(nc.vector.tensor_scalar(arg[:, :], u, bs[:, i:i + 1], fr[:, i:i + 1], ALU.add, ALU.mult))
                ch(nc.vector.tensor_scalar(rnd[:, :], arg[:, :], 1.0 / TWO_PI, MAGIC, ALU.mult, ALU.add))
                ch(nc.vector.tensor_scalar(rnd[:, :], rnd[:, :], -MAGIC, None, ALU.add))
                hi = 6.28125
                ch(nc.vector.scalar_tensor_tensor(arg[:, :], rnd[:, :], -hi, arg[:, :], ALU.mult, ALU.add))
                ch(nc.vector.scalar_tensor_tensor(arg[:, :], rnd[:, :], -(TWO_PI - hi), arg[:, :], ALU.mult, ALU.add))
                nc.vector.tensor_scalar(arg[:, :], arg[:, :], 3.1415925, -3.1415925, ALU.min, ALU.max
                                        ).then_inc(s.arg, 1)
            for i in range(2 * LT):
                lt, q = i // 2, i % 2
                dve.wait_ge(s.taps, i + 1)
                if i >= 2:
                    dve.wait_ge(s.sd, i - 1)
                nc.vector.tensor_tensor(tap[i % 2][:, :, :], S.ps[:, 2 + i % 4, :].rearrange("p (d c) -> p d c", d=2),
                                        win[:, lt, :].unsqueeze(1).to_broadcast([P, 2, DG]), ALU.mult
                                        ).then_inc(s.tapped, 1)
                if lt == 0:
                    dve.wait_ge(s.tapped, i + 1)
                    nc.vector.memset(tap[i % 2][0:1, 1, :], 0.0).then_inc(s.zeroed, 1)

        @s.block.gpsimd
        def _(pool):
            for i in range(2 * LT):
                lt, q = i // 2, i % 2
                pool.wait_ge(s.tapped, i + 1)
                if lt == 0:
                    pool.wait_ge(s.zeroed, i + 1)
                nc.gpsimd.tensor_tensor(hs[:, lt, q, :], tap[i % 2][:, 0, :], tap[i % 2][:, 1, :], ALU.add)
                nc.gpsimd.tensor_tensor(hd[:, lt, q, :], tap[i % 2][:, 0, :], tap[i % 2][:, 1, :], ALU.subtract
                                        ).then_inc(s.sd, 1)

    plan = Plan(nc, mark)
    kr = plan.take("hy_k_re", [P, 2, HT, 2, DG])
    kb = plan.take("hy_k_b", [P, 2, HT, 2, DG])
    with Stage(nc, "hy_k", "tab*2 sums even prod d_in chain") as s:
        tw = [plan.take(f"hy_dft{b}", [P, 2, LT, P]) for b in range(2)]
        dv = plan.take("hy_skip", [P, 2 * DG])
        ev = [plan.take(f"hy_even{b}", [P, 2, 2 * DG]) for b in range(2)]

        @s.block.sync
        def _(sp):
            sp.dma_start(dv[:, :], A["hy_d"].rearrange("a o c -> (a o c)").partition_broadcast(P)).then_inc(s.d_in, 16)
            for b in range(HT):
                if b >= 2:
                    sp.wait_ge(s.prod, b - 1)
                for q in range(2):
                    sp.dma_start(tw[b % 2][:, q, :, :],
                                 A["dft_whole"][q, :, b * P:(b + 1) * P].rearrange("(t p) k -> p t k", p=P)
                                 ).then_inc(s.tab[b % 2], 16)

        @s.block.tensor
        def _(pe):
            for b in range(HT):
                pe.wait_ge(s.tab[b % 2], 32 * (b // 2 + 1))
                if b >= 2:
                    pe.wait_ge(s.sums, b - 1)
                for q, x in enumerate((hs, hd)):
                    for par in range(2):
                        for t in range(HT):
                            lt = par * HT + t
                            last = nc.tensor.matmul(S.ps[:, 4 * (b % 2) + 2 * q + par, :], tw[b % 2][:, q, lt, :],
                                                    x[:, lt, :, :].rearrange("p o c -> p (o c)"),
                                                    start=(t == 0), stop=(t == HT - 1))
                last.then_inc(s.prod, 1)

        @s.block.scalar
        def _(act):
            for b in range(HT):
                act.wait_ge(s.prod, b + 1)
                if b >= 2:
                    act.wait_ge(s.sums, b - 1)
                nc.scalar.activation(ev[b % 2][:, 1, :], S.ps[:, 4 * (b % 2) + 2, :], ACT.Copy).then_inc(s.even, 1)

        @s.block.vector
        def _(dve):
            ch = Chain(dve, s.chain)
            dve.wait_ge(s.d_in, 16)
            for b in range(HT):
                dve.wait_ge(s.prod, b + 1)
                bank = 4 * (b % 2)
                flat = lambda t, w: t[:, w, b, :, :].rearrange("p o c -> p (o c)")
                ch(nc.vector.scalar_tensor_tensor(ev[b % 2][:, 0, :], dv[:, :], 1.0 / SEQ, S.ps[:, bank, :],
                                                  ALU.mult, ALU.add))
                nc.vector.tensor_tensor(flat(kr, 0), ev[b % 2][:, 0, :], S.ps[:, bank + 1, :], ALU.add)
                nc.vector.tensor_tensor(flat(kr, 1), ev[b % 2][:, 0, :], S.ps[:, bank + 1, :], ALU.subtract)
                dve.wait_ge(s.even, b + 1)
                nc.vector.tensor_tensor(flat(kb, 0), S.ps[:, bank + 3, :], ev[b % 2][:, 1, :], ALU.add)
                nc.vector.tensor_tensor(flat(kb, 1), S.ps[:, bank + 3, :], ev[b % 2][:, 1, :], ALU.subtract
                                        ).then_inc(s.sums, 1)

    low = Plan(nc, S.hT_at, S.stage_at)
    fwd = low.take("hy_fwd", [P, 2, LT, HALF])
    inv = low.take("hy_inv", [P, 2, HT, SEQ])
    plan = Plan(nc, mark + 2 * 2 * HT * 2 * DG * 4)
    with Stage(nc, "hy_d", "tab fwd even x pq uw y inv z fin pch") as s:
        Y = plan.take("hy_y", [P, 2, HT, 2, DG])
        ev = plan.take("hy_even", [P, 2 * DG])
        X = [plan.take(f"hy_x{b}", [P, 2, 2, DG]) for b in range(2)]
        p1 = plan.take("hy_p1", [P, 2, 2, DG])
        p2 = plan.take("hy_p2", [P, 2, 2, DG])
        UW = plan.take("hy_uw", [P, 2, 2, DG])

        @s.block.sync
        def _(sp):
            for q in range(2):
                sp.dma_start(fwd[:, q, :, :], A["dft_fwd"][q].rearrange("(t p) k -> p t k", p=P)).then_inc(s.tab, 16)
                sp.dma_start(inv[:, q, :, :], A["dft_inv"][q].rearrange("(t p) k -> p t k", p=P)).then_inc(s.tab, 16)

        @s.block.tensor
        def _(pe):
            pe.wait_ge(s.tab, 64)
            for o in range(2):
                if o == 1:
                    pe.wait_ge(s.z, LT)
                for b in range(HT):
                    i = o * HT + b
                    if i >= 2:
                        pe.wait_ge(s.x, i - 1)
                    for par in range(2):
                        for q in range(2):
                            for t in range(HT):
                                nt = par * HT + t
                                last = nc.tensor.matmul(S.ps[:, 2 * (i % 2) + par, q * DG:(q + 1) * DG],
                                                        fwd[:, q, nt, b * P:(b + 1) * P], v[:, nt, :],
                                                        start=(t == 0), stop=(t == HT - 1))
                    last.then_inc(s.fwd, 1)
                if o == 0:
                    for nt in range(LT):
                        if nt >= 2:
                            pe.wait_ge(s.z, nt - 1)
                        for b in range(HT):
                            if nt == 0:
                                pe.wait_ge(s.y, b + 1)
                            for q in range(2):
                                last = nc.tensor.matmul(S.ps[:, 4 + nt % 2, 0:DG], inv[:, q, b, nt * P:(nt + 1) * P],
                                                        Y[:, nt // HT, b, q, :], start=(q == 0 and b == 0),
                                                        stop=(q == 1 and b == HT - 1))
                        last.then_inc(s.inv, 1)
                else:
                    for i in range(4):
                        par, c = i // 2, i % 2
                        for b in range(HT):
                            if i == 0:
                                pe.wait_ge(s.y, HT + b + 1)
                            for q in range(2):
                                last = nc.tensor.matmul(S.ps[:, 4 + i, :], Y[:, par, b, q, c * P:(c + 1) * P],
                                                        inv[:, q, b, par * HALF:(par + 1) * HALF],
                                                        start=(q == 0 and b == 0), stop=(q == 1 and b == HT - 1))
                        last.then_inc(s.inv, 1)

        @s.block.scalar
        def _(act):
            for i in range(2 * HT):
                act.wait_ge(s.fwd, i + 1)
                if i:
                    act.wait_ge(s.x, i)
                nc.scalar.activation(ev[:, :], S.ps[:, 2 * (i % 2), :], ACT.Copy).then_inc(s.even, 1)

        @s.block.vector
        def _(dve):
            for o in range(2):
                for b in range(HT):
                    i = o * HT + b
                    x = X[i % 2]
                    dve.wait_ge(s.even, i + 1)
                    flat = lambda w: x[:, w, :, :].rearrange("p q c -> p (q c)")
                    nc.vector.tensor_tensor(flat(0), ev[:, :], S.ps[:, 2 * (i % 2) + 1, :], ALU.add)
                    nc.vector.tensor_tensor(flat(1), ev[:, :], S.ps[:, 2 * (i % 2) + 1, :], ALU.subtract).then_inc(s.x, 1)
                    dve.wait_ge(s.x, i + 1)
                    if i:
                        dve.wait_ge(s.uw, i)
                    for p, k in ((p1, kr), (p2, kb)):
                        for w in range(2):
                            last = nc.vector.tensor_tensor(p[:, w, :, :], x[:, w, :, :],
                                                           k[:, w, b, o, :].unsqueeze(1).to_broadcast([P, 2, DG]), ALU.mult)
                    last.then_inc(s.pq, 1)
                if o == 0:
                    for nt in range(LT):
                        dve.wait_ge(s.inv, nt + 1)
                        nc.vector.tensor_tensor(v[:, nt, :], x1[:, nt, :], S.ps[:, 4 + nt % 2, 0:DG], ALU.mult
                                                ).then_inc(s.z, 1)
                else:
                    for i in range(4):
                        par, c = i // 2, i % 2
                        dve.wait_ge(s.inv, LT + i + 1)
                        y = S.yT[:, 2 + c, par:SEQ:2]
                        nc.vector.tensor_tensor(y, y, S.ps[:, 4 + i, :], ALU.mult).then_inc(s.fin, 1)

        @s.block.gpsimd
        def _(pool):
            for i in range(2 * HT):
                o, b = i // HT, i % HT
                pool.wait_ge(s.pq, i + 1)
                if i:
                    pool.wait_ge(s.y, i)
                nc.gpsimd.tensor_tensor(UW[:, 0, 0, :], p1[:, 0, 0, :], p2[:, 0, 1, :], ALU.subtract)
                nc.gpsimd.tensor_tensor(UW[:, 0, 1, :], p1[:, 0, 1, :], p2[:, 0, 0, :], ALU.add)
                nc.gpsimd.tensor_tensor(UW[:, 1, 0, :], p1[:, 1, 0, :], p2[:, 1, 1, :], ALU.add)
                nc.gpsimd.tensor_tensor(UW[:, 1, 1, :], p1[:, 1, 1, :], p2[:, 1, 0, :], ALU.subtract).then_inc(s.uw, 1)
                pool.wait_ge(s.uw, i + 1)
                if o == 1 and b == 0:
                    pool.wait_ge(s.inv, LT)
                nc.gpsimd.tensor_tensor(Y[:, 0, b, :, :], UW[:, 0, :, :], UW[:, 1, :, :], ALU.add)
                nc.gpsimd.tensor_tensor(Y[:, 1, b, :, :], UW[:, 0, :, :], UW[:, 1, :, :], ALU.subtract).then_inc(s.y, 1)


def project_out(nc, S, A):
    low = Plan(nc, S.hT_at)
    wo = low.take("w_out", [P, KD, D])
    rows = low.take("row_broadcasts", [P, 4, D])
    rt = low.take("router", [P, KD, NE])
    xt = [low.take(f"res_x{b}", [P, D]) for b in range(2)]
    tm = [low.take(f"res_tmp{b}", [P, D]) for b in range(2)]
    h2 = [low.take(f"h2_{b}", [P, D]) for b in range(2)]
    hT = low.take("h2T", [P, KD, P])
    st = low.take("out_stats", [P, LT, 8])
    sm = [low.take(f"aff{b}", [P, NE]) for b in range(2)]
    x1, affT = S.x1, S.affT
    with Stage(nc, "out", "w_in rows_in r_in x_in*2 y ss rt y_sc x1d ss2 rt2 h2m h2d h2s*2 tr ht_a ht_v lg mx ex af at at_o "
                          "chain zero zst pch r1 r2") as s:

        @s.block.sync
        def _(sp):
            for h in range(2):
                sp.dma_start(wo[:, 4 * h:4 * h + 4, :],
                             A["w_out"][0, 512 * h:512 * h + 512, :].rearrange("(k p) n -> p k n", p=P)).then_inc(s.w_in, 16)
            sp.dma_start(rt[:, :, :], A["moe_router"][0].rearrange("(k p) n -> p k n", p=P)).then_inc(s.r_in, 16)
            for j in range(4):
                sp.dma_start(rows[:, j, :], A["rows"][j, :].partition_broadcast(P)).then_inc(s.rows_in, 16)
            sp.wait_ge(s.zero, 1)
            for t in range(LT):
                sp.dma_start(A["moe_sum"][t * P:(t + 1) * P, :], S.zrow[:, :]).then_inc(s.zst, 16)
            for t in range(LT + 1):
                if t < LT:
                    if t >= 2:
                        sp.wait_ge(s.x1d, t - 1)
                    sp.dma_start(xt[t % 2][:, :], A["x"][0, t * P:(t + 1) * P, :]).then_inc(s.x_in[t % 2], 16)
                if t >= 1:
                    u = t - 1
                    sp.wait_ge(s.h2d, u + 1)
                    sp.dma_start(A["h2"][u * P:(u + 1) * P, :], h2[u % 2][:, :]).then_inc(s.h2s[u % 2], 16)
            for b in range(2):
                sp.wait_ge(s.h2s[b], 16 * LT // 2)
            sp.wait_ge(s.zst, 16 * LT)

        @s.block.gpsimd
        def _(pool):
            for t in range(LT):
                pool.wait_ge(s.y_sc, t + 1)
                pool.wait_ge(s.x_in[t % 2], 16 * (t // 2 + 1))
                nc.gpsimd.tensor_tensor(x1[:, t, :], tm[t % 2][:, :], xt[t % 2][:, :], ALU.add).then_inc(s.x1d, 1)
                pool.wait_ge(s.rows_in, 64)
                pool.wait_ge(s.h2m, t + 1)
                nc.gpsimd.tensor_tensor(h2[t % 2][:, :], h2[t % 2][:, :], rows[:, 2, :], ALU.add).then_inc(s.h2d, 1)

        def turn_rows(pe, t):
            pe.wait_ge(s.h2d, t + 1)
            if t >= 1:
                pe.wait_ge(s.ht_a, t)
                pe.wait_ge(s.ht_v, t)
            for k in range(KD):
                last = nc.tensor.transpose(S.ps[:, 4 + k // 4, (k % 4) * P:(k % 4 + 1) * P],
                                           h2[t % 2][:, k * P:(k + 1) * P], S.t("ident"))
            last.then_inc(s.tr, 1)

        def router(pe, t):
            pe.wait_ge(s.ht_a, t + 1)
            pe.wait_ge(s.ht_v, t + 1)
            if t >= 1:
                pe.wait_ge(s.ex, t)
            for k in range(KD):
                last = nc.tensor.matmul(S.ps[:, 6, 0:NE], hT[:, k, :], rt[:, k, :], start=(k == 0), stop=(k == KD - 1))
            last.then_inc(s.lg, 1)

        def turned(pe, t):
            pe.wait_ge(s.af, t + 1)
            if t >= 1:
                pe.wait_ge(s.at_o, t)
            nc.tensor.transpose(S.ps[0:NE, 7, 0:P], sm[t % 2][:, :], S.t("ident")).then_inc(s.at, 1)

        @s.block.tensor
        def _(pe):
            pe.wait_ge(s.w_in, 32)
            pe.wait_ge(s.r_in, 16)
            for t in range(LT + 3):
                if t < LT and t >= 2:
                    pe.wait_ge(s.y_sc, t - 1)
                for h in range(2):
                    if h == 1 and 2 <= t <= LT + 1:
                        router(pe, t - 2)
                    if t < LT:
                        for k in range(KD):
                            last = nc.tensor.matmul(S.ps[:, 2 * (t % 2) + h, :], S.yT[:, k, t * P:(t + 1) * P],
                                                    wo[:, k, h * 512:(h + 1) * 512], start=(k == 0), stop=(k == KD - 1))
                if t < LT:
                    last.then_inc(s.y, 1)
                if 1 <= t <= LT:
                    turn_rows(pe, t - 1)
                if t >= 3:
                    turned(pe, t - 3)

        @s.block.scalar
        def _(act):
            for t in range(LT + 2):
                if t >= 2:
                    u = t - 2
                    act.wait_ge(s.mx, u + 1)
                    nc.scalar.activation(sm[u % 2][:, :], S.ps[:, 6, 0:NE], ACT.Exp, bias=st[:, u, 6:7],
                                         accum_out=st[:, u, 7:8]).then_inc(s.ex, 1)
                if 1 <= t <= LT:
                    act.wait_ge(s.tr, t)
                    nc.scalar.activation(hT[:, 0:4, :], S.ps[:, 4, :].rearrange("p (k c) -> p k c", c=P), ACT.Copy
                                         ).then_inc(s.ht_a, 1)
                if t < LT:
                    act.wait_ge(s.y, t + 1)
                    if t >= 1:
                        act.wait_ge(s.ss2, t)
                    y = S.ps[:, 2 * (t % 2):2 * (t % 2) + 2, :].rearrange("p a b -> p (a b)")
                    nc.scalar.activation(S.junk[:, :], y, ACT.Square, accum_out=st[:, t, 0:1]).then_inc(s.ss, 1)
                    act.wait_ge(s.ss, t + 1)
                    nc.scalar.activation(st[:, t, 1:2], st[:, t, 0:1], ACT.Sqrt, bias=S.eps[:, 0:1], scale=1.0 / D
                                         ).then_inc(s.rt, 1)
                    act.wait_ge(s.x1d, t + 1)
                    nc.scalar.activation(S.junk[:, :], x1[:, t, :], ACT.Square, accum_out=st[:, t, 3:4]).then_inc(s.ss2, 1)
                    act.wait_ge(s.ss2, t + 1)
                    nc.scalar.activation(st[:, t, 4:5], st[:, t, 3:4], ACT.Sqrt, bias=S.eps[:, 0:1], scale=1.0 / D
                                         ).then_inc(s.rt2, 1)

        @s.block.vector
        def _(dve):
            ch = Chain(dve, s.chain)
            nc.vector.memset(S.zrow[:, :], 0.0).then_inc(s.zero, 1)
            dve.wait_ge(s.rows_in, 64)
            for t in range(LT + 3):
                if 2 <= t <= LT + 1:
                    u = t - 2
                    dve.wait_ge(s.lg, u + 1)
                    nc.vector.tensor_reduce(st[:, u, 6:7], S.ps[:, 6, 0:NE], AX.X, ALU.max, negate=True).then_inc(s.mx, 1)
                    dve.wait_ge(s.ex, u + 1)
                    ch(nc.vector.reciprocal(st[:, u, 5:6], st[:, u, 7:8]))
                    nc.vector.tensor_scalar(sm[u % 2][:, :], sm[u % 2][:, :], st[:, u, 5:6], None, ALU.mult
                                            ).then_inc(s.af, 1)
                if 1 <= t <= LT:
                    dve.wait_ge(s.tr, t)
                    nc.vector.tensor_copy(hT[:, 4:8, :], S.ps[:, 5, :].rearrange("p (k c) -> p k c", c=P)
                                          ).then_inc(s.ht_v, 1)
                if t < LT:
                    dve.wait_ge(s.rt, t + 1)
                    ch(nc.vector.reciprocal(st[:, t, 2:3], st[:, t, 1:2]))
                    if t >= 2:
                        dve.wait_ge(s.x1d, t - 1)
                    y = S.ps[:, 2 * (t % 2):2 * (t % 2) + 2, :].rearrange("p a b -> p (a b)")
                    nc.vector.scalar_tensor_tensor(tm[t % 2][:, :], y, st[:, t, 2:3], rows[:, 0, :], ALU.mult, ALU.mult
                                                   ).then_inc(s.y_sc, 1)
                    dve.wait_ge(s.rt2, t + 1)
                    ch(nc.vector.reciprocal(st[:, t, 2:3], st[:, t, 4:5]))
                    if t >= 2:
                        dve.wait_ge(s.h2s[t % 2], 16 * (t // 2))
                        dve.wait_ge(s.tr, t - 1)
                    nc.vector.scalar_tensor_tensor(h2[t % 2][:, :], x1[:, t, :], st[:, t, 2:3], rows[:, 1, :],
                                                   ALU.mult, ALU.mult).then_inc(s.h2m, 1)
                if t >= 3:
                    u = t - 3
                    dve.wait_ge(s.at, u + 1)
                    nc.vector.tensor_copy(affT[:, u * P:(u + 1) * P], S.ps[0:NE, 7, 0:P]).then_inc(s.at_o, 1)


def experts(nc, S, A):
    plan = Plan(nc, S.moe_at)
    unit = [plan.take(f"w_unit{u}", [P, 4096]) for u in range(6)]
    xs = plan.take("xs", [P, D])
    xsT = plan.take("xsT", [P, KD, P])
    sg = [plan.take(f"gate_silu{j}", [P, 512]) for j in range(2)]
    a = [plan.take(f"hidden{j}", [P, 512]) for j in range(2)]
    aT = plan.take("hiddenT", [P, KD, P])
    y = plan.take("y", [P, D])
    work = plan.take("aff_work", [NE, SEQ])
    val = plan.take("top_val", [NE, CAP])
    idx = plan.take("top_idx", [NE, CAP], U32)
    idf = plan.take("top_idx_f", [NE, CAP])
    with Stage(nc, "moe", "chain picked turned cols u0 u1 u2 u3 u4 u5 f0 f1 f2 f3 f4 f5 xtr xt_a xt_v sg0 sg1 a0 a1 "
                          "atr0 atr1 at0 at1 ya yv") as s:
        ready = [s.u0, s.u1, s.u2, s.u3, s.u4, s.u5]
        freed = [s.f0, s.f1, s.f2, s.f3, s.f4, s.f5]
        sgs, as_, atr, ats = [s.sg0, s.sg1], [s.a0, s.a1], [s.atr0, s.atr1], [s.at0, s.at1]
        wg = A["moe_w_gate"].rearrange("a e (k p) n -> (a e) p k n", p=P)
        wu = A["moe_w_up"].rearrange("a e (k p) n -> (a e) p k n", p=P)
        wd = A["moe_w_down"].rearrange("a e (k p) n -> (a e) p k n", p=P)

        @s.block.sync
        def _(sp):
            with sp.Fori(0, NE) as e:
                for u in range(6):
                    sp.wait_ge(freed[u], e)
                    if u < 4:
                        src = (wg, wu)[u % 2][e, :, :, (u // 2) * 512:(u // 2 + 1) * 512]
                        dst = unit[u][:, :].rearrange("p (k n) -> p k n", k=KD)
                    else:
                        src = wd[e, :, (u - 4) * 4:(u - 3) * 4, :]
                        dst = unit[u][:, :].rearrange("p (k n) -> p k n", k=4)
                    sp.dma_start(dst, src).then_inc(ready[u], 16)

        def gather(pool, e):
            pool.indirect_dma_start(xs[:, :], None, A["h2"], bass.IndirectOffsetOnAxis(ap=S.icol[:, e:e + 1], axis=0)
                                    ).then_inc(S.xs_in, 16)

        @s.block.gpsimd
        def _(pool):
            pool.wait_ge(s.cols, 1)
            gather(pool, 0)
            for e in range(NE):
                if e < NE - 1:
                    pool.wait_ge(s.xtr, e + 1)
                    gather(pool, e + 1)
                if e:
                    pool.wait_ge(S.y_added, e * 16)
                pool.wait_ge(s.ya, e + 1)
                pool.wait_ge(s.yv, e + 1)
                pool.indirect_dma_start(A["moe_sum"], bass.IndirectOffsetOnAxis(ap=S.icol[:, e:e + 1], axis=0), y[:, :],
                                        None, compute_op=ALU.add).then_inc(S.y_added, 16)
            pool.wait_ge(S.y_added, NE * 16)

        def rows_turned(pe, e):
            pe.wait_ge(S.xs_in, e * 16 + 16)
            for k in range(KD):
                last = nc.tensor.transpose(S.ps[:, 2 + k // 4, (k % 4) * P:(k % 4 + 1) * P], xs[:, k * P:(k + 1) * P],
                                           S.t("ident"))
            last.then_inc(s.xtr, 1)

        def products(pe, e, more):
            pe.wait_ge(s.xt_a, e + 1)
            pe.wait_ge(s.xt_v, e + 1)
            for j in range(2):
                if j:
                    pe.wait_ge(as_[j], e)
                for g in range(2):
                    u = 2 * j + g
                    pe.wait_ge(ready[u], e * 16 + 16)
                    for k in range(KD):
                        last = nc.tensor.matmul(S.ps[:, 2 + u, :], xsT[:, k, :], unit[u][:, k * 512:(k + 1) * 512],
                                                start=(k == 0), stop=(k == KD - 1))
                    last.then_inc(freed[u], 1)
            for j in range(2):
                pe.wait_ge(as_[j], e + 1)
                pe.wait_ge(ats[j], e)
                for k in range(4):
                    last = nc.tensor.transpose(S.ps[:, j, k * P:(k + 1) * P], a[j][:, k * P:(k + 1) * P], S.t("ident"))
                last.then_inc(atr[j], 1)
                if j == 0 and more:
                    rows_turned(pe, e + 1)
            pe.wait_ge(s.ya, e)
            pe.wait_ge(s.yv, e)
            for u in range(2):
                pe.wait_ge(ready[4 + u], e * 16 + 16)
                pe.wait_ge(ats[u], e + 1)
                for k in range(4):
                    for h in range(2):
                        last = nc.tensor.matmul(S.ps[:, 6 + h, :], aT[:, 4 * u + k, :],
                                                unit[4 + u][:, k * D + h * 512:k * D + (h + 1) * 512],
                                                start=(u == 0 and k == 0), stop=(u == 1 and k == 3))
                last.then_inc(freed[4 + u], 1)

        @s.block.tensor
        def _(pe):
            pe.wait_ge(s.picked, 1)
            nc.tensor.transpose(S.ps[:, 0, 0:NE], val[:, :], S.t("ident")[0:NE, 0:NE])
            nc.tensor.transpose(S.ps[:, 1, 0:NE], idf[:, :], S.t("ident")[0:NE, 0:NE]).then_inc(s.turned, 1)
            pe.wait_ge(s.cols, 1)
            rows_turned(pe, 0)
            with pe.Fori(0, NE - 1) as e:
                products(pe, e, True)
            products(pe, NE - 1, False)

        def rows_a(act, e):
            act.wait_ge(s.xtr, e + 1)
            nc.scalar.activation(xsT[:, 0:4, :], S.ps[:, 2, :].rearrange("p (k c) -> p k c", c=P), ACT.Copy
                                 ).then_inc(s.xt_a, 1)

        def hidden_a(act, e, more):
            for j in range(2):
                act.wait_ge(freed[2 * j + 1], e + 1)
                act.wait_ge(as_[j], e)
                nc.scalar.activation(sg[j][:, :], S.ps[:, 2 + 2 * j, :], ACT.Silu).then_inc(sgs[j], 1)
            act.wait_ge(s.atr0, e + 1)
            act.wait_ge(s.f5, e)
            nc.scalar.activation(aT[:, 0:4, :], S.ps[:, 0, :].rearrange("p (k c) -> p k c", c=P), ACT.Copy
                                 ).then_inc(s.at0, 1)
            if more:
                rows_a(act, e + 1)
            act.wait_ge(s.f5, e + 1)
            act.wait_ge(S.y_added, e * 16)
            nc.scalar.activation(y[:, 0:512], S.ps[:, 6, :], ACT.Copy, scale=S.wcol[:, bass.ds(e, 1)]
                                 ).then_inc(s.ya, 1)

        @s.block.scalar
        def _(act):
            act.wait_ge(s.cols, 1)
            rows_a(act, 0)
            with act.Fori(0, NE - 1) as e:
                hidden_a(act, e, True)
            hidden_a(act, NE - 1, False)

        def rows_v(dve, e):
            dve.wait_ge(s.xtr, e + 1)
            nc.vector.tensor_copy(xsT[:, 4:8, :], S.ps[:, 3, :].rearrange("p (k c) -> p k c", c=P)).then_inc(s.xt_v, 1)

        def hidden_v(dve, e, more):
            for j in range(2):
                dve.wait_ge(sgs[j], e + 1)
                dve.wait_ge(atr[j], e)
                nc.vector.tensor_tensor(a[j][:, :], sg[j][:, :], S.ps[:, 3 + 2 * j, :], ALU.mult).then_inc(as_[j], 1)
            if more:
                rows_v(dve, e + 1)
            dve.wait_ge(s.atr1, e + 1)
            dve.wait_ge(s.f5, e)
            nc.vector.tensor_copy(aT[:, 4:8, :], S.ps[:, 1, :].rearrange("p (k c) -> p k c", c=P)).then_inc(s.at1, 1)
            dve.wait_ge(s.f5, e + 1)
            dve.wait_ge(S.y_added, e * 16)
            nc.vector.tensor_scalar(y[:, 512:1024], S.ps[:, 7, :], S.wcol[:, bass.ds(e, 1)], None, ALU.mult
                                    ).then_inc(s.yv, 1)

        @s.block.vector
        def _(dve):
            ch = Chain(dve, s.chain)
            R = CAP // 8
            for r in range(R):
                src = S.affT if r == 0 else work
                c = slice(8 * r, 8 * r + 8)
                ch(nc.vector.max(val[:, c], src[:, :]))
                ch(nc.vector.max_index(idx[:, c], val[:, c], src[:, :]))
                if r < R - 1:
                    ch(nc.vector.match_replace(work[:, :], val[:, c], src[:, :], -1.0))
            nc.vector.tensor_copy(idf[:, :], idx[:, :]).then_inc(s.picked, 1)
            dve.wait_ge(s.turned, 1)
            ch(nc.vector.tensor_copy(S.wcol[:, :], S.ps[:, 0, 0:NE]))
            nc.vector.tensor_copy(S.icol[:, :], S.ps[:, 1, 0:NE]).then_inc(s.cols, 1)
            rows_v(dve, 0)
            with dve.Fori(0, NE - 1) as e:
                hidden_v(dve, e, True)
            hidden_v(dve, NE - 1, False)


def finish(nc, S, A):
    plan = Plan(nc, S.moe_at)
    m = [plan.take(f"moe_rows{b}", [P, D]) for b in range(3)]
    g = plan.take("gate_row", [P, D])
    sq = plan.take("moe_sq", [P, D])
    r = [plan.take(f"moe_out{b}", [P, D]) for b in range(2)]
    st = plan.take("moe_stats", [P, LT, 3])
    with Stage(nc, "fin", "g_in m_in*3 ss rt chain sc out st*2") as s:
        @s.block.sync
        def _(sp):
            sp.dma_start(g[:, :], A["rows"][3, :].partition_broadcast(P)).then_inc(s.g_in, 16)
            for t in range(LT):
                if t >= 3:
                    sp.wait_ge(s.sc, t - 2)
                sp.dma_start(m[t % 3][:, :], A["moe_sum"][t * P:(t + 1) * P, :]).then_inc(s.m_in[t % 3], 16)

        @s.block.scalar
        def _(act):
            for t in range(LT):
                act.wait_ge(s.m_in[t % 3], 16 * (t // 3 + 1))
                if t:
                    act.wait_ge(s.ss, t)
                nc.scalar.activation(sq[:, :], m[t % 3][:, :], ACT.Square, accum_out=st[:, t, 0:1]).then_inc(s.ss, 1)
                act.wait_ge(s.ss, t + 1)
                nc.scalar.activation(st[:, t, 1:2], st[:, t, 0:1], ACT.Sqrt, bias=S.eps[:, 0:1], scale=1.0 / D
                                     ).then_inc(s.rt, 1)
                act.wait_ge(s.out, t + 1)
                act.dma_start(A["out"][0, t * P:(t + 1) * P, :], r[t % 2][:, :]).then_inc(s.st[t % 2], 16)
            for b in range(2):
                act.wait_ge(s.st[b], 16 * LT // 2)

        @s.block.vector
        def _(dve):
            ch = Chain(dve, s.chain)
            dve.wait_ge(s.g_in, 16)
            for t in range(LT):
                dve.wait_ge(s.rt, t + 1)
                ch(nc.vector.reciprocal(st[:, t, 2:3], st[:, t, 1:2]))
                if t >= 2:
                    dve.wait_ge(s.st[t % 2], 16 * (t // 2))
                nc.vector.scalar_tensor_tensor(r[t % 2][:, :], m[t % 3][:, :], st[:, t, 2:3], g[:, :], ALU.mult, ALU.mult
                                               ).then_inc(s.sc, 1)
                dve.wait_ge(s.sc, t + 1)
                nc.vector.tensor_tensor(r[t % 2][:, :], r[t % 2][:, :], S.x1[:, t, :], ALU.add).then_inc(s.out, 1)


STAGES = (load_and_modulate, normalise, gla, mamba, deltanet, hyena, project_out, experts, finish)


def program(nc, A, stages=STAGES):
    S = Store()
    SPENT.clear()
    (tab, S.off), (gla_tab, S.goff) = tables()
    S.gn = gla_tab.shape[1]
    plan = Plan(nc, SBUF0)
    S.tab = plan.take("tables", [P, tab.shape[1]])
    S.pcols = plan.take("param_cols", [P, 69])
    S.gla_norm = plan.take("gla_norm", [P, DG])
    S.mb_norm = plan.take("mb_norm", [P, DG])
    S.dn_norm = plan.take("dn_norm", [P, DG])
    S.gates = plan.take("gate_params", [P, 4, 8])
    S.mb_d = plan.take("mb_d", [P, HEADS])
    S.mod1 = plan.take("mod1", [P, 2, 2, KD])
    S.eps = plan.take("eps", [P, 1])
    S.eps64 = plan.take("eps64", [P, 1])
    S.one = plan.take("one", [P, 1])
    S.zero = plan.take("zero", [P, 1])
    S.ones = plan.take("ones", [P, P])
    S.yT = plan.take("yT", [P, KD, SEQ])
    S.hT_at = plan.at
    S.hT = plan.take("hT", [P, KD, TOK])
    S.w = plan.take("w_mixer", [P, KD, WCOLS])
    S.stage_at = plan.at
    top = Plan(nc, SBUF_END - LT * D * 4 - 4096 - 256)
    S.x1 = top.take("x1", [P, LT, D])
    S.affT = top.take("affT", [NE, SEQ])
    S.wcol = top.take("w_col", [P, NE])
    S.icol = top.take("idx_col", [P, NE], U32)
    S.moe_at = S.hT_at - KD * SEQ * 4
    S.zrow = nc.alloc_sbuf_tensor_at("zero_row", [P, D], F32, offset=SBUF_END - LT * D * 4 - 4096 - 256 - 4096)
    S.junk = nc.alloc_sbuf_tensor_at("squares", [P, D], F32, offset=SBUF_END - LT * D * 4 - 4096 - 256 - 8192)
    S.w_count = 0

    def t(name):
        o, n = S.off[name]
        return S.tab[:, o:o + n]

    S.t = t
    with nc.psum_tensor("ps", [P, 8, BANK], F32) as ps, nc.semaphore("w_ready") as w_ready, \
            nc.semaphore("xs_in") as xs_in, nc.semaphore("y_added") as y_added:
        S.ps, S.w_ready, S.xs_in, S.y_added = ps, w_ready, xs_in, y_added
        with Stage(nc, "init", "done") as s:
            @s.block.vector
            def _(dve):
                nc.vector.memset(S.eps[:, :], EPS)
                nc.vector.memset(S.eps64[:, :], EPS * HV)
                nc.vector.memset(S.one[:, :], 1.0)
                nc.vector.memset(S.zero[:, :], 0.0)
                nc.vector.memset(S.ones[:, :], 1.0)
        for stage in stages:
            stage(nc, S, A)
        with Stage(nc, "end", "") as s:
            @s.block.sync
            def _(sp):
                sp.wait_ge(S.w_ready, S.w_count)
        nc.clear_and_free_semaphores(list(SPENT))
        SPENT.clear()
    return S


_INS = ["x", "c", "ctx", "c_ctx", "w_mod", "b_mod", "norm_g", "w_in", "w_out", "gla_w2", "gla_b", "gla_norm",
        "hy_conv_w", "hy_conv_b", "hy_w1", "hy_b1", "hy_w2", "hy_b2", "hy_w3", "hy_b3", "hy_w4", "hy_freq", "hy_d",
        "mb_conv_w", "mb_conv_b", "mb_a_log", "mb_dt_bias", "mb_d", "mb_norm", "dn_conv_w", "dn_a_log", "dn_dt_bias",
        "dn_norm", "moe_router", "moe_w_gate", "moe_w_up", "moe_w_down"]


def declare(nc, arrays):
    A = {n: nc.dram_tensor("in_" + n, a.shape, F32, kind="ExternalInput").ap() for n, a in arrays.items()}
    A["rows"] = nc.dram_tensor("rows", (4, D), F32, kind="Internal").ap()
    A["h2"] = nc.dram_tensor("h2", (SEQ, D), F32, kind="Internal").ap()
    A["moe_sum"] = nc.dram_tensor("moe_sum", (SEQ, D), F32, kind="Internal").ap()
    A["out"] = nc.dram_tensor("out_0_dram", (1, SEQ, D), F32, kind="ExternalOutput").ap()
    return A


def kernel(**inputs):
    import numpy as _np
    import concourse.bacc as _bacc
    from concourse.bass_utils import run_bass_kernel_spmd as _run

    nc = _bacc.Bacc("TRN2", target_bir_lowering=False, num_devices=1)
    arrays = {n: _np.ascontiguousarray(inputs[n]) for n in _INS}
    arrays.update(shape_tables())
    program(nc, declare(nc, arrays))
    r = _run(nc, [{"in_" + n: a for n, a in arrays.items()}], core_ids=[0])
    return r.results[0]["out_0_dram"]
```

```python
import math
from collections import namedtuple
from contextlib import contextmanager

import numpy as np

import concourse.bass as bass
from concourse import mybir

F32 = mybir.dt.float32
F32R = mybir.dt.float32r
U32 = mybir.dt.uint32
ACT = mybir.ActivationFunctionType
ALU = mybir.AluOpType
AX = mybir.AxisListType

P = 128
D = 1024
KD = D // P
SEQ, CTX = 1024, 256
TOK = SEQ + CTX
CT, LT = CTX // P, SEQ // P
T = CT + LT
GRID_W = 64
GRID_H = SEQ // GRID_W
N_MOD = 6
EPS = 1e-6
DG = 256
HEADS = 4
HV = DG // HEADS
GLA_DK = 32
GLA_RANK = 16
GLA_TAU = 16.0
GLA_COLS, HY_COLS, MB_COLS, DN_COLS = 800, 768, 1032, 1040
HY0, MB0, DN0 = 800, 1568, 2600
WCOLS = 1040
NE = 16
CAP = 2 * SEQ // NE
FF = 1024
BIG = 1.0e30
BANK = 512
CHUNKS = ((0, 256), (256, 512), (768, 512))
PADS = (0, 257, 258, 1283)
CTX_AT, LAT_AT = 1, 259

SBUF0, SBUF_END = 16512, 229344


def tables():
    i = np.arange(P)
    j, c = i[:, None], i[None, :]
    f = np.float32
    low = (j <= c).astype(f)
    up = (j >= c).astype(f)
    mid = P // 2
    tabs = {}
    tabs["ident"] = np.eye(P, dtype=f)
    for name, m, strict_after in (("f", low, (j > c).astype(f)), ("b", up, (j < c).astype(f))):
        tabs["tri_" + name] = m
        tabs["after_" + name] = strict_after
        tabs["neg_" + name] = ((1.0 - m) * -BIG).astype(f)
    tabs["head32"] = (j // GLA_DK == np.arange(HEADS)[None, :]).astype(f)
    wide = {}
    for name, m in (("f", low), ("b", up)):
        cm = np.concatenate([m - m[:, mid:mid + 1], m[:, mid:mid + 1], np.ones((P, 1), f)], axis=1) / GLA_TAU
        wide["gcum_" + name] = cm.astype(f)
        wide["gafter_" + name] = (tabs["after_" + name] / GLA_TAU).astype(f)
    levels = []
    s = 1
    while s < P:
        m = ((j // (2 * s) == c // (2 * s)) & (j // s != c // s) & (j > c)).astype(f)
        levels.append(m)
        s *= 2
    tabs["levels_f"] = np.stack(levels, 1).reshape(P, -1)
    tabs["levels_b"] = np.stack([m.T for m in levels], 1).reshape(P, -1)
    gbd = (j // GLA_DK == np.arange(DG)[None, :] // HV).astype(f)
    wide["gla_bd"] = gbd
    q = np.arange(DG)[None, :]
    tabs["dn_bd"] = (j // HV == (q % P) // HV).astype(f)
    tabs["half"] = (j // HV == np.arange(2)[None, :]).astype(f)

    def packed(ts):
        offs, at = {}, 0
        for n, m in ts.items():
            offs[n] = (at, m.shape[1])
            at += m.shape[1]
        return np.ascontiguousarray(np.concatenate(list(ts.values()), 1)), offs

    return packed(tabs), packed(wide)


HALF = SEQ // 2
HT = HALF // P


def even_odd(t):
    return 2 * P * (t % HT) + t // HT


PARITY = np.concatenate([np.arange(0, SEQ, 2), np.arange(1, SEQ, 2)])


def dft_tables():
    n = np.arange(SEQ, dtype=np.float64)[:, None]
    th = math.pi * (2 * np.arange(HALF)[None, :] + 1) / (2 * SEQ)
    half = np.stack([np.cos(th * (n + 0.5)), np.sin(th * (n + 0.5))]).astype(np.float32)
    whole = np.stack([np.cos(th * n), np.sin(th * n)]).astype(np.float32)
    half, whole = half[:, PARITY], whole[:, PARITY]
    return half, np.ascontiguousarray(half.transpose(0, 2, 1)), whole


def filter_tables():
    pos = np.arange(SEQ, dtype=np.float32)
    t = pos / np.float32(SEQ - 1)
    bands = np.linspace(1e-4, 15, 16, dtype=np.float32)
    ang = np.float32(2.0 * math.pi / SEQ) * pos[:, None] * bands[None, :]
    feats = np.concatenate([t[:, None], np.cos(ang), -np.sin(ang)], axis=-1).astype(np.float32)
    lo, hi = math.log(1e-2) / 1.5, math.log(1e-2) / 0.3
    deltas = np.abs(np.linspace(lo, hi, DG, dtype=np.float32))
    window = np.exp(-t[:, None] * deltas[None, :]).astype(np.float32) / np.float32(SEQ)
    return np.ascontiguousarray(feats.T[:, PARITY]), np.ascontiguousarray(window[PARITY])


def shape_tables():
    (tab, _), (gla_tab, _) = tables()
    half, half_t, whole = dft_tables()
    feats, window = filter_tables()
    return {"tab": tab, "gla_tab": gla_tab, "dft_fwd": half, "dft_inv": half_t, "dft_whole": whole, "feats": feats, "window": window}


class Plan:

    def __init__(self, nc, at, end=SBUF_END):
        self.nc, self.at, self.end = nc, at, end

    def take(self, name, shape, dtype=F32):
        n = int(np.prod(shape[1:])) * 4
        t = self.nc.alloc_sbuf_tensor_at(name, list(shape), dtype, offset=self.at)
        self.at += (n + 31) // 32 * 32
        assert self.at <= self.end, (name, self.at, self.end)
        return t


class Chain:

    def __init__(self, eng, sem):
        self.eng, self.sem, self.n = eng, sem, 0

    def __call__(self, ins):
        self.n += 1
        ins.then_inc(self.sem, 1)
        self.eng.wait_ge(self.sem, self.n)


SPENT = []
SPENT_MAX = 110


@contextmanager
def Stage(nc, name, sems):
    if len(SPENT) > SPENT_MAX:
        nc.clear_and_free_semaphores(list(SPENT))
        nc.all_engine_barrier()
        SPENT.clear()
    named = {}
    for n in sems.split():
        n, _, ring = n.partition("*")
        got = [nc.alloc_semaphore(f"{name}_{n}{i}") for i in range(int(ring or 1))]
        SPENT.extend(got)
        named[n] = got if ring else got[0]
    with nc.Block() as block:
        yield namedtuple("Signals", ["block", *named])(block, *named.values())


class Store:
    pass


def load_and_modulate(nc, S, A):
    with Stage(nc, "mod", "cond params rows_in silu_c w_in*4 prod row_out cols_done pcols_t dve") as s:
        plan = Plan(nc, S.hT_at)
        wm = [plan.take(f"w_mod{b}", [P, KD // 2, D]) for b in range(4)]
        cc = plan.take("cond", [P, 2, KD])
        prow = plan.take("param_rows", [66, P])
        bmod = plan.take("b_mod_cols", [P, 2, KD])
        ngc = plan.take("norm_g_cols", [P, KD])
        row = plan.take("mod_rows", [2, 2, D])
        modc = plan.take("mod_cols", [P, 2, KD, 2])
        n_small = [0]

        @s.block.sync
        def _(sp):
            sp.dma_start(cc[:, 0, :], A["c"].rearrange("a (p k) -> p (a k)", p=P)).then_inc(s.cond, 16)
            sp.dma_start(cc[:, 1, :], A["c_ctx"].rearrange("(p k) -> p k", p=P)).then_inc(s.cond, 16)
            for b in range(4):
                j, h = b // 2, b % 2
                src = A["w_mod"][0, :, j * D:(j + 1) * D].rearrange("(p k) n -> p k n", p=P)
                sp.dma_start(wm[b][:, :, :], src[:, 4 * h:4 * h + 4, :]).then_inc(s.w_in[b], 16)

        @s.block.scalar
        def _(act):
            def load(dst, src):
                act.dma_start(dst, src).then_inc(s.params, 16)
                n_small[0] += 16
            act.wait_ge(s.cond, 32)
            nc.scalar.activation(S.silu_c[:, :, :].rearrange("p k s -> p s k"), cc[:, :, :], ACT.Silu
                                 ).then_inc(s.silu_c, 1)
            load(S.tab[:, :], A["tab"])
            load(prow[0:18, :], A["hy_conv_w"].rearrange("a t (b p) -> (a t b) p", p=P))
            load(prow[18:24, :], A["hy_conv_b"].rearrange("a (b p) -> (a b) p", p=P))
            load(prow[24:42, :], A["mb_conv_w"].rearrange("a t (b p) -> (a t b) p", p=P))
            load(prow[42:48, :], A["mb_conv_b"].rearrange("a (b p) -> (a b) p", p=P))
            load(prow[48:66, :], A["dn_conv_w"].rearrange("a t (b p) -> (a t b) p", p=P))
            load(bmod[:, :, :], A["b_mod"][:, 0:2 * D].rearrange("a (j p k) -> p (a j) k", p=P, k=KD))
            load(ngc[:, :], A["norm_g"][:, 0, :].rearrange("a (p k) -> p (a k)", p=P))
            for dst, src in ((S.gla_norm, A["gla_norm"]), (S.mb_norm, A["mb_norm"]), (S.dn_norm, A["dn_norm"])):
                act.dma_start(dst[:, :], src.rearrange("a n -> (a n)").partition_broadcast(P)).then_inc(s.rows_in, 16)
            for i, n in enumerate(("mb_a_log", "mb_dt_bias", "dn_a_log", "dn_dt_bias")):
                act.dma_start(S.gates[:, i, :], A[n].rearrange("a d h -> (a d h)").partition_broadcast(P)
                              ).then_inc(s.rows_in, 16)
            act.dma_start(S.mb_d[:, :], A["mb_d"].rearrange("a h -> (a h)").partition_broadcast(P)
                          ).then_inc(s.rows_in, 16)
            act.wait_ge(s.prod, 1)
            nc.scalar.activation(row[:, :, :].rearrange("p j n -> p (j n)"),
                                 S.ps[0:2, 2:6, :].rearrange("p a b -> p (a b)"), ACT.Copy).then_inc(s.row_out, 1)
            act.wait_ge(s.rows_in, 8 * 16)

        @s.block.tensor
        def _(pe):
            pe.wait_ge(s.silu_c, 1)
            for b in range(4):
                pe.wait_ge(s.w_in[b], 16)
                j, h = b // 2, b % 2
                for k in range(KD // 2):
                    for n in range(2):
                        last = nc.tensor.matmul(S.ps[0:2, 2 + 2 * j + n, :], S.silu_c[:, 4 * h + k, :],
                                                wm[b][:, k, n * 512:(n + 1) * 512],
                                                start=(h == 0 and k == 0), stop=(h == 1 and k == KD // 2 - 1))
            last.then_inc(s.prod, 1)
            pe.wait_ge(s.params, n_small[0])
            nc.tensor.transpose(S.ps[:, 1, 0:66], prow[:, :], S.t("ident")[0:66, 0:66]).then_inc(s.pcols_t, 1)
            pe.wait_ge(s.row_out, 1)
            for j in range(2):
                for k in range(KD):
                    q = (j * KD + k) * 2
                    last = nc.tensor.transpose(S.ps[:, 0, q:q + 2], row[:, j, k::KD], S.t("ident")[0:2, 0:2])
            last.then_inc(s.cols_done, 1)

        @s.block.vector
        def _(dve):
            ch = Chain(dve, s.dve)
            dve.wait_ge(s.pcols_t, 1)
            ch(nc.vector.tensor_copy(S.pcols[:, 0:66], S.ps[:, 1, 0:66]))
            ch(nc.vector.memset(S.pcols[:, 66:69], 0.0))
            ch(nc.vector.memset(S.pcols[:, 67:68], 1.0))
            dve.wait_ge(s.params, n_small[0])
            dve.wait_ge(s.cols_done, 1)
            m = S.ps[:, 0, 0:2 * KD * 2].rearrange("p (j k s) -> p j k s", j=2, k=KD)
            for st in range(2):
                ch(nc.vector.tensor_tensor(modc[:, :, :, st], m[:, :, :, st], bmod[:, :, :], ALU.add))
            for st in range(2):
                ch(nc.vector.scalar_tensor_tensor(S.mod1[:, 0, st, :], modc[:, 1, :, st], 1.0, ngc[:, :],
                                                  ALU.add, ALU.mult))
                ch(nc.vector.tensor_copy(S.mod1[:, 1, st, :], modc[:, 0, :, st]))


def normalise(nc, S, A):
    with Stage(nc, "nrm", "x_in*3 ss rt xs_done tr evac_a evac_v chain") as s:
        plan = Plan(nc, S.stage_at)
        xt = [plan.take(f"x_tile{b}", [P, D]) for b in range(3)]
        xn = [plan.take(f"x_norm{b}", [P, D]) for b in range(2)]
        sq = plan.take("x_square", [P, D])
        ss = plan.take("x_sum", [P, T, 3])

        @s.block.sync
        def _(sp):
            for t in range(T):
                src = A["ctx"][0, t * P:(t + 1) * P, :] if t < CT else A["x"][0, (t - CT) * P:(t - CT + 1) * P, :]
                if t >= 3:
                    sp.wait_ge(s.xs_done, t - 2)
                sp.dma_start(xt[t % 3][:, :], src).then_inc(s.x_in[t % 3], 16)
            load_weights(sp, S, A, 0, GLA_COLS)

        def evac(act, t):
            act.wait_ge(s.tr, t + 1)
            st = 1 if t < CT else 0
            for k in range(4):
                last = nc.scalar.activation(S.hT[:, k, t * P:(t + 1) * P],
                                            S.ps[:, 2 * (t % 2), k * P:(k + 1) * P], ACT.Identity,
                                            bias=S.mod1[:, 1, st, k:k + 1], scale=S.mod1[:, 0, st, k:k + 1])
            last.then_inc(s.evac_a, 1)

        @s.block.scalar
        def _(act):
            for t in range(T):
                act.wait_ge(s.x_in[t % 3], 16 * (t // 3 + 1))
                if t >= 1:
                    act.wait_ge(s.ss, t)
                nc.scalar.activation(sq[:, :], xt[t % 3][:, :], ACT.Square, accum_out=ss[:, t, 0:1]).then_inc(s.ss, 1)
                act.wait_ge(s.ss, t + 1)
                nc.scalar.activation(ss[:, t, 1:2], ss[:, t, 0:1], ACT.Sqrt, bias=S.eps[:, 0:1], scale=1.0 / D
                                     ).then_inc(s.rt, 1)
                if t >= 1:
                    evac(act, t - 1)
            evac(act, T - 1)

        @s.block.vector
        def _(dve):
            ch = Chain(dve, s.chain)

            def evac_v(t):
                dve.wait_ge(s.tr, t + 1)
                st = 1 if t < CT else 0
                for k in range(4, 8):
                    last = nc.vector.tensor_scalar(S.hT[:, k, t * P:(t + 1) * P],
                                                   S.ps[:, 2 * (t % 2) + 1, (k - 4) * P:(k - 3) * P],
                                                   S.mod1[:, 0, st, k:k + 1], S.mod1[:, 1, st, k:k + 1],
                                                   ALU.mult, ALU.add)
                last.then_inc(s.evac_v, 1)

            for t in range(T):
                dve.wait_ge(s.rt, t + 1)
                ch(nc.vector.reciprocal(ss[:, t, 2:3], ss[:, t, 1:2]))
                if t >= 2:
                    dve.wait_ge(s.tr, t - 1)
                nc.vector.tensor_scalar(xn[t % 2][:, :], xt[t % 3][:, :], ss[:, t, 2:3], None, ALU.mult
                                        ).then_inc(s.xs_done, 1)
                if t >= 1:
                    evac_v(t - 1)
            evac_v(T - 1)

        @s.block.tensor
        def _(pe):
            for t in range(T):
                pe.wait_ge(s.xs_done, t + 1)
                if t >= 2:
                    pe.wait_ge(s.evac_a, t - 1)
                    pe.wait_ge(s.evac_v, t - 1)
                for k in range(KD):
                    last = nc.tensor.transpose(S.ps[:, 2 * (t % 2) + k // 4, (k % 4) * P:(k % 4 + 1) * P],
                                               xn[t % 2][:, k::KD], S.t("ident"))
                last.then_inc(s.tr, 1)


def load_weights(sp, S, A, col, n):
    src = A["w_in"][0, :, col:col + n].rearrange("(p k) n -> p k n", p=P)
    for h in range(2):
        sp.dma_start(S.w[:, 4 * h:4 * h + 4, 0:n], src[:, 4 * h:4 * h + 4, :]).then_inc(S.w_ready, 16)
    S.w_count += 32


def project_conv(nc, S, A, name, blocks, plan, ctx=True, side=None):
    chunks = CHUNKS if ctx else CHUNKS[1:]
    groups = ((0, 2), (2, 6), (6, 10)) if ctx else ((2, 6), (6, 10))
    NC = len(chunks)
    lo = CTX_AT if ctx else LAT_AT
    tok0 = 0 if ctx else CTX
    t_first = 0 if ctx else CT
    with Stage(nc, name, "zeroed prod evac centre conv_ch conv_done tok_t tok_e cm_done "
                         + (side.sems if side else "")) as s:
        line = [plan.take(f"{name}_line{b}", [P, 1284]) for b in range(2)]
        cv = [plan.take(f"{name}_conv{b}", [P, 1284]) for b in range(2)]
        out = [plan.take(f"{name}_act{b}", [P, TOK]) for b in range(2)]
        NB = len(blocks)
        toks = [i for i, b in enumerate(blocks) if b["tok"] is not None]

        if side:
            @s.block.sync
            def _(sp):
                side.load(s, sp)

        def dst(i):
            return blocks[i]["cm"] if blocks[i]["cm"] is not None else out[i % 2][:, :]

        @s.block.gpsimd
        def _(pool):
            for b in range(2):
                last = nc.gpsimd.memset(line[b][:, 0:1], 0.0)
                last = nc.gpsimd.memset(line[b][:, 257:259], 0.0)
                last = nc.gpsimd.memset(line[b][:, 1283:1284], 0.0)
            last.then_inc(s.zeroed, 1)

        def to_tokens(pe, i):
            b = blocks[i]
            pe.wait_ge(s.cm_done, i + 1)
            n = toks.index(i)
            for g, (t0, t1) in enumerate(groups):
                if n * NC + g >= 2:
                    pe.wait_ge(s.tok_e, n * NC + g - 1)
                for t in range(t0, t1):
                    if b.get("by_parity"):
                        at = even_odd(t - CT)
                        src = dst(i)[:, at:at + 2 * P - 1:2]
                    else:
                        src = dst(i)[:, t * P - tok0:(t + 1) * P - tok0]
                    last = nc.tensor.transpose(S.ps[:, 6 + (n * NC + g) % 2, (t - t0) * P:(t - t0 + 1) * P], src,
                                               S.t("ident"))
                last.then_inc(s.tok_t, 1)

        @s.block.tensor
        def _(pe):
            pe.wait_ge(S.w_ready, S.w_count)
            for i, b in enumerate(blocks):
                for c, (t0, n) in enumerate(chunks):
                    if i >= 2:
                        pe.wait_ge(s.evac, NC * (i - 2) + c + 1)
                    for k in range(KD):
                        last = nc.tensor.matmul(S.ps[:, 3 * (i % 2) + c, 0:n], S.w[:, k, b["col"]:b["col"] + P],
                                                S.hT[:, k, t0:t0 + n], start=(k == 0), stop=(k == KD - 1))
                    last.then_inc(s.prod, 1)
                if i >= 1 and blocks[i - 1]["tok"] is not None:
                    to_tokens(pe, i - 1)
                if side:
                    side.pe(s, pe, i)
            if blocks[NB - 1]["tok"] is not None:
                to_tokens(pe, NB - 1)

        @s.block.scalar
        def _(act):
            act.wait_ge(s.zeroed, 1)

            def finish(i):
                b = blocks[i]
                act.wait_ge(s.conv_done, i + 1)
                if i >= 2 and blocks[i - 2]["tok"] is not None and blocks[i - 2]["cm"] is None:
                    act.wait_ge(s.tok_t, NC * (toks.index(i - 2) + 1))
                d = dst(i)
                c = cv[i % 2]
                f = ACT.Silu if b["silu"] else ACT.Identity
                if ctx:
                    nc.scalar.activation(d[:, 0:CTX], c[:, CTX_AT:CTX_AT + CTX], f)
                nc.scalar.activation(d[:, CTX - tok0:TOK - tok0], c[:, LAT_AT:LAT_AT + SEQ], f).then_inc(s.cm_done, 1)

            for i, b in enumerate(blocks):
                if i >= 2:
                    act.wait_ge(s.conv_done, i - 1)
                for c, (t0, n) in enumerate(chunks):
                    if c == NC - 1 and i >= 1:
                        finish(i - 1)
                        if side:
                            side.act(s, act, i - 1)
                    act.wait_ge(s.prod, NC * i + c + 1)
                    src = S.ps[:, 3 * (i % 2) + c, 0:n]
                    if t0 < CTX:
                        d = line[i % 2][:, CTX_AT:CTX_AT + CTX]
                    else:
                        l0 = t0 - CTX
                        r0 = l0 // GRID_W
                        if b["colmajor"]:
                            d = line[i % 2][:, LAT_AT:LAT_AT + SEQ].rearrange("p (w r) -> p r w", r=GRID_H)
                            d = d[:, r0:r0 + 8, :]
                            src = src.rearrange("p (r w) -> p r w", w=GRID_W)
                        else:
                            d = line[i % 2][:, LAT_AT + l0:LAT_AT + l0 + n]
                    nc.scalar.activation(d, src, ACT.Copy).then_inc(s.evac, 1)
                act.wait_ge(s.evac, NC * (i + 1))
                if i >= 2:
                    act.wait_ge(s.cm_done, i - 1)
                bias = S.pcols[:, b["bias"]:b["bias"] + 1] if b["bias"] is not None else S.zero[:, 0:1]
                w1 = b["tap"] + b["step"]
                nc.scalar.activation(cv[i % 2][:, lo:1283], line[i % 2][:, lo:1283], ACT.Identity, bias=bias,
                                     scale=S.pcols[:, w1:w1 + 1]).then_inc(s.centre, 1)
            finish(NB - 1)

        @s.block.vector
        def _(dve):
            ch = Chain(dve, s.conv_ch)

            def copy_tokens(i):
                b = blocks[i]
                n = toks.index(i)
                for g, (t0, t1) in enumerate(groups):
                    dve.wait_ge(s.tok_t, n * NC + g + 1)
                    src = S.ps[:, 6 + (n * NC + g) % 2, 0:(t1 - t0) * P].rearrange("p (t c) -> p t c", c=P)
                    a0 = CT if b.get("latents") else t_first
                    if t1 <= a0:
                        nc.vector.engine_nop().then_inc(s.tok_e, 1)
                    else:
                        nc.vector.tensor_copy(b["tok"][:, t0 - a0:t1 - a0, :], src[:, :, b.get("sub", 0):P]
                                              ).then_inc(s.tok_e, 1)

            for i, b in enumerate(blocks):
                if i >= 1 and blocks[i - 1]["tok"] is not None:
                    copy_tokens(i - 1)
                dve.wait_ge(s.centre, i + 1)
                c, l = cv[i % 2], line[i % 2]
                ch(nc.vector.scalar_tensor_tensor(c[:, lo:1283], l[:, lo - 1:1282], S.pcols[:, b["tap"]:b["tap"] + 1],
                                                  c[:, lo:1283], ALU.mult, ALU.add))
                w2 = b["tap"] + 2 * b["step"]
                nc.vector.scalar_tensor_tensor(c[:, lo:1283], l[:, lo + 1:1284], S.pcols[:, w2:w2 + 1],
                                               c[:, lo:1283], ALU.mult, ALU.add).then_inc(s.conv_done, 1)
                if side:
                    side.dve(s, dve, ch, i)
            if blocks[NB - 1]["tok"] is not None:
                copy_tokens(NB - 1)


def token_products(nc, S, s, pe, jobs):
    pe.wait_ge(S.w_ready, S.w_count)
    for i, (t, col, n) in enumerate(jobs):
        if i >= 6:
            pe.wait_ge(s.tp_out, i - 5)
        for k in range(KD):
            lhs = S.hT[:, k, t * P:(t + 1) * P]
            last = nc.tensor.matmul(S.ps[:, i % 6, 0:n], lhs, S.w[:, k, col:col + n], start=(k == 0), stop=(k == KD - 1))
        last.then_inc(s.tp, 1)


def token_copies(nc, S, s, act, jobs, dsts):
    for i in range(len(jobs)):
        act.wait_ge(s.tp, i + 1)
        for d, a, n in dsts[i]:
            last = nc.scalar.activation(d, S.ps[:, i % 6, a:a + n], ACT.Copy)
        last.then_inc(s.tp_out, 1)


def head_norm(nc, S, name, o, gate, norm_w, gate_first, block0, plan, colmajor, extra=None, loads=None):
    with Stage(nc, name, "sil weighed sq red rt chain tr cp") as s:
        n = LT * HEADS
        w = norm_w[:, :].unsqueeze(1).to_broadcast([P, LT, DG])
        sq = plan.take(name + "_sq", [P, LT, DG])
        st = plan.take(name + "_stat", [P, 3, n])
        o4 = o[:, :, :].rearrange("p t (h v) -> p (t h) v", v=HV)

        if loads is not None:
            @s.block.sync
            def _(sp):
                loads(sp)

        @s.block.scalar
        def _(act):
            nc.scalar.activation(gate[:, :, :], gate[:, :, :], ACT.Silu).then_inc(s.sil, 1)
            act.wait_ge(s.red, 1)
            nc.scalar.activation(st[:, 1, :], st[:, 0, :], ACT.Sqrt, bias=S.eps[:, 0:1], scale=1.0 / HV
                                 ).then_inc(s.rt, 1)
            for i in range(4):
                act.wait_ge(s.tr, i + 1)
                kb, half = i // 2, i % 2
                if colmajor:
                    d = S.yT[:, block0 + kb, :].rearrange("p (r w) -> p w r", w=GRID_W)
                    d = d[:, half * 32:half * 32 + 32, :]
                    src = S.ps[:, i % 2, :].rearrange("p (w r) -> p w r", r=GRID_H)
                else:
                    d = S.yT[:, block0 + kb, half * 512:half * 512 + 512]
                    src = S.ps[:, i % 2, :]
                nc.scalar.activation(d, src, ACT.Copy).then_inc(s.cp, 1)

        @s.block.vector
        def _(dve):
            ch = Chain(dve, s.chain)
            if extra is not None:
                extra(dve, ch)
            if gate_first:
                dve.wait_ge(s.sil, 1)
                ch(nc.vector.tensor_tensor(o[:, :, :], o[:, :, :], gate[:, :, :], ALU.mult))
            ch(nc.vector.tensor_tensor(sq[:, :, :], o[:, :, :], o[:, :, :], ALU.mult))
            nc.vector.tensor_reduce(st[:, 0, :], sq[:, :, :].rearrange("p t (h v) -> p (t h) v", v=HV), AX.X, ALU.add
                                    ).then_inc(s.red, 1)
            dve.wait_ge(s.rt, 1)
            ch(nc.vector.reciprocal(st[:, 2, :], st[:, 1, :]))
            ch(nc.vector.tensor_tensor(o4, o4, st[:, 2, :].unsqueeze(2).to_broadcast([P, n, HV]), ALU.mult))
            if gate_first:
                nc.vector.tensor_tensor(o[:, :, :], o[:, :, :], w, ALU.mult).then_inc(s.sq, 1)
            else:
                dve.wait_ge(s.weighed, 1)
                nc.vector.tensor_tensor(o[:, :, :], o[:, :, :], gate[:, :, :], ALU.mult).then_inc(s.sq, 1)

        if not gate_first:
            @s.block.gpsimd
            def _(pool):
                pool.wait_ge(s.sil, 1)
                nc.gpsimd.tensor_tensor(gate[:, :, :], gate[:, :, :], w, ALU.mult).then_inc(s.weighed, 1)

        @s.block.tensor
        def _(pe):
            pe.wait_ge(s.sq, 1)
            for i in range(4):
                kb, half = i // 2, i % 2
                if i >= 2:
                    pe.wait_ge(s.cp, i - 1)
                for t in range(4):
                    last = nc.tensor.transpose(S.ps[:, i % 2, t * P:(t + 1) * P],
                                               o[:, half * 4 + t, kb * P:(kb + 1) * P], S.t("ident"))
                last.then_inc(s.tr, 1)


ORDER = {"f": list(range(T)), "b": [1, 0] + list(range(T - 1, CT - 1, -1))}


def units():
    return [(2 * st + d, st, d, ORDER["fb"[d]][st]) for st in range(T) for d in range(2)]


def gla(nc, S, A):
    plan = Plan(nc, S.stage_at)
    v = plan.take("gla_v", [P, T, DG])
    og = plan.take("gla_og", [P, LT, DG])
    kt = plan.take("gla_k_tok", [P, T, P])
    qT = plan.take("gla_qT", [P, TOK])
    kT = plan.take("gla_kT", [P, TOK])
    la = plan.take("gla_log_alpha", [P, T, 2, P])
    o = plan.take("gla_o", [P, LT, DG])
    gt = plan.take("gla_tables", [P, S.gn])
    goff = S.goff

    def G(name):
        return gt[:, goff[name][0]:goff[name][0] + goff[name][1]]

    mark = plan.at
    with Stage(nc, "gla_p", "tabs ones w2 w2_in prod evac tp tp_out z e1 e2 abs_done chain wm_in*4 mod_in g_one added "
                            "summed k_turned kt_out rows_done rows_st") as s:
        lr = plan.take("gla_lrT", [33, TOK])
        w2 = plan.take("gla_w2", [33, 2, P])
        ab = plan.take("gla_abs", [P, T, 2, P])
        low = Plan(nc, S.yT_at, S.hT_at)
        acc = low.take("mod_acc", [P, 4, D])
        wm = [low.take(f"w_mod_row{b}", [P, D]) for b in range(4)]
        mrow = plan.take("mod_later", [4, 3, D])
        pick = plan.take("mod_pick", [P, 4, 4])
        MODS = (2, 4, 3, 5)
        cms = ((0, P, qT, GLA_DK ** -0.5), (P, P, kT, 1.0), (768, 32, lr, 1.0))
        jobs, dsts = [], []
        for t in range(T):
            jobs.append((t, 256, 512 if t >= CT else 256))
            dsts.append([(v[:, t, :], 0, DG)] + ([(og[:, t - CT, :], DG, DG)] if t >= CT else []))

        @s.block.sync
        def _(sp):
            sp.dma_start(gt[:, :], A["gla_tab"]).then_inc(s.tabs, 16)
            sp.wait_ge(s.w2, 1)
            for d in range(2):
                sp.dma_start(w2[16 * d:16 * d + 16, d, :], A["gla_w2"][0, d, :, :]).then_inc(s.w2_in, 16)
            sp.dma_start(w2[32:33, :, :], A["gla_b"]).then_inc(s.w2_in, 16)
            for i, j in enumerate(MODS):
                sp.dma_start(mrow[i:i + 1, 1, :], A["b_mod"][:, j * D:(j + 1) * D]).then_inc(s.mod_in, 16)
            sp.wait_ge(s.g_one, 1)
            for i, j in ((0, 1), (1, 2), (3, 3)):
                sp.dma_start(mrow[i:i + 1, 2, :], A["norm_g"][:, j, :]).then_inc(s.mod_in, 16)
            for q in range(4 * KD):
                i, k = q // KD, q % KD
                if q >= 4:
                    sp.wait_ge(s.added, q - 3)
                src = A["w_mod"][0, :, MODS[i] * D:(MODS[i] + 1) * D].rearrange("(p k) n -> p k n", p=P)
                sp.dma_start(wm[q % 4][:, :], src[:, k, :]).then_inc(s.wm_in[q % 4], 16)
            sp.wait_ge(s.tabs, 16)
            sp.wait_ge(s.rows_done, 1)
            sp.dma_start(A["rows"], mrow[:, 0, :]).then_inc(s.rows_st, 16)
            sp.wait_ge(s.rows_st, 16)

        @s.block.gpsimd
        def _(pool):
            nc.gpsimd.memset(lr[32:33, :], 1.0).then_inc(s.ones, 1)
            pool.wait_ge(s.ones, 1)
            nc.gpsimd.memset(w2[:, :, :], 0.0).then_inc(s.w2, 1)

        @s.block.tensor
        def _(pe):
            pe.wait_ge(S.w_ready, S.w_count)
            for i, (col, m, dst, _) in enumerate(cms):
                for c, (t0, n) in enumerate(CHUNKS):
                    q = 3 * i + c
                    if q >= 6:
                        pe.wait_ge(s.evac, q - 5)
                    for k in range(KD):
                        last = nc.tensor.matmul(S.ps[0:m, q % 6, 0:n], S.w[:, k, col:col + m], S.hT[:, k, t0:t0 + n],
                                                start=(k == 0), stop=(k == KD - 1))
                    last.then_inc(s.prod, 1)
            pe.wait_ge(s.evac, 9)
            for g in range(3):
                t1 = min(4 * g + 4, T)
                if g == 2:
                    pe.wait_ge(s.kt_out, 1)
                for t in range(4 * g, t1):
                    last = nc.tensor.transpose(S.ps[:, 6 + g % 2, (t - 4 * g) * P:(t - 4 * g + 1) * P],
                                               kT[:, t * P:(t + 1) * P], S.t("ident"))
                last.then_inc(s.k_turned, 1)
            token_products(nc, S, s, pe, jobs)
            pe.wait_ge(s.tp_out, len(jobs))
            pe.wait_ge(s.w2_in, 48)
            pe.wait_ge(s.ones, 1)
            for t in range(T):
                last = nc.tensor.matmul(S.ps[:, t // 2, (t % 2) * 256:(t % 2) * 256 + 256],
                                        lr[:, t * P:(t + 1) * P], w2[:, :, :].rearrange("p d c -> p (d c)"),
                                        start=True, stop=True)
            last.then_inc(s.z, 1)
            pe.wait_ge(s.added, 4 * KD)
            pe.wait_ge(s.kt_out, 3)
            for n in range(2):
                for i in range(4):
                    last = nc.tensor.matmul(S.ps[0:4, 6 + n, :], pick[:, i, :], acc[:, i, n * 512:(n + 1) * 512],
                                            start=(i == 0), stop=(i == 3))
            last.then_inc(s.summed, 1)

        @s.block.scalar
        def _(act):
            for i, (col, m, dst, scale) in enumerate(cms):
                for c, (t0, n) in enumerate(CHUNKS):
                    q = 3 * i + c
                    act.wait_ge(s.prod, q + 1)
                    nc.scalar.activation(dst[0:m, t0:t0 + n], S.ps[0:m, q % 6, 0:n], ACT.Copy, scale=scale
                                         ).then_inc(s.evac, 1)
            for g in range(3):
                t1 = min(4 * g + 4, T)
                act.wait_ge(s.k_turned, g + 1)
                nc.scalar.activation(kt[:, 4 * g:t1, :].rearrange("p t c -> p (t c)"),
                                     S.ps[:, 6 + g % 2, 0:(t1 - 4 * g) * P], ACT.Copy).then_inc(s.kt_out, 1)
            token_copies(nc, S, s, act, jobs, dsts)
            act.wait_ge(s.z, 1)
            nc.scalar.activation(ab[:, :, :, :].rearrange("p t d c -> p (t d c)"),
                                 S.ps[:, 0:5, :].rearrange("p b n -> p (b n)"), ACT.Abs).then_inc(s.abs_done, 1)
            act.wait_ge(s.abs_done, 1)
            nc.scalar.activation(ab[:, :, :, :], ab[:, :, :, :], ACT.Exp, scale=-1.0).then_inc(s.e1, 1)
            act.wait_ge(s.e1, 1)
            nc.scalar.activation(ab[:, :, :, :], ab[:, :, :, :], ACT.Ln, bias=S.one[:, 0:1]).then_inc(s.e2, 1)

        @s.block.vector
        def _(dve):
            ch = Chain(dve, s.chain)
            nc.vector.memset(mrow[:, 2, :], 1.0).then_inc(s.g_one, 1)
            ch(nc.vector.memset(pick[:, :, :], 0.0))
            ch(nc.vector.memset(pick[:, :, :].rearrange("p j i -> p (j i)")[:, 0:16:5], 1.0))
            for q in range(4 * KD):
                i, k = q // KD, q % KD
                dve.wait_ge(s.wm_in[q % 4], 16 * (q // 4 + 1))
                if k == 0:
                    nc.vector.tensor_scalar(acc[:, i, :], wm[q % 4][:, :], S.silu_c[:, k, 0:1], None, ALU.mult
                                            ).then_inc(s.added, 1)
                else:
                    dve.wait_ge(s.added, q)
                    nc.vector.scalar_tensor_tensor(acc[:, i, :], wm[q % 4][:, :], S.silu_c[:, k, 0:1], acc[:, i, :],
                                                   ALU.mult, ALU.add).then_inc(s.added, 1)
            dve.wait_ge(s.z, 1)
            z = S.ps[:, 0:5, :].rearrange("p b n -> p (b n)")
            abf = ab[:, :, :, :].rearrange("p t d c -> p (t d c)")
            dve.wait_ge(s.e2, 1)
            nc.vector.scalar_tensor_tensor(la[:, :, :, :].rearrange("p t d c -> p (t d c)"), z, 0.0, abf,
                                           ALU.min, ALU.subtract)
            dve.wait_ge(s.summed, 1)
            dve.wait_ge(s.mod_in, 7 * 16)
            ch(nc.vector.tensor_tensor(mrow[:, 0, :], S.ps[0:4, 6:8, :].rearrange("p a b -> p (a b)"), mrow[:, 1, :], ALU.add))
            ch(nc.vector.tensor_scalar(mrow[:, 0, :], mrow[:, 0, :], S.t("ident")[0:4, 1:2], None, ALU.add))
            nc.vector.tensor_tensor(mrow[:, 0, :], mrow[:, 0, :], mrow[:, 2, :], ALU.mult).then_inc(s.rows_done, 1)

    plan.at = mark
    with Stage(nc, "gla_s", "cum exps prep_v prep_p attn masked o kv s_use s_ch o_out chain") as s:
        ex = [plan.take(f"gla_exp{b}", [P, 258]) for b in range(3)]
        en = [plan.take(f"gla_expn{b}", [P, P]) for b in range(3)]
        qg = [plan.take(f"gla_qg{b}", [P, P]) for b in range(3)]
        qb = [plan.take(f"gla_qbd{b}", [P, HEADS, P]) for b in range(3)]
        kg = [plan.take(f"gla_kg{b}", [P, P]) for b in range(3)]
        ke = [plan.take(f"gla_ke{b}", [P, P]) for b in range(3)]
        am = [plan.take(f"gla_attn{b}", [P, HEADS, P]) for b in range(2)]
        kv = [plan.take(f"gla_kv{b}", [P, DG]) for b in range(2)]
        Sd = [plan.take(f"gla_state{b}", [P, DG]) for b in range(2)]
        Su = [plan.take(f"gla_state_use{b}", [P, DG]) for b in range(4)]
        U = units()
        N = len(U)

        @s.block.sync
        def _(sp):
            load_weights(sp, S, A, MB0, MB_COLS)

        @s.block.tensor
        def _(pe):
            for n in range(N + 2):
                if n < N:
                    _, st, d, t = U[n]
                    dn = "fb"[d]
                    if n >= 2:
                        pe.wait_ge(s.exps, n - 1)
                    nc.tensor.matmul(S.ps[:, n % 2, 0:130], la[:, t, d, :], G("gcum_" + dn), start=True, stop=True)
                    nc.tensor.matmul(S.ps[:, n % 2, 130:258], G("gafter_" + dn), la[:, t, d, :],
                                     start=True, stop=True).then_inc(s.cum, 1)
                if 1 <= n <= N:
                    m = n - 1
                    t = U[m][3]
                    pe.wait_ge(s.prep_v, m + 1)
                    pe.wait_ge(s.prep_p, m + 1)
                    if m >= 2:
                        pe.wait_ge(s.masked, m - 1)
                        pe.wait_ge(s.s_use, m - 1)
                    nc.tensor.matmul(S.ps[:, 2 + m % 2, :], kg[m % 3][:, :], qb[m % 3][:, :, :].rearrange("p h c -> p (h c)"),
                                     start=True, stop=True).then_inc(s.attn, 1)
                    nc.tensor.matmul(S.ps[:, 6 + m % 2, 0:DG], ke[m % 3][:, :], v[:, t, :], start=True, stop=True
                                     ).then_inc(s.kv, 1)
                if n >= 2:
                    m = n - 2
                    t = U[m][3]
                    pe.wait_ge(s.masked, m + 1)
                    pe.wait_ge(s.s_use, m + 1)
                    if m >= 2:
                        pe.wait_ge(s.o_out, m - 1)
                    nc.tensor.matmul(S.ps[:, 4 + m % 2, 0:DG], qg[m % 3][:, :], Su[m % 4][:, :], start=True, stop=False,
                                     skip_group_check=True)
                    for h in range(HEADS):
                        last = nc.tensor.matmul(S.ps[:, 4 + m % 2, h * HV:(h + 1) * HV], am[m % 2][:, h, :],
                                                v[:, t, h * HV:(h + 1) * HV], start=False, stop=(h == HEADS - 1),
                                                skip_group_check=True)
                    last.then_inc(s.o, 1)

        @s.block.scalar
        def _(act):
            for n in range(N):
                act.wait_ge(s.cum, n + 1)
                if n >= 3:
                    act.wait_ge(s.prep_v, n - 2)
                    act.wait_ge(s.prep_p, n - 2)
                    act.wait_ge(s.s_use, n - 2)
                    act.wait_ge(s.s_ch, n - 2)
                nc.scalar.activation(ex[n % 3][:, :], S.ps[:, n % 2, 0:258], ACT.Exp)
                nc.scalar.activation(en[n % 3][:, :], S.ps[:, n % 2, 0:P], ACT.Exp, scale=-1.0).then_inc(s.exps, 1)

        @s.block.gpsimd
        def _(pool):
            for n in range(N):
                _, st, d, t = U[n]
                pool.wait_ge(s.exps, n + 1)
                if n >= 3:
                    pool.wait_ge(s.attn, n - 2)
                    pool.wait_ge(s.kv, n - 2)
                nc.gpsimd.tensor_tensor(kg[n % 3][:, :], kT[:, t * P:(t + 1) * P], en[n % 3][:, :], ALU.mult)
                nc.gpsimd.tensor_tensor(ke[n % 3][:, :], kt[:, t, :], ex[n % 3][:, 130:258], ALU.mult
                                        ).then_inc(s.prep_p, 1)

        @s.block.vector
        def _(dve):
            ch = Chain(dve, s.chain)
            for d in range(2):
                ch(nc.vector.memset(Sd[d][:, :], 0.0))
            hm = S.t("head32").unsqueeze(2).to_broadcast([P, HEADS, P])

            def prep(n):
                _, st, d, t = U[n]
                dve.wait_ge(s.exps, n + 1)
                if n >= 3:
                    dve.wait_ge(s.o, n - 2)
                ch(nc.vector.tensor_tensor(qg[n % 3][:, :], qT[:, t * P:(t + 1) * P], ex[n % 3][:, 0:P], ALU.mult))
                nc.vector.tensor_tensor(qb[n % 3][:, :, :], qg[n % 3][:, :].unsqueeze(1).to_broadcast([P, HEADS, P]),
                                        hm, ALU.mult).then_inc(s.prep_v, 1)

            def mask(m):
                _, st, d, t = U[m]
                dve.wait_ge(s.attn, m + 1)
                if m >= 2:
                    dve.wait_ge(s.o, m - 1)
                tri = S.t("tri_" + "fb"[d]).unsqueeze(1).to_broadcast([P, HEADS, P])
                nc.vector.tensor_tensor(am[m % 2][:, :, :], S.ps[:, 2 + m % 2, :].rearrange("p (h c) -> p h c", c=P),
                                        tri, ALU.mult).then_inc(s.masked, 1)

            def state(m):
                _, st, d, t = U[m]
                dve.wait_ge(s.kv, m + 1)
                if m >= 2:
                    dve.wait_ge(s.s_ch, m - 1)
                ch(nc.vector.tensor_tensor(kv[m % 2][:, :], S.ps[:, 6 + m % 2, 0:DG], G("gla_bd"), ALU.mult))
                if m >= 4:
                    dve.wait_ge(s.o, m - 3)
                nc.vector.tensor_scalar(Su[m % 4][:, :], Sd[d][:, :], ex[m % 3][:, P:P + 1], None, ALU.mult
                                        ).then_inc(s.s_use, 1)
                dve.wait_ge(s.s_use, m + 1)
                nc.vector.scalar_tensor_tensor(Sd[d][:, :], Sd[d][:, :], ex[m % 3][:, P + 1:P + 2], kv[m % 2][:, :],
                                               ALU.mult, ALU.add).then_inc(s.s_ch, 1)

            def take(m):
                _, st, d, t = U[m]
                dve.wait_ge(s.o, m + 1)
                add_output(nc, dve, s, S.ps[:, 4 + m % 2, 0:DG], o, st, d, t, s.o_out)

            for n in range(N + 3):
                if 3 <= n:
                    take(n - 3)
                if n < N:
                    prep(n)
                if 1 <= n <= N:
                    mask(n - 1)
                    state(n - 1)

    plan.at = mark
    head_norm(nc, S, "gla_n", o, og, S.gla_norm, False, 0, plan, False)


def add_output(nc, dve, s, src, o, st, d, t, done):
    if t < CT:
        nc.vector.engine_nop().then_inc(done, 1)
        return
    first = st < T - st + 1
    if first:
        nc.vector.tensor_copy(o[:, t - CT, :], src).then_inc(done, 1)
    else:
        dve.wait_ge(done, 2 * (T + 1 - st) + (1 - d) + 1)
        nc.vector.tensor_tensor(o[:, t - CT, :], src, o[:, t - CT, :], ALU.add).then_inc(done, 1)


def gate_sums(nc, S, s, pe, g, bank):
    out = S.ps[:, bank, 0:240].rearrange("p (w d n) -> p w d n", w=3, d=2)
    for d in range(2):
        rhs = g[:, :, d, :]
        for w, m in enumerate((S.t("tri_" + "fb"[d]), S.t("after_" + "fb"[d]), S.ones[:, :])):
            last = nc.tensor.matmul(out[:, w, d, :], m, rhs, start=True, stop=True)
    return last


def mamba(nc, S, A):
    plan = Plan(nc, S.stage_at)
    xt = plan.take("mb_x", [P, T, DG])
    bt = plan.take("mb_b", [P, T, DG])
    bT = plan.take("mb_bT", [P, 2, TOK])
    cT = plan.take("mb_cT", [P, 2, TOK])
    z = plan.take("mb_z", [P, LT, DG])
    dt = plan.take("mb_dt", [P, T, 2, HEADS])
    ga = plan.take("mb_g", [P, T, 2, HEADS])
    cu = plan.take("mb_cum", [P, 3, 2, T * HEADS])
    eu = plan.take("mb_cum_exp", [P, 3, 2, T * HEADS])
    small = plan.at
    o = plan.take("mb_o", [P, LT, DG])
    mark = plan.at
    blocks = []
    for b in range(6):
        cm = None if b < 2 else (bT if b < 4 else cT)[:, b % 2, :]
        tok = (xt if b < 2 else bt)[:, :, (b % 2) * P:(b % 2 + 1) * P] if b < 4 else None
        blocks.append(dict(col=256 + b * P, tap=24 + b, step=6, bias=42 + b, silu=True, colmajor=True, cm=cm, tok=tok))
    for b in range(2):
        blocks.append(dict(col=b * P, tap=66, step=1, bias=None, silu=False, colmajor=True, cm=None,
                           tok=z[:, :, b * P:(b + 1) * P], latents=True))
    blocks.append(dict(col=MB_COLS - P, tap=66, step=1, bias=None, silu=False, colmajor=True, cm=None,
                       tok=dt[:, :, :, :].rearrange("p t d h -> p t (d h)"), sub=P - 8))
    project_conv(nc, S, A, "mb_c", blocks, Plan(nc, small))
    with Stage(nc, "mb_t", "biased ab e1 e2 ea sp chain sums") as s:
        ab = plan.take("mb_abs", [P, T * 8])
        ea = plan.take("mb_decay", [P, 8])
        @s.block.tensor
        def _(pe):
            pe.wait_ge(s.sp, 1)
            gate_sums(nc, S, s, pe, ga, 6).then_inc(s.sums, 1)

        @s.block.scalar
        def _(act):
            act.wait_ge(s.biased, 1)
            nc.scalar.activation(ab[:, :], dt[:, :, :, :].rearrange("p t d h -> p (t d h)"), ACT.Abs).then_inc(s.ab, 1)
            act.wait_ge(s.ab, 1)
            nc.scalar.activation(ab[:, :], ab[:, :], ACT.Exp, scale=-1.0).then_inc(s.e1, 1)
            act.wait_ge(s.e1, 1)
            nc.scalar.activation(ab[:, :], ab[:, :], ACT.Ln, bias=S.one[:, 0:1]).then_inc(s.e2, 1)
            nc.scalar.activation(ea[:, :], S.gates[:, 0, :], ACT.Exp).then_inc(s.ea, 1)
            act.wait_ge(s.sums, 1)
            nc.scalar.activation(eu[:, :, :, :], S.ps[:, 6, 0:240].rearrange("p (w d n) -> p w d n", w=3, d=2), ACT.Exp
                                 ).then_inc(s.ea, 1)

        @s.block.vector
        def _(dve):
            ch = Chain(dve, s.chain)
            dtf = dt[:, :, :, :].rearrange("p t d h -> p t (d h)")
            nc.vector.tensor_tensor(dtf, dtf, S.gates[:, 1, :].unsqueeze(1).to_broadcast([P, T, 8]), ALU.add
                                    ).then_inc(s.biased, 1)
            dt1 = dt[:, :, :, :].rearrange("p t d h -> p (t d h)")
            dve.wait_ge(s.e2, 1)
            ch(nc.vector.scalar_tensor_tensor(dt1, dt1, 0.0, ab[:, :], ALU.max, ALU.add))
            dve.wait_ge(s.ea, 1)
            ch(nc.vector.tensor_scalar(ea[:, :], ea[:, :], -1.0, None, ALU.mult))
            nc.vector.tensor_tensor(ga[:, :, :, :].rearrange("p t d h -> p t (d h)"), dtf,
                                    ea[:, :].unsqueeze(1).to_broadcast([P, T, 8]), ALU.mult).then_inc(s.sp, 1)
            dve.wait_ge(s.ea, 2)
            ch(nc.vector.tensor_copy(cu[:, :, :, :], S.ps[:, 6, 0:240].rearrange("p (w d n) -> p w d n", w=3, d=2)))

    plan.at = mark
    with Stage(nc, "mb_s", "rows rel seg cb at xdt xde y y_out st s_new chain") as s:
        sg = [plan.take(f"mb_seg{b}", [P, HEADS, P]) for b in range(2)]
        am = [plan.take(f"mb_attn{b}", [P, HEADS, P]) for b in range(2)]
        xd = [plan.take(f"mb_xdt{b}", [P, DG]) for b in range(3)]
        xe = [plan.take(f"mb_xde{b}", [P, DG]) for b in range(3)]
        yo = [plan.take(f"mb_yo{b}", [P, DG]) for b in range(2)]
        St = [plan.take(f"mb_state{b}", [P, DG]) for b in range(2)]
        U = units()
        N = len(U)

        @s.block.sync
        def _(sp):
            load_weights(sp, S, A, DN0, DN_COLS)

        @s.block.tensor
        def _(pe):
            for n in range(N + 2):
                if n < N:
                    _, st, d, t = U[n]
                    if n >= 2:
                        pe.wait_ge(s.rel, n - 1)
                        pe.wait_ge(s.at, n - 1)
                    for h in range(HEADS):
                        last = nc.tensor.matmul(S.ps[:, n % 2, h * P:(h + 1) * P],
                                                ga[:, t, d, h:h + 1].to_broadcast([P, P]), S.t("tri_" + "fb"[d]),
                                                start=True, stop=True)
                    last.then_inc(s.rows, 1)
                    for g in range(2):
                        last = nc.tensor.matmul(S.ps[:, 2 + n % 2, g * P:(g + 1) * P], bT[:, g, t * P:(t + 1) * P],
                                                cT[:, g, t * P:(t + 1) * P], start=True, stop=True)
                    last.then_inc(s.cb, 1)
                if 1 <= n <= N:
                    m = n - 1
                    t = U[m][3]
                    pe.wait_ge(s.xde, m + 1)
                    if m >= 2:
                        pe.wait_ge(s.s_new, m - 1)
                    for g in range(2):
                        last = nc.tensor.matmul(S.ps[:, 6 + m % 2, g * P:(g + 1) * P], bt[:, t, g * P:(g + 1) * P],
                                                xe[m % 3][:, g * P:(g + 1) * P], start=True, stop=True)
                    last.then_inc(s.st, 1)
                if n >= 2:
                    m = n - 2
                    t, d = U[m][3], U[m][2]
                    pe.wait_ge(s.at, m + 1)
                    pe.wait_ge(s.s_new, m - 1) if m >= 2 else pe.wait_ge(s.chain, 2)
                    if m >= 2:
                        pe.wait_ge(s.y_out, m - 1)
                    for h in range(HEADS):
                        nc.tensor.matmul(S.ps[:, 4 + m % 2, h * HV:(h + 1) * HV], am[m % 2][:, h, :],
                                         xd[m % 3][:, h * HV:(h + 1) * HV], start=True, stop=True)
                    for g in range(2):
                        last = nc.tensor.matmul(S.ps[:, 4 + m % 2, DG + g * P:DG + (g + 1) * P],
                                                cT[:, g, t * P:(t + 1) * P], St[d][:, g * P:(g + 1) * P],
                                                start=True, stop=True)
                    last.then_inc(s.y, 1)

        @s.block.scalar
        def _(act):
            for n in range(N):
                act.wait_ge(s.rel, n + 1)
                nc.scalar.activation(sg[n % 2][:, :, :], sg[n % 2][:, :, :], ACT.Exp).then_inc(s.seg, 1)

        @s.block.gpsimd
        def _(pool):
            for n in range(N):
                _, st, d, t = U[n]
                if n >= 3:
                    pool.wait_ge(s.y, n - 2)
                    pool.wait_ge(s.st, n - 2)
                nc.gpsimd.tensor_tensor(xd[n % 3][:, :].rearrange("p (h v) -> p h v", v=HV),
                                        xt[:, t, :].rearrange("p (h v) -> p h v", v=HV),
                                        dt[:, t, d, :].unsqueeze(2).to_broadcast([P, HEADS, HV]), ALU.mult
                                        ).then_inc(s.xdt, 1)
                pool.wait_ge(s.xdt, n + 1)
                nc.gpsimd.tensor_tensor(xe[n % 3][:, :].rearrange("p (h v) -> p h v", v=HV),
                                        xd[n % 3][:, :].rearrange("p (h v) -> p h v", v=HV),
                                        eu[:, 1, d, t * HEADS:(t + 1) * HEADS].unsqueeze(2).to_broadcast([P, HEADS, HV]),
                                        ALU.mult).then_inc(s.xde, 1)

        @s.block.vector
        def _(dve):
            ch = Chain(dve, s.chain)
            for d in range(2):
                ch(nc.vector.memset(St[d][:, :], 0.0))

            def front(n):
                _, st, d, t = U[n]
                dve.wait_ge(s.rows, n + 1)
                if n >= 2:
                    dve.wait_ge(s.at, n - 1)
                for h in range(HEADS):
                    c = t * HEADS + h
                    last = nc.vector.scalar_tensor_tensor(sg[n % 2][:, h, :], S.ps[:, n % 2, h * P:(h + 1) * P],
                                                          cu[:, 0, d, c:c + 1], S.t("neg_" + "fb"[d]),
                                                          ALU.subtract, ALU.add)
                last.then_inc(s.rel, 1)

            def scores(n):
                dve.wait_ge(s.seg, n + 1)
                dve.wait_ge(s.cb, n + 1)
                if n >= 2:
                    dve.wait_ge(s.y, n - 1)
                nc.vector.tensor_tensor(am[n % 2][:, :, :].rearrange("p (g r) c -> p g r c", g=2),
                                        sg[n % 2][:, :, :].rearrange("p (g r) c -> p g r c", g=2),
                                        S.ps[:, 2 + n % 2, 0:DG].rearrange("p (g c) -> p g c", g=2).unsqueeze(2)
                                        .to_broadcast([P, 2, 2, P]), ALU.mult).then_inc(s.at, 1)

            def tail(m):
                _, st, d, t = U[m]
                cols = slice(t * HEADS, (t + 1) * HEADS)
                dve.wait_ge(s.y, m + 1)
                ch(nc.vector.tensor_tensor(yo[m % 2][:, :].rearrange("p (h v) -> p h v", v=HV),
                                           S.ps[:, 4 + m % 2, DG:2 * DG].rearrange("p (h v) -> p h v", v=HV),
                                           eu[:, 0, d, cols].unsqueeze(2).to_broadcast([P, HEADS, HV]), ALU.mult))
                if t >= CT and not st < T - st + 1:
                    dve.wait_ge(s.y_out, 2 * (T + 1 - st) + (1 - d) + 1)
                    ch(nc.vector.tensor_tensor(yo[m % 2][:, :], yo[m % 2][:, :], o[:, t - CT, :], ALU.add))
                if t >= CT:
                    nc.vector.tensor_tensor(o[:, t - CT, :], yo[m % 2][:, :], S.ps[:, 4 + m % 2, 0:DG], ALU.add
                                            ).then_inc(s.y_out, 1)
                else:
                    nc.vector.engine_nop().then_inc(s.y_out, 1)
                sd = St[d][:, :].rearrange("p (h v) -> p h v", v=HV)
                ch(nc.vector.tensor_tensor(sd, sd, eu[:, 2, d, cols].unsqueeze(2).to_broadcast([P, HEADS, HV]), ALU.mult))
                dve.wait_ge(s.st, m + 1)
                nc.vector.tensor_tensor(St[d][:, :], St[d][:, :], S.ps[:, 6 + m % 2, 0:DG], ALU.add
                                        ).then_inc(s.s_new, 1)

            for n in range(N + 3):
                if n >= 3:
                    tail(n - 3)
                if 1 <= n <= N:
                    scores(n - 1)
                if n < N:
                    front(n)

    plan.at = mark

    def skip(dve, ch):
        xl = xt[:, CT:T, :]
        for h in range(HEADS):
            hs = slice(h * HV, (h + 1) * HV)
            ch(nc.vector.scalar_tensor_tensor(o[:, :, hs], xl[:, :, hs], S.mb_d[:, h:h + 1], o[:, :, hs],
                                              ALU.mult, ALU.add))

    head_norm(nc, S, "mb_n", o, z, S.mb_norm, True, 4, plan, True, skip)


def deltanet(nc, S, A):
    plan = Plan(nc, S.stage_at)
    vt = plan.take("dn_v", [P, T, DG])
    kt = plan.take("dn_k", [P, T, DG])
    kz = plan.take("dn_kz", [P, HEADS, TOK])
    qT = plan.take("dn_qT", [P, 2, TOK])
    o = plan.take("dn_o", [P, LT, DG])
    ga = plan.take("dn_g", [P, T, 2, HEADS])
    be = plan.take("dn_beta", [P, T, 2, HEADS])
    bec = plan.take("dn_beta_cum", [P, 2, T * HEADS])
    cu = plan.take("dn_cum", [P, 3, 2, T * HEADS])
    eu = plan.take("dn_cum_exp", [P, 3, 2, T * HEADS])
    mark = plan.at
    qt = nc.alloc_sbuf_tensor_at("dn_q", [P, T, DG], F32, offset=S.stage_at + 2 * T * DG * 4)
    plan = Plan(nc, S.stage_at + 3 * T * DG * 4)
    blocks = []
    for b in range(6):
        tok = (qt, kt, vt)[b // 2][:, :, (b % 2) * P:(b % 2 + 1) * P]
        blocks.append(dict(col=b * P, tap=48 + b, step=6, bias=None, silu=True, colmajor=False, cm=None, tok=tok))
    raw = Plan(nc, SBUF_END - 4 * T * 16).take("dn_raw", [P, T, 16])
    blocks.append(dict(col=DN_COLS - P, tap=66, step=1, bias=None, silu=False, colmajor=False, cm=None, tok=raw,
                       sub=P - 16))
    project_conv(nc, S, A, "dn_c", blocks, plan)

    plan = Plan(nc, mark)
    with Stage(nc, "dn_l", "sq red rt normed tr tr_out chain") as s:
        sq = plan.take("dn_square", [P, T, DG])
        ss = plan.take("dn_norms", [P, 3, 2, T * HEADS])
        qc = plan.take("dn_qn", [P, T, DG])

        @s.block.vector
        def _(dve):
            ch = Chain(dve, s.chain)
            for i, x in enumerate((qt, kt)):
                ch(nc.vector.tensor_tensor(sq[:, :, :], x[:, :, :], x[:, :, :], ALU.mult))
                nc.vector.tensor_reduce(ss[:, 0, i, :], sq[:, :, :].rearrange("p t (h v) -> p (t h) v", v=HV), AX.X,
                                        ALU.add).then_inc(s.red, 1)
                dve.wait_ge(s.red, i + 1)
            dve.wait_ge(s.rt, 2)
            ch(nc.vector.reciprocal(ss[:, 2, :, :], ss[:, 1, :, :]))
            for i, (x, y) in enumerate(((qt, qc), (kt, kt))):
                nc.vector.tensor_tensor(y[:, :, :].rearrange("p t (h v) -> p (t h) v", v=HV),
                                        x[:, :, :].rearrange("p t (h v) -> p (t h) v", v=HV),
                                        ss[:, 2, i, :].unsqueeze(2).to_broadcast([P, T * HEADS, HV]), ALU.mult
                                        ).then_inc(s.normed, 1)
            for i in range(10, 20):
                p, t = (i - 10) // 5, 2 * (i % 5)
                dve.wait_ge(s.tr, i + 1)
                for h in range(2):
                    last = nc.vector.tensor_scalar(kz[:, 2 * p + h, t * P:(t + 2) * P], S.ps[:, 4 + i % 4, 0:2 * P],
                                                   S.t("half")[:, h:h + 1], None, ALU.mult)
                last.then_inc(s.tr_out, 1)

        @s.block.scalar
        def _(act):
            for i, sc in enumerate((HV, 1.0)):
                act.wait_ge(s.red, i + 1)
                nc.scalar.activation(ss[:, 1, i, :], ss[:, 0, i, :], ACT.Sqrt,
                                     bias=(S.eps64 if i == 0 else S.eps)[:, 0:1], scale=float(sc)).then_inc(s.rt, 1)
            for i in range(10):
                p, t = i // 5, 2 * (i % 5)
                act.wait_ge(s.tr, i + 1)
                nc.scalar.activation(qT[:, p, t * P:(t + 2) * P], S.ps[:, i % 4, 0:2 * P], ACT.Copy).then_inc(s.sq, 1)

        @s.block.tensor
        def _(pe):
            for i in range(20):
                src = qc if i < 10 else kt
                p, t = (i % 10) // 5, 2 * (i % 5)
                pe.wait_ge(s.normed, 1 if i < 10 else 2)
                b = i % 4 + (0 if i < 10 else 4)
                if 4 <= i < 10:
                    pe.wait_ge(s.sq, i - 3)
                if i >= 14:
                    pe.wait_ge(s.tr_out, i - 13)
                for u in range(2):
                    last = nc.tensor.transpose(S.ps[:, b, u * P:(u + 1) * P], src[:, t + u, p * P:(p + 1) * P],
                                               S.t("ident"))
                last.then_inc(s.tr, 1)

    plan = Plan(nc, mark)
    with Stage(nc, "dn_t", "biased ab e1 e2 ea sp chain sums sg") as s:
        ab = plan.take("dn_abs", [P, T * 8])
        ea = plan.take("dn_decay", [P, 8])

        @s.block.tensor
        def _(pe):
            pe.wait_ge(s.sp, 1)
            gate_sums(nc, S, s, pe, ga, 6).then_inc(s.sums, 1)

        @s.block.scalar
        def _(act):
            nc.scalar.activation(be[:, :, :, :].rearrange("p t d h -> p t (d h)"), raw[:, :, 0:8], ACT.Sigmoid
                                 ).then_inc(s.sg, 1)
            act.wait_ge(s.biased, 1)
            nc.scalar.activation(ab[:, :], ga[:, :, :, :].rearrange("p t d h -> p (t d h)"), ACT.Abs).then_inc(s.ab, 1)
            act.wait_ge(s.ab, 1)
            nc.scalar.activation(ab[:, :], ab[:, :], ACT.Exp, scale=-1.0).then_inc(s.e1, 1)
            act.wait_ge(s.e1, 1)
            nc.scalar.activation(ab[:, :], ab[:, :], ACT.Ln, bias=S.one[:, 0:1]).then_inc(s.e2, 1)
            nc.scalar.activation(ea[:, :], S.gates[:, 2, :], ACT.Exp).then_inc(s.ea, 1)
            act.wait_ge(s.sums, 1)
            nc.scalar.activation(eu[:, :, :, :], S.ps[:, 6, 0:240].rearrange("p (w d n) -> p w d n", w=3, d=2), ACT.Exp
                                 ).then_inc(s.ea, 1)

        @s.block.vector
        def _(dve):
            ch = Chain(dve, s.chain)
            gf = ga[:, :, :, :].rearrange("p t d h -> p t (d h)")
            g1 = ga[:, :, :, :].rearrange("p t d h -> p (t d h)")
            nc.vector.tensor_tensor(gf, raw[:, :, 8:16], S.gates[:, 3, :].unsqueeze(1).to_broadcast([P, T, 8]), ALU.add
                                    ).then_inc(s.biased, 1)
            dve.wait_ge(s.e2, 1)
            ch(nc.vector.scalar_tensor_tensor(g1, g1, 0.0, ab[:, :], ALU.max, ALU.add))
            dve.wait_ge(s.ea, 1)
            ch(nc.vector.tensor_scalar(ea[:, :], ea[:, :], -1.0, None, ALU.mult))
            nc.vector.tensor_tensor(gf, gf, ea[:, :].unsqueeze(1).to_broadcast([P, T, 8]), ALU.mult).then_inc(s.sp, 1)
            dve.wait_ge(s.ea, 2)
            ch(nc.vector.tensor_copy(cu[:, :, :, :], S.ps[:, 6, 0:240].rearrange("p (w d n) -> p w d n", w=3, d=2)))
            for d in range(2):
                ch(nc.vector.tensor_tensor(bec[:, d, :].rearrange("p (t h) -> p t h", h=HEADS),
                                           eu[:, 0, d, :].rearrange("p (t h) -> p t h", h=HEADS), be[:, :, d, :],
                                           ALU.mult))

    plan = Plan(nc, mark)
    with Stage(nc, "dn_s", "dt_init1 decayed rows kk qk rel seg z at zt m_nat mt mt_out d_init dt_init p_ps p_sb dp pd d_new dt_new "
                           "rhs rhs_v ke uw uw_out ws v_new q_out av o_out s_new chain pchain") as s:
        NL = 7
        X = [plan.take(f"dn_x{b}", [P, HEADS, P]) for b in range(2)]
        MT = [plan.take(f"dn_mT{b}", [P, HEADS, P]) for b in range(2)]
        AT = [plan.take(f"dn_attnT{b}", [P, HEADS, P]) for b in range(2)]
        Dn = [plan.take(f"dn_inv{b}", [P, HEADS, P]) for b in range(2)]
        DT = [plan.take(f"dn_invT{b}", [P, HEADS, P]) for b in range(2)]
        St = [plan.take(f"dn_state{b}", [P, DG]) for b in range(2)]
        oq = [plan.take(f"dn_oq{b}", [P, DG]) for b in range(2)]
        flat = lambda x: x[:, :, :].rearrange("p h c -> p (h c)")

        def lev(l, d):
            return S.t("levels_" + "fb"[d])[:, l * P:(l + 1) * P]

        def hb(x):
            return x.unsqueeze(1).to_broadcast([P, HEADS, P])

        def tile_of(st, d):
            return ORDER["fb"[d]][st]

        def decay_rows(st):
            for d in range(2):
                t, b = tile_of(st, d), 4 * d
                for h in range(HEADS):
                    last = nc.tensor.matmul(S.ps[:, b, h * P:(h + 1) * P], ga[:, t, d, h:h + 1].to_broadcast([P, P]),
                                            S.t("tri_" + "fb"[d]), start=True, stop=True)
                last.then_inc(s.rows, 1)

        @s.block.tensor
        def _(pe):
            decay_rows(0)
            for st in range(T):
                for d in range(2):
                    n, t, b = 2 * st + d, tile_of(st, d), 4 * d
                    ts_ = slice(t * P, (t + 1) * P)
                    if n >= 2:
                        pe.wait_ge(s.uw_out, n - 1)
                        pe.wait_ge(s.v_new, n - 1)
                    for h in range(HEADS):
                        last = nc.tensor.matmul(S.ps[:, b + 1, h * P:(h + 1) * P], kz[:, h, ts_], kz[:, h, ts_],
                                                start=True, stop=True)
                    last.then_inc(s.kk, 1)
                for d in range(2):
                    n, t, b = 2 * st + d, tile_of(st, d), 4 * d
                    ts_ = slice(t * P, (t + 1) * P)
                    if n >= 2:
                        pe.wait_ge(s.q_out, n - 1)
                    for h in range(HEADS):
                        last = nc.tensor.matmul(S.ps[:, b + 2, h * P:(h + 1) * P], kz[:, h, ts_], qT[:, h // 2, ts_],
                                                start=True, stop=True)
                    last.then_inc(s.qk, 1)
                    pe.wait_ge(s.z, n + 1)
                    for h in range(HEADS):
                        last = nc.tensor.transpose(S.ps[:, b, h * P:(h + 1) * P], MT[d][:, h, :], S.t("ident"))
                    last.then_inc(s.zt, 1)
                for d in range(2):
                    n, b = 2 * st + d, 4 * d
                    pe.wait_ge(s.m_nat, n + 1)
                    for h in range(HEADS):
                        last = nc.tensor.transpose(S.ps[:, b + 1, h * P:(h + 1) * P], X[d][:, h, :], S.t("ident"))
                    last.then_inc(s.mt, 1)
                for l in range(1, NL):
                    for d in range(2):
                        n, b = 2 * st + d, 4 * d
                        e = (n // 2 * (NL - 1) + l - 1) * 2 + d
                        if l == 1:
                            pe.wait_ge(s.mt_out, n + 1)
                            pe.wait_ge(s.d_init, n + 1)
                        else:
                            pe.wait_ge(s.d_new, e - 1)
                        for h in range(HEADS):
                            last = nc.tensor.matmul(S.ps[:, b, h * P:(h + 1) * P], MT[d][:, h, :], Dn[d][:, h, :],
                                                    start=True, stop=True)
                        last.then_inc(s.p_ps, 1)
                    for d in range(2):
                        n, b = 2 * st + d, 4 * d
                        e = (n // 2 * (NL - 1) + l - 1) * 2 + d
                        pe.wait_ge(s.p_sb, e + 1)
                        if l == 1:
                            pe.wait_ge((s.dt_init, s.dt_init1)[d], st + 1)
                        else:
                            pe.wait_ge(s.dt_new, e - 1)
                        for h in range(HEADS):
                            last = nc.tensor.matmul(S.ps[:, b + 2, h * P:(h + 1) * P], X[d][:, h, :], DT[d][:, h, :],
                                                    start=True, stop=True)
                        last.then_inc(s.pd, 1)
                        if l < NL - 1:
                            for h in range(HEADS):
                                last = nc.tensor.matmul(S.ps[:, b + 1, h * P:(h + 1) * P], DT[d][:, h, :], X[d][:, h, :],
                                                        start=True, stop=True)
                            last.then_inc(s.dp, 1)
                for d in range(2):
                    n, t, b = 2 * st + d, tile_of(st, d), 4 * d
                    pe.wait_ge(s.dt_new, 2 * (NL - 1) * (st + 1) - (1 - d))
                    pe.wait_ge(s.rhs, n + 1)
                    pe.wait_ge(s.rhs_v, n + 1)
                    for h in range(HEADS):
                        nc.tensor.matmul(S.ps[:, b + 1, h * HV:(h + 1) * HV], DT[d][:, h, :], X[d][:, h, 0:HV],
                                         start=True, stop=True)
                    for h in range(HEADS):
                        r0 = (h % 2) * HV
                        last = nc.tensor.matmul(S.ps[r0:r0 + HV, b + 1, DG + (h // 2) * P:DG + (h // 2 + 1) * P],
                                                X[d][:, h, HV:P], DT[d][:, h, :], start=True, stop=True)
                    last.then_inc(s.uw, 1)
                for d in range(2):
                    n, t, b = 2 * st + d, tile_of(st, d), 4 * d
                    ts_ = slice(t * P, (t + 1) * P)
                    pe.wait_ge(s.uw_out, n + 1)
                    if st == 0:
                        pe.wait_ge(s.chain, 2)
                    else:
                        pe.wait_ge(s.s_new, n - 1)
                        pe.wait_ge(s.o_out, n - 1)
                    wT = flat(MT[d])[:, DG:2 * DG]
                    for p in range(2):
                        nc.tensor.matmul(S.ps[:, b + 2, p * P:(p + 1) * P], wT[:, p * P:(p + 1) * P],
                                         St[d][:, p * P:(p + 1) * P], start=True, stop=True)
                    for p in range(2):
                        last = nc.tensor.matmul(S.ps[:, b + 2, DG + p * P:DG + (p + 1) * P], qT[:, p, ts_],
                                                St[d][:, p * P:(p + 1) * P], start=True, stop=True)
                    last.then_inc(s.ws, 1)
                if st + 1 < T:
                    decay_rows(st + 1)
                for d in range(2):
                    n, t, b = 2 * st + d, tile_of(st, d), 4 * d
                    pe.wait_ge(s.v_new, n + 1)
                    pe.wait_ge(s.ke, n + 1)
                    vn, ke = flat(Dn[d])[:, 0:DG], flat(Dn[d])[:, DG:2 * DG]
                    for h in range(HEADS):
                        nc.tensor.matmul(S.ps[:, b + 3, h * HV:(h + 1) * HV], AT[d][:, h, :], vn[:, h * HV:(h + 1) * HV],
                                         start=True, stop=True)
                    for p in range(2):
                        last = nc.tensor.matmul(S.ps[:, b + 3, DG + p * P:DG + (p + 1) * P], ke[:, p * P:(p + 1) * P],
                                                vn[:, p * P:(p + 1) * P], start=True, stop=True)
                    last.then_inc(s.av, 1)

        @s.block.scalar
        def _(act):
            for st in range(T):
                for d in range(2):
                    n = 2 * st + d
                    act.wait_ge(s.rel, n + 1)
                    nc.scalar.activation(flat(X[d]), flat(X[d]), ACT.Exp).then_inc(s.seg, 1)
                for d in range(2):
                    n = 2 * st + d
                    act.wait_ge(s.mt, n + 1)
                    nc.scalar.activation(flat(MT[d]), S.ps[:, 4 * d + 1, :], ACT.Copy).then_inc(s.mt_out, 1)
                for d in range(2):
                    n = 2 * st + d
                    act.wait_ge(s.uw, n + 1)
                    nc.scalar.activation(flat(MT[d]), S.ps[:, 4 * d + 1, :], ACT.Copy).then_inc(s.uw_out, 1)

        @s.block.gpsimd
        def _(pool):
            pc = Chain(pool, s.pchain)
            for st in range(T):
                pool.wait_ge(s.mt_out, 2 * st + 1)
                pc(nc.gpsimd.tensor_tensor(DT[0][:, :, :], MT[0][:, :, :], hb(lev(0, 1)), ALU.mult))
                nc.gpsimd.tensor_tensor(DT[0][:, :, :], hb(S.t("ident")), DT[0][:, :, :], ALU.subtract
                                        ).then_inc(s.dt_init, 1)
                for d in range(2):
                    n, t = 2 * st + d, tile_of(st, d)
                    cols = slice(t * HEADS, (t + 1) * HEADS)
                    pool.wait_ge(s.pd, 2 * (NL - 1) * (st + 1) - (1 - d))
                    nc.gpsimd.tensor_tensor(X[d][:, :, 0:HV], vt[:, t, :].rearrange("p (h v) -> p h v", v=HV),
                                            be[:, t, d, :].unsqueeze(2).to_broadcast([P, HEADS, HV]), ALU.mult
                                            ).then_inc(s.rhs_v, 1)
                    nc.gpsimd.tensor_tensor(X[d][:, :, HV:P], kt[:, t, :].rearrange("p (h v) -> p h v", v=HV),
                                            bec[:, d, cols].unsqueeze(2).to_broadcast([P, HEADS, HV]), ALU.mult
                                            ).then_inc(s.rhs, 1)
                    nc.gpsimd.tensor_tensor(flat(Dn[d])[:, DG:2 * DG].rearrange("p (h v) -> p h v", v=HV),
                                            kt[:, t, :].rearrange("p (h v) -> p h v", v=HV),
                                            eu[:, 1, d, cols].unsqueeze(2).to_broadcast([P, HEADS, HV]), ALU.mult
                                            ).then_inc(s.ke, 1)
                for d in range(2):
                    n, t = 2 * st + d, tile_of(st, d)
                    cols = slice(t * HEADS, (t + 1) * HEADS)
                    sd = St[d][:, :].rearrange("p (h v) -> p h v", v=HV)
                    pool.wait_ge(s.ws, n + 1)
                    nc.gpsimd.tensor_tensor(sd, sd, eu[:, 2, d, cols].unsqueeze(2).to_broadcast([P, HEADS, HV]), ALU.mult
                                            ).then_inc(s.decayed, 1)

        @s.block.vector
        def _(dve):
            ch = Chain(dve, s.chain)
            for d in range(2):
                ch(nc.vector.memset(St[d][:, :], 0.0))

            def relative(st):
                for d in range(2):
                    n, t, b = 2 * st + d, tile_of(st, d), 4 * d
                    dve.wait_ge(s.rows, n + 1)
                    if n >= 2:
                        dve.wait_ge(s.uw, n - 1)
                    for h in range(HEADS):
                        c = t * HEADS + h
                        last = nc.vector.scalar_tensor_tensor(X[d][:, h, :], S.ps[:, b, h * P:(h + 1) * P],
                                                              cu[:, 0, d, c:c + 1], S.t("neg_" + "fb"[d]),
                                                              ALU.subtract, ALU.add)
                    last.then_inc(s.rel, 1)

            def settle(st, d):
                n, t, b = 2 * st + d, tile_of(st, d), 4 * d
                dve.wait_ge(s.av, n + 1)
                if t >= CT:
                    dve.wait_ge(s.q_out, n + 1)
                    if not st < T - st + 1:
                        dve.wait_ge(s.o_out, 2 * (T + 1 - st) + (1 - d) + 1)
                        ch(nc.vector.tensor_tensor(oq[d][:, :], oq[d][:, :], o[:, t - CT, :], ALU.add))
                    nc.vector.tensor_tensor(o[:, t - CT, :], oq[d][:, :], S.ps[:, b + 3, 0:DG], ALU.add
                                            ).then_inc(s.o_out, 1)
                else:
                    nc.vector.engine_nop().then_inc(s.o_out, 1)
                dve.wait_ge(s.q_out, n + 1)
                dve.wait_ge(s.o_out, n + 1)
                ch(nc.vector.tensor_tensor(oq[d][:, :], S.ps[:, b + 3, DG:2 * DG], S.t("dn_bd"), ALU.mult))
                dve.wait_ge(s.decayed, n + 1)
                nc.vector.tensor_tensor(St[d][:, :], St[d][:, :], oq[d][:, :], ALU.add).then_inc(s.s_new, 1)

            relative(0)
            for st in range(T):
                for d in range(2):
                    n, b = 2 * st + d, 4 * d
                    dve.wait_ge(s.seg, n + 1)
                    dve.wait_ge(s.kk, n + 1)
                    if n >= 2:
                        dve.wait_ge(s.ws, n - 1)
                    nc.vector.tensor_tensor(flat(MT[d]), flat(X[d]), S.ps[:, b + 1, :], ALU.mult).then_inc(s.z, 1)
                for d in range(2):
                    n, t, b = 2 * st + d, tile_of(st, d), 4 * d
                    dve.wait_ge(s.qk, n + 1)
                    if n >= 2:
                        dve.wait_ge(s.av, n - 1)
                    nc.vector.tensor_tensor(flat(AT[d]), flat(X[d]), S.ps[:, b + 2, :], ALU.mult).then_inc(s.at, 1)
                    dve.wait_ge(s.zt, n + 1)
                    dve.wait_ge(s.at, n + 1)
                    nc.vector.tensor_tensor(X[d][:, :, :], S.ps[:, b, :].rearrange("p (h c) -> p h c", c=P),
                                            be[:, t, d, :].unsqueeze(2).to_broadcast([P, HEADS, P]), ALU.mult
                                            ).then_inc(s.m_nat, 1)
                for d in range(2):
                    n, t, b = 2 * st + d, tile_of(st, d), 4 * d
                    dve.wait_ge(s.m_nat, n + 1)
                    ch(nc.vector.tensor_tensor(Dn[d][:, :, :], X[d][:, :, :], hb(lev(0, d)), ALU.mult))
                    nc.vector.tensor_tensor(Dn[d][:, :, :], hb(S.t("ident")), Dn[d][:, :, :], ALU.subtract
                                            ).then_inc(s.d_init, 1)
                dve.wait_ge(s.mt_out, 2 * st + 2)
                ch(nc.vector.tensor_tensor(DT[1][:, :, :], MT[1][:, :, :], hb(lev(0, 0)), ALU.mult))
                nc.vector.tensor_tensor(DT[1][:, :, :], hb(S.t("ident")), DT[1][:, :, :], ALU.subtract
                                        ).then_inc(s.dt_init1, 1)
                for l in range(1, NL):
                    for d in range(2):
                        n, b = 2 * st + d, 4 * d
                        e = (n // 2 * (NL - 1) + l - 1) * 2 + d
                        dve.wait_ge(s.p_ps, e + 1)
                        if l == 1:
                            dve.wait_ge(s.mt, n + 1)
                        nc.vector.tensor_tensor(X[d][:, :, :], S.ps[:, b, :].rearrange("p (h c) -> p h c", c=P),
                                                hb(lev(l, d)), ALU.mult).then_inc(s.p_sb, 1)
                    if st and l <= 2:
                        settle(st - 1, l - 1)
                    for d in range(2):
                        n, b = 2 * st + d, 4 * d
                        e = (n // 2 * (NL - 1) + l - 1) * 2 + d
                        if l < NL - 1:
                            dve.wait_ge(s.dp, (n // 2 * (NL - 2) + l - 1) * 2 + d + 1)
                            if l == 1:
                                dve.wait_ge(s.d_init, n + 1)
                            nc.vector.tensor_tensor(flat(Dn[d]), flat(Dn[d]), S.ps[:, b + 1, :], ALU.subtract
                                                    ).then_inc(s.d_new, 1)
                        else:
                            nc.vector.engine_nop().then_inc(s.d_new, 1)
                        dve.wait_ge(s.pd, e + 1)
                        if l == 1:
                            dve.wait_ge((s.dt_init, s.dt_init1)[d], st + 1)
                        else:
                            dve.wait_ge(s.dt_new, e - 1)
                            dve.wait_ge(s.d_new, e - 1)
                        nc.vector.tensor_tensor(flat(DT[d]), flat(DT[d]), S.ps[:, b + 2, :], ALU.subtract
                                                ).then_inc(s.dt_new, 1)
                for d in range(2):
                    n, t, b = 2 * st + d, tile_of(st, d), 4 * d
                    cols = slice(t * HEADS, (t + 1) * HEADS)
                    dve.wait_ge(s.ws, n + 1)
                    nc.vector.tensor_tensor(flat(Dn[d])[:, 0:DG], flat(MT[d])[:, 0:DG], S.ps[:, b + 2, 0:DG], ALU.subtract
                                            ).then_inc(s.v_new, 1)
                    nc.vector.tensor_tensor(oq[d][:, :].rearrange("p (h v) -> p h v", v=HV),
                                            S.ps[:, b + 2, DG:2 * DG].rearrange("p (h v) -> p h v", v=HV),
                                            eu[:, 0, d, cols].unsqueeze(2).to_broadcast([P, HEADS, HV]), ALU.mult
                                            ).then_inc(s.q_out, 1)
                if st + 1 < T:
                    relative(st + 1)
            settle(T - 1, 0)
            settle(T - 1, 1)

    plan = Plan(nc, mark)
    og = plan.take("dn_og", [P, LT, DG])
    with Stage(nc, "dn_g", "tp tp_out") as s:
        jobs = [(t, 768, DG) for t in range(CT, T)]
        dsts = [[(og[:, t - CT, :], 0, DG)] for t in range(CT, T)]

        @s.block.tensor
        def _(pe):
            token_products(nc, S, s, pe, jobs)

        @s.block.scalar
        def _(act):
            token_copies(nc, S, s, act, jobs, dsts)

    head_norm(nc, S, "dn_n", o, og, S.dn_norm, False, 6, Plan(nc, S.stage_at), False,
              loads=lambda sp: load_weights(sp, S, A, HY0, HY_COLS))


class FilterLayers:
    HF, EMB = 64, 33
    sems = "small lin arg sin side_ch"

    def __init__(self, nc, A, plan):
        HF, EMB = self.HF, self.EMB
        self.nc, self.A, self.at = nc, A, plan.at
        self.h = plan.take("hy_h", [HF, SEQ])
        self.w4 = plan.take("hy_fw3", [HF, 2 * 2 * DG])
        self.feats = plan.take("hy_feats", [EMB, SEQ])
        self.ws = [plan.take(f"hy_fw{i}", [EMB if i == 0 else HF, HF]) for i in range(3)]
        self.bs = plan.take("hy_fb", [HF, 3])
        self.fr = plan.take("hy_ff", [HF, 3])
        self.arg = plan.take("hy_arg", [HF, SEQ])
        self.rnd = plan.take("hy_round", [HF, SEQ])

    def load(self, s, sp):
        A, bs, fr, ws = self.A, self.bs, self.fr, self.ws
        for dst, src in ((self.feats[:, :], A["feats"]), (ws[0][:, :], A["hy_w1"][0]), (ws[1][:, :], A["hy_w2"][0]),
                         (ws[2][:, :], A["hy_w3"][0]), (self.w4[:, :], A["hy_w4"][0]),
                         (bs[:, 0:1], A["hy_b1"].rearrange("a p -> p a")), (bs[:, 1:2], A["hy_b2"].rearrange("a p -> p a")),
                         (bs[:, 2:3], A["hy_b3"].rearrange("a p -> p a")),
                         (fr[:, 0:1], A["hy_freq"][0, 0:1, :].rearrange("a p -> p a")),
                         (fr[:, 1:2], A["hy_freq"][0, 1:2, :].rearrange("a p -> p a")),
                         (fr[:, 2:3], A["hy_freq"][0, 2:3, :].rearrange("a p -> p a"))):
            sp.dma_start(dst, src).then_inc(s.small, 16)

    def pe(self, s, pe, i):
        if i % 2 or i > 4:
            return
        if i == 0:
            pe.wait_ge(s.small, 11 * 16)
        else:
            pe.wait_ge(s.sin, i // 2)
        rhs = self.feats if i == 0 else self.h
        for c in range(2):
            last = self.nc.tensor.matmul(self.ps[0:self.HF, 2 + 3 * c, :], self.ws[i // 2][:, :],
                                         rhs[:, c * 512:(c + 1) * 512], start=True, stop=True)
        last.then_inc(s.lin, 1)

    def act(self, s, act, i):
        if i % 2 or i > 4:
            return
        act.wait_ge(s.arg, i // 2 + 1)
        self.nc.scalar.activation(self.h[:, :], self.arg[:, :], ACT.Sin).then_inc(s.sin, 1)

    def dve(self, s, dve, ch, i):
        if i % 2 or i > 4:
            return
        i //= 2
        nc, arg, rnd = self.nc, self.arg, self.rnd
        TWO_PI = 2.0 * math.pi
        MAGIC = 12582912.0
        dve.wait_ge(s.lin, i + 1)
        for c in range(2):
            ch(nc.vector.tensor_scalar(arg[:, c * 512:(c + 1) * 512], self.ps[0:self.HF, 2 + 3 * c, :],
                                       self.bs[:, i:i + 1], self.fr[:, i:i + 1], ALU.add, ALU.mult))
        ch(nc.vector.tensor_scalar(rnd[:, :], arg[:, :], 1.0 / TWO_PI, MAGIC, ALU.mult, ALU.add))
        ch(nc.vector.tensor_scalar(rnd[:, :], rnd[:, :], -MAGIC, None, ALU.add))
        hi = 6.28125
        ch(nc.vector.scalar_tensor_tensor(arg[:, :], rnd[:, :], -hi, arg[:, :], ALU.mult, ALU.add))
        ch(nc.vector.scalar_tensor_tensor(arg[:, :], rnd[:, :], -(TWO_PI - hi), arg[:, :], ALU.mult, ALU.add))
        nc.vector.tensor_scalar(arg[:, :], arg[:, :], 3.1415925, -3.1415925, ALU.min, ALU.max).then_inc(s.arg, 1)


def hyena(nc, S, A):
    plan = Plan(nc, S.stage_at)
    v = plan.take("hy_v", [P, LT, DG])
    x1 = plan.take("hy_x1", [P, LT, DG])
    mark = plan.at
    blocks = []
    for b in range(6):
        cm = S.yT[:, 2 + b % 2, :] if b >= 4 else None
        tok = (v if b < 2 else x1)[:, :, (b % 2) * P:(b % 2 + 1) * P] if b < 4 else None
        blocks.append(dict(col=b * P, tap=b, step=6, bias=18 + b, silu=False, colmajor=False, cm=cm, tok=tok,
                           by_parity=True))
    side = FilterLayers(nc, A, Plan(nc, mark + 3 * 2 * 1284 * 4 + 96))
    side.ps = S.ps
    project_conv(nc, S, A, "hy_c", blocks, plan, ctx=False, side=side)
    assert plan.at <= side.at
    h, w4 = side.h, side.w4

    low = Plan(nc, S.hT_at, S.stage_at)
    hs = low.take("hy_sum", [P, LT, 2, DG])
    hd = low.take("hy_diff", [P, LT, 2, DG])
    plan = Plan(nc, mark)
    late = Plan(nc, SBUF_END - 2 * 2 * SEQ * 4)
    with Stage(nc, "hy_f", "win_in tables taps tapped zeroed sd") as s:
        win = plan.take("hy_window", [P, LT, DG])
        tap = [plan.take(f"hy_taps{b}", [P, 2, DG]) for b in range(2)]
        assert plan.at <= side.at
        tw = [late.take(f"hy_dft{b}", [P, 2, LT, P]) for b in range(2)]
        fwd = low.take("hy_fwd", [P, 2, LT, HALF])

        @s.block.sync
        def _(sp):
            sp.dma_start(win[:, :, :], A["window"].rearrange("(t p) c -> p t c", p=P)).then_inc(s.win_in, 16)
            for b in range(2):
                for q in range(2):
                    sp.dma_start(tw[b][:, q, :, :],
                                 A["dft_whole"][q, :, b * P:(b + 1) * P].rearrange("(t p) k -> p t k", p=P)
                                 ).then_inc(s.tables, 16)
            for q in range(2):
                sp.dma_start(fwd[:, q, :, :], A["dft_fwd"][q].rearrange("(t p) k -> p t k", p=P)).then_inc(s.tables, 16)
            sp.wait_ge(s.tables, 6 * 16)

        @s.block.tensor
        def _(pe):
            for i in range(2 * LT):
                lt, q = i // 2, i % 2
                if i >= 4:
                    pe.wait_ge(s.tapped, i - 3)
                nc.tensor.matmul(S.ps[:, 2 + i % 4, :], h[:, lt * P:(lt + 1) * P], w4[:, q * 512:(q + 1) * 512],
                                 start=True, stop=True).then_inc(s.taps, 1)

        @s.block.vector
        def _(dve):
            dve.wait_ge(s.win_in, 16)
            for i in range(2 * LT):
                lt, q = i // 2, i % 2
                dve.wait_ge(s.taps, i + 1)
                if i >= 2:
                    dve.wait_ge(s.sd, i - 1)
                nc.vector.tensor_tensor(tap[i % 2][:, :, :], S.ps[:, 2 + i % 4, :].rearrange("p (d c) -> p d c", d=2),
                                        win[:, lt, :].unsqueeze(1).to_broadcast([P, 2, DG]), ALU.mult
                                        ).then_inc(s.tapped, 1)
                if lt == 0:
                    dve.wait_ge(s.tapped, i + 1)
                    nc.vector.memset(tap[i % 2][0:1, 1, :], 0.0).then_inc(s.zeroed, 1)

        @s.block.gpsimd
        def _(pool):
            for i in range(2 * LT):
                lt, q = i // 2, i % 2
                pool.wait_ge(s.tapped, i + 1)
                if lt == 0:
                    pool.wait_ge(s.zeroed, i + 1)
                nc.gpsimd.tensor_tensor(hs[:, lt, q, :], tap[i % 2][:, 0, :], tap[i % 2][:, 1, :], ALU.add)
                nc.gpsimd.tensor_tensor(hd[:, lt, q, :], tap[i % 2][:, 0, :], tap[i % 2][:, 1, :], ALU.subtract
                                        ).then_inc(s.sd, 1)

    plan = Plan(nc, mark)
    kr = plan.take("hy_k_re", [P, 2, HT, 2, DG])
    kb = plan.take("hy_k_b", [P, 2, HT, 2, DG])
    with Stage(nc, "hy_k", "tab*2 sums even prod d_in chain") as s:
        dv = plan.take("hy_skip", [P, 2 * DG])
        ev = [plan.take(f"hy_even{b}", [P, 2, 2 * DG]) for b in range(2)]

        @s.block.sync
        def _(sp):
            sp.dma_start(dv[:, :], A["hy_d"].rearrange("a o c -> (a o c)").partition_broadcast(P)).then_inc(s.d_in, 16)
            for b in range(2, HT):
                sp.wait_ge(s.prod, b - 1)
                for q in range(2):
                    sp.dma_start(tw[b % 2][:, q, :, :],
                                 A["dft_whole"][q, :, b * P:(b + 1) * P].rearrange("(t p) k -> p t k", p=P)
                                 ).then_inc(s.tab[b % 2], 16)

        @s.block.tensor
        def _(pe):
            for b in range(HT):
                if b >= 2:
                    pe.wait_ge(s.tab[b % 2], 32 * (b // 2))
                    pe.wait_ge(s.sums, b - 1)
                for q, x in enumerate((hs, hd)):
                    for par in range(2):
                        for t in range(HT):
                            lt = par * HT + t
                            last = nc.tensor.matmul(S.ps[:, 4 * (b % 2) + 2 * q + par, :], tw[b % 2][:, q, lt, :],
                                                    x[:, lt, :, :].rearrange("p o c -> p (o c)"),
                                                    start=(t == 0), stop=(t == HT - 1))
                last.then_inc(s.prod, 1)

        @s.block.scalar
        def _(act):
            for b in range(HT):
                act.wait_ge(s.prod, b + 1)
                if b >= 2:
                    act.wait_ge(s.sums, b - 1)
                nc.scalar.activation(ev[b % 2][:, 1, :], S.ps[:, 4 * (b % 2) + 2, :], ACT.Copy).then_inc(s.even, 1)

        @s.block.vector
        def _(dve):
            ch = Chain(dve, s.chain)
            dve.wait_ge(s.d_in, 16)
            for b in range(HT):
                dve.wait_ge(s.prod, b + 1)
                bank = 4 * (b % 2)
                flat = lambda t, w: t[:, w, b, :, :].rearrange("p o c -> p (o c)")
                ch(nc.vector.scalar_tensor_tensor(ev[b % 2][:, 0, :], dv[:, :], 1.0 / SEQ, S.ps[:, bank, :],
                                                  ALU.mult, ALU.add))
                nc.vector.tensor_tensor(flat(kr, 0), ev[b % 2][:, 0, :], S.ps[:, bank + 1, :], ALU.add)
                nc.vector.tensor_tensor(flat(kr, 1), ev[b % 2][:, 0, :], S.ps[:, bank + 1, :], ALU.subtract)
                dve.wait_ge(s.even, b + 1)
                nc.vector.tensor_tensor(flat(kb, 0), S.ps[:, bank + 3, :], ev[b % 2][:, 1, :], ALU.add)
                nc.vector.tensor_tensor(flat(kb, 1), S.ps[:, bank + 3, :], ev[b % 2][:, 1, :], ALU.subtract
                                        ).then_inc(s.sums, 1)

    low = Plan(nc, S.hT_at, S.stage_at)
    inv = low.take("hy_inv", [P, 2, HT, SEQ])
    S.w_out = Plan(nc, low.at).take("w_out", [P, KD, D])
    plan = Plan(nc, mark + 2 * 2 * HT * 2 * DG * 4)
    with Stage(nc, "hy_d", "tab w_out fwd even x pq uw y inv z fin") as s:
        Y = plan.take("hy_y", [P, 2, HT, 2, DG])
        ev = plan.take("hy_even", [P, 2 * DG])
        X = [plan.take(f"hy_x{b}", [P, 2, 2, DG]) for b in range(2)]
        p1 = plan.take("hy_p1", [P, 2, 2, DG])
        p2 = plan.take("hy_p2", [P, 2, 2, DG])
        UW = plan.take("hy_uw", [P, 2, 2, DG])

        @s.block.sync
        def _(sp):
            for q in range(2):
                sp.dma_start(inv[:, q, :, :], A["dft_inv"][q].rearrange("(t p) k -> p t k", p=P)).then_inc(s.tab, 16)
            sp.wait_ge(s.fwd, 2 * HT)
            for h in range(2):
                sp.dma_start(S.w_out[:, 4 * h:4 * h + 4, :],
                             A["w_out"][0, 512 * h:512 * h + 512, :].rearrange("(k p) n -> p k n", p=P)).then_inc(s.w_out, 16)
            sp.wait_ge(s.w_out, 32)

        @s.block.tensor
        def _(pe):
            for o in range(2):
                if o == 1:
                    pe.wait_ge(s.z, LT)
                for b in range(HT):
                    i = o * HT + b
                    if i >= 2:
                        pe.wait_ge(s.x, i - 1)
                    for par in range(2):
                        for q in range(2):
                            for t in range(HT):
                                nt = par * HT + t
                                last = nc.tensor.matmul(S.ps[:, 2 * (i % 2) + par, q * DG:(q + 1) * DG],
                                                        fwd[:, q, nt, b * P:(b + 1) * P], v[:, nt, :],
                                                        start=(t == 0), stop=(t == HT - 1))
                    last.then_inc(s.fwd, 1)
                if o == 0:
                    pe.wait_ge(s.tab, 32)
                    for nt in range(LT):
                        if nt >= 2:
                            pe.wait_ge(s.z, nt - 1)
                        for b in range(HT):
                            if nt == 0:
                                pe.wait_ge(s.y, b + 1)
                            for q in range(2):
                                last = nc.tensor.matmul(S.ps[:, 4 + nt % 2, 0:DG], inv[:, q, b, nt * P:(nt + 1) * P],
                                                        Y[:, nt // HT, b, q, :], start=(q == 0 and b == 0),
                                                        stop=(q == 1 and b == HT - 1))
                        last.then_inc(s.inv, 1)
                else:
                    for i in range(4):
                        par, c = i // 2, i % 2
                        for b in range(HT):
                            if i == 0:
                                pe.wait_ge(s.y, HT + b + 1)
                            for q in range(2):
                                last = nc.tensor.matmul(S.ps[:, 4 + i, :], Y[:, par, b, q, c * P:(c + 1) * P],
                                                        inv[:, q, b, par * HALF:(par + 1) * HALF],
                                                        start=(q == 0 and b == 0), stop=(q == 1 and b == HT - 1))
                        last.then_inc(s.inv, 1)

        @s.block.scalar
        def _(act):
            for i in range(2 * HT):
                act.wait_ge(s.fwd, i + 1)
                if i:
                    act.wait_ge(s.x, i)
                nc.scalar.activation(ev[:, :], S.ps[:, 2 * (i % 2), :], ACT.Copy).then_inc(s.even, 1)

        @s.block.vector
        def _(dve):
            for o in range(2):
                for b in range(HT):
                    i = o * HT + b
                    x = X[i % 2]
                    dve.wait_ge(s.even, i + 1)
                    flat = lambda w: x[:, w, :, :].rearrange("p q c -> p (q c)")
                    nc.vector.tensor_tensor(flat(0), ev[:, :], S.ps[:, 2 * (i % 2) + 1, :], ALU.add)
                    nc.vector.tensor_tensor(flat(1), ev[:, :], S.ps[:, 2 * (i % 2) + 1, :], ALU.subtract).then_inc(s.x, 1)
                    dve.wait_ge(s.x, i + 1)
                    if i:
                        dve.wait_ge(s.uw, i)
                    for p, k in ((p1, kr), (p2, kb)):
                        for w in range(2):
                            last = nc.vector.tensor_tensor(p[:, w, :, :], x[:, w, :, :],
                                                           k[:, w, b, o, :].unsqueeze(1).to_broadcast([P, 2, DG]), ALU.mult)
                    last.then_inc(s.pq, 1)
                if o == 0:
                    for nt in range(LT):
                        dve.wait_ge(s.inv, nt + 1)
                        nc.vector.tensor_tensor(v[:, nt, :], x1[:, nt, :], S.ps[:, 4 + nt % 2, 0:DG], ALU.mult
                                                ).then_inc(s.z, 1)
                else:
                    for i in range(4):
                        par, c = i // 2, i % 2
                        dve.wait_ge(s.inv, LT + i + 1)
                        y = S.yT[:, 2 + c, par:SEQ:2]
                        nc.vector.tensor_tensor(y, y, S.ps[:, 4 + i, :], ALU.mult).then_inc(s.fin, 1)

        @s.block.gpsimd
        def _(pool):
            for i in range(2 * HT):
                o, b = i // HT, i % HT
                pool.wait_ge(s.pq, i + 1)
                if i:
                    pool.wait_ge(s.y, i)
                nc.gpsimd.tensor_tensor(UW[:, 0, 0, :], p1[:, 0, 0, :], p2[:, 0, 1, :], ALU.subtract)
                nc.gpsimd.tensor_tensor(UW[:, 0, 1, :], p1[:, 0, 1, :], p2[:, 0, 0, :], ALU.add)
                nc.gpsimd.tensor_tensor(UW[:, 1, 0, :], p1[:, 1, 0, :], p2[:, 1, 1, :], ALU.add)
                nc.gpsimd.tensor_tensor(UW[:, 1, 1, :], p1[:, 1, 1, :], p2[:, 1, 0, :], ALU.subtract).then_inc(s.uw, 1)
                pool.wait_ge(s.uw, i + 1)
                if o == 1 and b == 0:
                    pool.wait_ge(s.inv, LT)
                nc.gpsimd.tensor_tensor(Y[:, 0, b, :, :], UW[:, 0, :, :], UW[:, 1, :, :], ALU.add)
                nc.gpsimd.tensor_tensor(Y[:, 1, b, :, :], UW[:, 0, :, :], UW[:, 1, :, :], ALU.subtract).then_inc(s.y, 1)


def project_out(nc, S, A):
    wo = S.w_out
    low = Plan(nc, S.hT_at, S.hT_at + KD * D * 4)
    rows = low.take("row_broadcasts", [P, 3, D])
    rt = low.take("router", [P, KD, NE])
    xt = [low.take(f"res_x{b}", [P, D]) for b in range(2)]
    tm = [low.take(f"res_tmp{b}", [P, D]) for b in range(2)]
    low = Plan(nc, S.hT_at + 2 * KD * D * 4)
    h2 = [low.take(f"h2_{b}", [P, D]) for b in range(2)]
    hT = low.take("h2T", [P, KD, P])
    st = low.take("out_stats", [P, LT, 8])
    sm = [low.take(f"aff{b}", [P, NE]) for b in range(2)]
    x1, affT = S.x1, S.affT
    with Stage(nc, "out", "rows_in r_in x_in*2 y ss rt y_sc x1d ss2 rt2 h2m h2d h2s*2 tr ht_a ht_v lg mx ex af at at_o "
                          "chain zero zst") as s:

        @s.block.sync
        def _(sp):
            sp.dma_start(rt[:, :, :], A["moe_router"][0].rearrange("(k p) n -> p k n", p=P)).then_inc(s.r_in, 16)
            for j in range(3):
                sp.dma_start(rows[:, j, :], A["rows"][j, :].partition_broadcast(P)).then_inc(s.rows_in, 16)
            sp.wait_ge(s.zero, 1)
            for t in range(LT):
                sp.dma_start(A["moe_sum"][t * P:(t + 1) * P, :], S.zrow[:, :]).then_inc(s.zst, 16)
            for t in range(LT + 1):
                if t < LT:
                    if t >= 2:
                        sp.wait_ge(s.x1d, t - 1)
                    sp.dma_start(xt[t % 2][:, :], A["x"][0, t * P:(t + 1) * P, :]).then_inc(s.x_in[t % 2], 16)
                if t >= 1:
                    u = t - 1
                    sp.wait_ge(s.h2d, u + 1)
                    sp.dma_start(A["h2"][u * P:(u + 1) * P, :], h2[u % 2][:, :]).then_inc(s.h2s[u % 2], 16)
            for b in range(2):
                sp.wait_ge(s.h2s[b], 16 * LT // 2)
            sp.wait_ge(s.zst, 16 * LT)

        @s.block.gpsimd
        def _(pool):
            for t in range(LT):
                pool.wait_ge(s.y_sc, t + 1)
                pool.wait_ge(s.x_in[t % 2], 16 * (t // 2 + 1))
                nc.gpsimd.tensor_tensor(x1[:, t, :], tm[t % 2][:, :], xt[t % 2][:, :], ALU.add).then_inc(s.x1d, 1)
                pool.wait_ge(s.rows_in, 48)
                pool.wait_ge(s.h2m, t + 1)
                nc.gpsimd.tensor_tensor(h2[t % 2][:, :], h2[t % 2][:, :], rows[:, 2, :], ALU.add).then_inc(s.h2d, 1)

        def turn_rows(pe, t):
            pe.wait_ge(s.h2d, t + 1)
            if t >= 1:
                pe.wait_ge(s.ht_a, t)
                pe.wait_ge(s.ht_v, t)
            for k in range(KD):
                last = nc.tensor.transpose(S.ps[:, 4 + k // 4, (k % 4) * P:(k % 4 + 1) * P],
                                           h2[t % 2][:, k * P:(k + 1) * P], S.t("ident"))
            last.then_inc(s.tr, 1)

        def router(pe, t):
            pe.wait_ge(s.ht_a, t + 1)
            pe.wait_ge(s.ht_v, t + 1)
            if t >= 1:
                pe.wait_ge(s.ex, t)
            for k in range(KD):
                last = nc.tensor.matmul(S.ps[:, 6, 0:NE], hT[:, k, :], rt[:, k, :], start=(k == 0), stop=(k == KD - 1))
            last.then_inc(s.lg, 1)

        def turned(pe, t):
            pe.wait_ge(s.af, t + 1)
            if t >= 1:
                pe.wait_ge(s.at_o, t)
            nc.tensor.transpose(S.ps[0:NE, 7, 0:P], sm[t % 2][:, :], S.t("ident")).then_inc(s.at, 1)

        @s.block.tensor
        def _(pe):
            pe.wait_ge(s.r_in, 16)
            for t in range(LT + 3):
                if t < LT and t >= 2:
                    pe.wait_ge(s.y_sc, t - 1)
                for h in range(2):
                    if h == 1 and 2 <= t <= LT + 1:
                        router(pe, t - 2)
                    if t < LT:
                        for k in range(KD):
                            last = nc.tensor.matmul(S.ps[:, 2 * (t % 2) + h, :], S.yT[:, k, t * P:(t + 1) * P],
                                                    wo[:, k, h * 512:(h + 1) * 512], start=(k == 0), stop=(k == KD - 1))
                if t < LT:
                    last.then_inc(s.y, 1)
                if 1 <= t <= LT:
                    turn_rows(pe, t - 1)
                if t >= 3:
                    turned(pe, t - 3)

        @s.block.scalar
        def _(act):
            for t in range(LT + 2):
                if t >= 2:
                    u = t - 2
                    act.wait_ge(s.mx, u + 1)
                    nc.scalar.activation(sm[u % 2][:, :], S.ps[:, 6, 0:NE], ACT.Exp, bias=st[:, u, 6:7],
                                         accum_out=st[:, u, 7:8]).then_inc(s.ex, 1)
                if 1 <= t <= LT:
                    act.wait_ge(s.tr, t)
                    nc.scalar.activation(hT[:, 0:4, :], S.ps[:, 4, :].rearrange("p (k c) -> p k c", c=P), ACT.Copy
                                         ).then_inc(s.ht_a, 1)
                if t < LT:
                    act.wait_ge(s.y, t + 1)
                    if t >= 1:
                        act.wait_ge(s.ss2, t)
                    y = S.ps[:, 2 * (t % 2):2 * (t % 2) + 2, :].rearrange("p a b -> p (a b)")
                    nc.scalar.activation(S.junk[:, :], y, ACT.Square, accum_out=st[:, t, 0:1]).then_inc(s.ss, 1)
                    act.wait_ge(s.ss, t + 1)
                    nc.scalar.activation(st[:, t, 1:2], st[:, t, 0:1], ACT.Sqrt, bias=S.eps[:, 0:1], scale=1.0 / D
                                         ).then_inc(s.rt, 1)
                    act.wait_ge(s.x1d, t + 1)
                    nc.scalar.activation(S.junk[:, :], x1[:, t, :], ACT.Square, accum_out=st[:, t, 3:4]).then_inc(s.ss2, 1)
                    act.wait_ge(s.ss2, t + 1)
                    nc.scalar.activation(st[:, t, 4:5], st[:, t, 3:4], ACT.Sqrt, bias=S.eps[:, 0:1], scale=1.0 / D
                                         ).then_inc(s.rt2, 1)

        @s.block.vector
        def _(dve):
            ch = Chain(dve, s.chain)
            nc.vector.memset(S.zrow[:, :], 0.0).then_inc(s.zero, 1)
            dve.wait_ge(s.rows_in, 48)
            for t in range(LT + 3):
                if 2 <= t <= LT + 1:
                    u = t - 2
                    dve.wait_ge(s.lg, u + 1)
                    nc.vector.tensor_reduce(st[:, u, 6:7], S.ps[:, 6, 0:NE], AX.X, ALU.max, negate=True).then_inc(s.mx, 1)
                    dve.wait_ge(s.ex, u + 1)
                    ch(nc.vector.reciprocal(st[:, u, 5:6], st[:, u, 7:8]))
                    nc.vector.tensor_scalar(sm[u % 2][:, :], sm[u % 2][:, :], st[:, u, 5:6], None, ALU.mult
                                            ).then_inc(s.af, 1)
                if 1 <= t <= LT:
                    dve.wait_ge(s.tr, t)
                    nc.vector.tensor_copy(hT[:, 4:8, :], S.ps[:, 5, :].rearrange("p (k c) -> p k c", c=P)
                                          ).then_inc(s.ht_v, 1)
                if t < LT:
                    dve.wait_ge(s.rt, t + 1)
                    ch(nc.vector.reciprocal(st[:, t, 2:3], st[:, t, 1:2]))
                    if t >= 2:
                        dve.wait_ge(s.x1d, t - 1)
                    y = S.ps[:, 2 * (t % 2):2 * (t % 2) + 2, :].rearrange("p a b -> p (a b)")
                    nc.vector.scalar_tensor_tensor(tm[t % 2][:, :], y, st[:, t, 2:3], rows[:, 0, :], ALU.mult, ALU.mult
                                                   ).then_inc(s.y_sc, 1)
                    dve.wait_ge(s.rt2, t + 1)
                    ch(nc.vector.reciprocal(st[:, t, 2:3], st[:, t, 4:5]))
                    if t >= 2:
                        dve.wait_ge(s.h2s[t % 2], 16 * (t // 2))
                        dve.wait_ge(s.tr, t - 1)
                    nc.vector.scalar_tensor_tensor(h2[t % 2][:, :], x1[:, t, :], st[:, t, 2:3], rows[:, 1, :],
                                                   ALU.mult, ALU.mult).then_inc(s.h2m, 1)
                if t >= 3:
                    u = t - 3
                    dve.wait_ge(s.at, u + 1)
                    nc.vector.tensor_copy(affT[:, u * P:(u + 1) * P], S.ps[0:NE, 7, 0:P]).then_inc(s.at_o, 1)


def experts(nc, S, A):
    PIECES, RAW, RING = 12, 6, 4
    BY_POOL = (1, 5, 9)
    BY_DVE = tuple(i for i in range(PIECES) if i not in BY_POOL)
    plan = Plan(nc, S.moe_at)
    raw = [plan.take(f"w_raw{i}", [P, 2048]) for i in range(RAW)]
    wh = [plan.take(f"w_hi{i}", [P, 2048], F32R) for i in range(RING)]
    wl = [plan.take(f"w_lo{i}", [P, 2048], F32R) for i in range(RING)]
    xs = plan.take("xs", [P, D])
    xh = plan.take("xsT_hi", [P, KD, P], F32R)
    xl = plan.take("xsT_lo", [P, KD, P], F32R)
    a = [plan.take(f"hidden{j}", [P, 512]) for j in range(2)]
    ah = plan.take("hiddenT_hi", [P, KD, P], F32R)
    al = plan.take("hiddenT_lo", [P, KD, P], F32R)
    early = Plan(nc, plan.at)
    sg = [plan.take(f"gate_silu{j}", [P, 512]) for j in range(2)]
    y = plan.take("y", [P, D])
    work = early.take("aff_work", [NE, SEQ])
    val = early.take("top_val", [NE, CAP])
    idx = early.take("top_idx", [NE, CAP], U32)
    idf = early.take("top_idx_f", [NE, CAP])
    with Stage(nc, "moe", "chain picked turned cols raw_in*6 hi lo_v lo_p used xtr xh_done xl_done sg0 sg1 a0 a1 "
                          "atr0 atr1 ah0 ah1 al0 al1 ya yv") as s:
        sgs, as_, atr = [s.sg0, s.sg1], [s.a0, s.a1], [s.atr0, s.atr1]
        ahs, als = [s.ah0, s.ah1], [s.al0, s.al1]
        wg = A["moe_w_gate"].rearrange("a e (k p) n -> (a e) p k n", p=P)
        wu = A["moe_w_up"].rearrange("a e (k p) n -> (a e) p k n", p=P)
        wd = A["moe_w_down"].rearrange("a e (k p) n -> (a e) p k n", p=P)

        def wait_hi(eng, e, i):
            eng.wait_ge(s.hi, e * PIECES + (PIECES + i + 1))

        def wait_lo(eng, e, i):
            mine, sem = (BY_POOL, s.lo_p) if i % PIECES in BY_POOL else (BY_DVE, s.lo_v)
            n = len(mine)
            eng.wait_ge(sem, e * n + (n + (i // PIECES) * n + mine.index(i % PIECES) + 1))

        def wait_used(eng, e, i):
            eng.wait_ge(s.used, e * PIECES + (PIECES + i + 1))

        @s.block.sync
        def _(sp):
            with sp.Fori(0, NE) as e:
                for i in range(PIECES):
                    wait_lo(sp, e, i - RAW)
                    if i < 8:
                        k, j = 4 * (i % 2), i // 4
                        src = (wg, wu)[i // 2 % 2][e, :, k:k + 4, j * 512:(j + 1) * 512]
                        dst = raw[i % RAW][:, :].rearrange("p (k n) -> p k n", k=4)
                    else:
                        k = 2 * (i - 8)
                        src = wd[e, :, k:k + 2, :]
                        dst = raw[i % RAW][:, :].rearrange("p (k n) -> p k n", k=2)
                    sp.dma_start(dst, src).then_inc(s.raw_in[i % RAW], 16)

        def wait_raw(eng, e, i):
            eng.wait_ge(s.raw_in[i % RAW], e * (16 * PIECES // RAW) + 16 * (i // RAW + 1))

        def split_lo(eng, ops, e, i):
            wait_hi(eng, e, i)
            wait_raw(eng, e, i)
            wait_used(eng, e, i - RING)
            ops.tensor_tensor(wl[i % RING][:, :], raw[i % RAW][:, :], wh[i % RING][:, :].bitcast(F32), ALU.subtract
                              ).then_inc(s.lo_p if i in BY_POOL else s.lo_v, 1)

        def gather(pool, e):
            pool.indirect_dma_start(xs[:, :], None, A["h2"], bass.IndirectOffsetOnAxis(ap=S.icol[:, e:e + 1], axis=0)
                                    ).then_inc(S.xs_in, 16)

        def add_rows(pool, e):
            if e:
                pool.wait_ge(S.y_added, e * 16)
            pool.wait_ge(s.ya, e + 1)
            pool.wait_ge(s.yv, e + 1)
            pool.indirect_dma_start(A["moe_sum"], bass.IndirectOffsetOnAxis(ap=S.icol[:, e:e + 1], axis=0), y[:, :],
                                    None, compute_op=ALU.add).then_inc(S.y_added, 16)

        @s.block.gpsimd
        def _(pool):
            nc.gpsimd.engine_nop().then_inc(s.lo_p, len(BY_POOL))
            pool.wait_ge(s.cols, 1)
            gather(pool, 0)
            for e in range(NE):
                split_lo(pool, nc.gpsimd, e, BY_POOL[0])
                if e < NE - 1:
                    pool.wait_ge(s.xtr, e + 1)
                    gather(pool, e + 1)
                if e:
                    add_rows(pool, e - 1)
                for i in BY_POOL[1:]:
                    split_lo(pool, nc.gpsimd, e, i)
            add_rows(pool, NE - 1)
            pool.wait_ge(S.y_added, NE * 16)

        def rows_turned(pe, e):
            pe.wait_ge(S.xs_in, e * 16 + 16)
            for k in range(KD):
                last = nc.tensor.transpose(S.ps[:, 2 + k // 4, (k % 4) * P:(k % 4 + 1) * P], xs[:, k * P:(k + 1) * P],
                                           S.t("ident"))
            last.then_inc(s.xtr, 1)

        def hidden_turned(pe, e, j):
            pe.wait_ge(as_[j], e + 1)
            pe.wait_ge(ahs[j], e)
            pe.wait_ge(als[j], e)
            for k in range(4):
                last = nc.tensor.transpose(S.ps[:, j, k * P:(k + 1) * P], a[j][:, k * P:(k + 1) * P], S.t("ident"))
            last.then_inc(atr[j], 1)

        def three(out, h, l, w, c, start, stop):
            nc.tensor.matmul(out, h, wh[w][:, c:c + 512], start=start, stop=False)
            nc.tensor.matmul(out, h, wl[w][:, c:c + 512], start=False, stop=False)
            return nc.tensor.matmul(out, l, wh[w][:, c:c + 512], start=False, stop=stop)

        def products(pe, e, last_one):
            pe.wait_ge(s.xh_done, e + 1)
            pe.wait_ge(s.xl_done, e + 1)
            for i in range(PIECES):
                w = i % RING
                if i == 4:
                    pe.wait_ge(as_[1], e)
                if i == 6:
                    hidden_turned(pe, e, 0)
                if i == 8:
                    if not last_one:
                        rows_turned(pe, e + 1)
                    hidden_turned(pe, e, 1)
                    pe.wait_ge(s.ya, e)
                    pe.wait_ge(s.yv, e)
                if i in (8, 10):
                    pe.wait_ge(ahs[i // 2 - 4], e + 1)
                    pe.wait_ge(als[i // 2 - 4], e + 1)
                wait_hi(pe, e, i)
                wait_lo(pe, e, i)
                if i < 8:
                    for k in range(4):
                        kk = 4 * (i % 2) + k
                        last = three(S.ps[:, 2 + i // 2, :], xh[:, kk, :], xl[:, kk, :], w, k * 512, kk == 0, kk == KD - 1)
                else:
                    for k in range(2):
                        kk = 2 * (i - 8) + k
                        for h in range(2):
                            last = three(S.ps[:, 6 + h, :], ah[:, kk, :], al[:, kk, :], w, k * D + h * 512,
                                         kk == 0, kk == KD - 1)
                last.then_inc(s.used, 1)

        @s.block.tensor
        def _(pe):
            pe.wait_ge(s.picked, 1)
            nc.tensor.transpose(S.ps[:, 0, 0:NE], val[:, :], S.t("ident")[0:NE, 0:NE])
            nc.tensor.transpose(S.ps[:, 1, 0:NE], idf[:, :], S.t("ident")[0:NE, 0:NE]).then_inc(s.turned, 1)
            pe.wait_ge(s.cols, 1)
            rows_turned(pe, 0)
            with pe.Fori(0, NE - 1) as e:
                products(pe, e, False)
            products(pe, NE - 1, True)

        def rows_hi(act, e):
            act.wait_ge(s.xtr, e + 1)
            nc.scalar.activation(xh[:, :, :].rearrange("p k c -> p (k c)"),
                                 S.ps[:, 2:4, :].rearrange("p a b -> p (a b)"), ACT.Copy).then_inc(s.xh_done, 1)

        def out_a(act, e):
            wait_used(act, e, PIECES - 1)
            act.wait_ge(S.y_added, e * 16)
            nc.scalar.activation(y[:, 0:512], S.ps[:, 6, :], ACT.Copy, scale=S.wcol[:, bass.ds(e, 1)]
                                 ).then_inc(s.ya, 1)

        def weights_a(act, e, first, last_one):
            for i in range(PIECES):
                if i == 3 and not first:
                    out_a(act, e - 1)
                if i in (7, 11):
                    j = i // 4 - 1
                    wait_used(act, e, 4 * j + 3)
                    act.wait_ge(as_[j], e)
                    nc.scalar.activation(sg[j][:, :], S.ps[:, 2 + 2 * j, :], ACT.Silu).then_inc(sgs[j], 1)
                if i == 10:
                    act.wait_ge(atr[0], e + 1)
                    nc.scalar.activation(ah[:, 0:4, :].rearrange("p k c -> p (k c)"), S.ps[:, 0, :], ACT.Copy
                                         ).then_inc(s.ah0, 1)
                wait_raw(act, e, i)
                wait_used(act, e, i - RING)
                nc.scalar.activation(wh[i % RING][:, :], raw[i % RAW][:, :], ACT.Copy).then_inc(s.hi, 1)
            if not last_one:
                rows_hi(act, e + 1)
            act.wait_ge(atr[1], e + 1)
            nc.scalar.activation(ah[:, 4:8, :].rearrange("p k c -> p (k c)"), S.ps[:, 1, :], ACT.Copy
                                 ).then_inc(s.ah1, 1)

        @s.block.scalar
        def _(act):
            act.wait_ge(s.cols, 1)
            rows_hi(act, 0)
            weights_a(act, 0, True, False)
            with act.Fori(1, NE - 1) as e:
                weights_a(act, e, False, False)
            weights_a(act, NE - 1, False, True)
            out_a(act, NE - 1)

        def rows_lo(dve, e):
            dve.wait_ge(s.xh_done, e + 1)
            xf = xl[:, :, :].rearrange("p k c -> p (k c)")
            nc.vector.tensor_tensor(xf, S.ps[:, 2:4, :].rearrange("p a b -> p (a b)"),
                                    xh[:, :, :].rearrange("p k c -> p (k c)").bitcast(F32), ALU.subtract
                                    ).then_inc(s.xl_done, 1)

        def hidden_lo(dve, e, j):
            dve.wait_ge(ahs[j], e + 1)
            nc.vector.tensor_tensor(al[:, 4 * j:4 * j + 4, :].rearrange("p k c -> p (k c)"), S.ps[:, j, :],
                                    ah[:, 4 * j:4 * j + 4, :].rearrange("p k c -> p (k c)").bitcast(F32), ALU.subtract
                                    ).then_inc(als[j], 1)

        def out_v(dve, e):
            wait_used(dve, e, PIECES - 1)
            dve.wait_ge(S.y_added, e * 16)
            nc.vector.tensor_scalar(y[:, 512:1024], S.ps[:, 7, :], S.wcol[:, bass.ds(e, 1)], None, ALU.mult
                                    ).then_inc(s.yv, 1)

        def weights_v(dve, e, first, last_one):
            for i in range(PIECES):
                if i == 3 and not first:
                    out_v(dve, e - 1)
                if i in (7, 11):
                    j = i // 4 - 1
                    dve.wait_ge(sgs[j], e + 1)
                    dve.wait_ge(atr[j], e)
                    nc.vector.tensor_tensor(a[j][:, :], sg[j][:, :], S.ps[:, 3 + 2 * j, :], ALU.mult).then_inc(as_[j], 1)
                if i == 10:
                    hidden_lo(dve, e, 0)
                if i in BY_DVE:
                    split_lo(dve, nc.vector, e, i)
            if not last_one:
                rows_lo(dve, e + 1)
            hidden_lo(dve, e, 1)

        @s.block.vector
        def _(dve):
            ch = Chain(dve, s.chain)
            nc.vector.engine_nop().then_inc(s.lo_v, len(BY_DVE))
            nc.vector.engine_nop().then_inc(s.used, PIECES)
            nc.vector.engine_nop().then_inc(s.hi, PIECES)
            R = CAP // 8
            for r in range(R):
                src = S.affT if r == 0 else work
                c = slice(8 * r, 8 * r + 8)
                ch(nc.vector.max(val[:, c], src[:, :]))
                ch(nc.vector.max_index(idx[:, c], val[:, c], src[:, :]))
                if r < R - 1:
                    ch(nc.vector.match_replace(work[:, :], val[:, c], src[:, :], -1.0))
            nc.vector.tensor_copy(idf[:, :], idx[:, :]).then_inc(s.picked, 1)
            dve.wait_ge(s.turned, 1)
            ch(nc.vector.tensor_copy(S.wcol[:, :], S.ps[:, 0, 0:NE]))
            nc.vector.tensor_copy(S.icol[:, :], S.ps[:, 1, 0:NE]).then_inc(s.cols, 1)
            rows_lo(dve, 0)
            weights_v(dve, 0, True, False)
            with dve.Fori(1, NE - 1) as e:
                weights_v(dve, e, False, False)
            weights_v(dve, NE - 1, False, True)
            out_v(dve, NE - 1)


def finish(nc, S, A):
    plan = Plan(nc, S.moe_at)
    m = [plan.take(f"moe_rows{t}", [P, D]) for t in range(LT)]
    g = plan.take("gate_row", [P, D])
    sq = plan.take("moe_sq", [P, D])
    st = plan.take("moe_stats", [P, LT, 3])
    with Stage(nc, "fin", f"g_in m_in*{LT} ss rt chain sc out*2 st") as s:
        @s.block.sync
        def _(sp):
            sp.dma_start(g[:, :], A["rows"][3, :].partition_broadcast(P)).then_inc(s.g_in, 16)
            for t in range(LT):
                sp.dma_start(m[t][:, :], A["moe_sum"][t * P:(t + 1) * P, :]).then_inc(s.m_in[t], 16)
            for t in range(LT):
                sp.wait_ge(s.out[t % 2], t // 2 + 1)
                sp.dma_start(A["out"][0, t * P:(t + 1) * P, :], m[t][:, :]).then_inc(s.st, 16)
            sp.wait_ge(s.st, 16 * LT)

        @s.block.scalar
        def _(act):
            for t in range(LT):
                act.wait_ge(s.m_in[t], 16)
                if t:
                    act.wait_ge(s.ss, t)
                nc.scalar.activation(sq[:, :], m[t][:, :], ACT.Square, accum_out=st[:, t, 0:1]).then_inc(s.ss, 1)
                act.wait_ge(s.ss, t + 1)
                nc.scalar.activation(st[:, t, 1:2], st[:, t, 0:1], ACT.Sqrt, bias=S.eps[:, 0:1], scale=1.0 / D
                                     ).then_inc(s.rt, 1)

        @s.block.vector
        def _(dve):
            ch = Chain(dve, s.chain)
            dve.wait_ge(s.g_in, 16)
            for t in range(LT):
                dve.wait_ge(s.rt, t + 1)
                ch(nc.vector.reciprocal(st[:, t, 2:3], st[:, t, 1:2]))
                nc.vector.scalar_tensor_tensor(m[t][:, :], m[t][:, :], st[:, t, 2:3], g[:, :], ALU.mult, ALU.mult
                                               ).then_inc(s.sc, 1)
                if t % 2:
                    dve.wait_ge(s.sc, t + 1)
                    nc.vector.tensor_tensor(m[t][:, :], m[t][:, :], S.x1[:, t, :], ALU.add).then_inc(s.out[1], 1)

        @s.block.gpsimd
        def _(pool):
            for t in range(0, LT, 2):
                pool.wait_ge(s.sc, t + 1)
                nc.gpsimd.tensor_tensor(m[t][:, :], m[t][:, :], S.x1[:, t, :], ALU.add).then_inc(s.out[0], 1)


STAGES = (load_and_modulate, normalise, gla, mamba, deltanet, hyena, project_out, experts, finish)


def program(nc, A, stages=STAGES):
    S = Store()
    SPENT.clear()
    (tab, S.off), (gla_tab, S.goff) = tables()
    S.gn = gla_tab.shape[1]
    plan = Plan(nc, SBUF0)
    S.tab = plan.take("tables", [P, tab.shape[1]])
    S.pcols = plan.take("param_cols", [P, 69])
    S.gla_norm = plan.take("gla_norm", [P, DG])
    S.mb_norm = plan.take("mb_norm", [P, DG])
    S.dn_norm = plan.take("dn_norm", [P, DG])
    S.gates = plan.take("gate_params", [P, 4, 8])
    S.mb_d = plan.take("mb_d", [P, HEADS])
    S.mod1 = plan.take("mod1", [P, 2, 2, KD])
    S.silu_c = plan.take("silu_cond", [P, KD, 2])
    S.eps = plan.take("eps", [P, 1])
    S.eps64 = plan.take("eps64", [P, 1])
    S.one = plan.take("one", [P, 1])
    S.zero = plan.take("zero", [P, 1])
    S.ones = plan.take("ones", [P, P])
    S.yT_at = plan.at
    S.yT = plan.take("yT", [P, KD, SEQ])
    S.hT_at = plan.at
    S.hT = plan.take("hT", [P, KD, TOK])
    S.w = plan.take("w_mixer", [P, KD, WCOLS])
    S.stage_at = plan.at
    top = Plan(nc, SBUF_END - LT * D * 4 - 4096 - 256)
    S.x1 = top.take("x1", [P, LT, D])
    S.affT = top.take("affT", [NE, SEQ])
    S.wcol = top.take("w_col", [P, NE])
    S.icol = top.take("idx_col", [P, NE], U32)
    S.moe_at = S.hT_at - KD * SEQ * 4
    S.zrow = nc.alloc_sbuf_tensor_at("zero_row", [P, D], F32, offset=SBUF_END - LT * D * 4 - 4096 - 256 - 4096)
    S.junk = nc.alloc_sbuf_tensor_at("squares", [P, D], F32, offset=SBUF_END - LT * D * 4 - 4096 - 256 - 8192)
    S.w_count = 0

    def t(name):
        o, n = S.off[name]
        return S.tab[:, o:o + n]

    S.t = t
    with nc.psum_tensor("ps", [P, 8, BANK], F32) as ps, nc.semaphore("w_ready") as w_ready, \
            nc.semaphore("xs_in") as xs_in, nc.semaphore("y_added") as y_added:
        S.ps, S.w_ready, S.xs_in, S.y_added = ps, w_ready, xs_in, y_added
        with Stage(nc, "init", "done") as s:
            @s.block.vector
            def _(dve):
                nc.vector.memset(S.eps[:, :], EPS)
                nc.vector.memset(S.eps64[:, :], EPS * HV)
                nc.vector.memset(S.one[:, :], 1.0)
                nc.vector.memset(S.zero[:, :], 0.0)
                nc.vector.memset(S.ones[:, :], 1.0)
        for stage in stages:
            stage(nc, S, A)
        with Stage(nc, "end", "") as s:
            @s.block.sync
            def _(sp):
                sp.wait_ge(S.w_ready, S.w_count)
        nc.clear_and_free_semaphores(list(SPENT))
        SPENT.clear()
    return S


_INS = ["x", "c", "ctx", "c_ctx", "w_mod", "b_mod", "norm_g", "w_in", "w_out", "gla_w2", "gla_b", "gla_norm",
        "hy_conv_w", "hy_conv_b", "hy_w1", "hy_b1", "hy_w2", "hy_b2", "hy_w3", "hy_b3", "hy_w4", "hy_freq", "hy_d",
        "mb_conv_w", "mb_conv_b", "mb_a_log", "mb_dt_bias", "mb_d", "mb_norm", "dn_conv_w", "dn_a_log", "dn_dt_bias",
        "dn_norm", "moe_router", "moe_w_gate", "moe_w_up", "moe_w_down"]


def declare(nc, arrays):
    A = {n: nc.dram_tensor("in_" + n, a.shape, F32, kind="ExternalInput").ap() for n, a in arrays.items()}
    A["rows"] = nc.dram_tensor("rows", (4, D), F32, kind="Internal").ap()
    A["h2"] = nc.dram_tensor("h2", (SEQ, D), F32, kind="Internal").ap()
    A["moe_sum"] = nc.dram_tensor("moe_sum", (SEQ, D), F32, kind="Internal").ap()
    A["out"] = nc.dram_tensor("out_0_dram", (1, SEQ, D), F32, kind="ExternalOutput").ap()
    return A


def kernel(**inputs):
    import numpy as _np
    import concourse.bacc as _bacc
    from concourse.bass_utils import run_bass_kernel_spmd as _run

    nc = _bacc.Bacc("TRN2", target_bir_lowering=False, num_devices=1)
    arrays = {n: _np.ascontiguousarray(inputs[n]) for n in _INS}
    arrays.update(shape_tables())
    program(nc, declare(nc, arrays))
    r = _run(nc, [{"in_" + n: a for n, a in arrays.items()}], core_ids=[0])
    return r.results[0]["out_0_dram"]
```
